# Optimizing a Trainium2 kernel written in Bass

```python
import math
import jax, jax.numpy as jnp
from jax import lax
import numpy as np

D_MODEL = 1024
BATCH = 1
SEQ = 1024
DEPTH = 1

BLOCK = 128
HEAD_DIM = 64
A_HEADS = 4
A_QK = 32
A_V = 2 * A_QK
B_QHEADS = 4
B_KVHEADS = 2
B_WINDOW = 128
C_PATTERNS = ((128, 1), (512, 4), (2048, 16))
C_HEADS = 4
D_HEADS = 4
D_TOPK_MAX = 256
IDX_HEADS = 8
IDX_DIM = 32
REL_BUCKETS = 32
REL_MAX_DIST = 2048
A_BIAS0 = 0
B_BIAS0 = A_BIAS0 + A_HEADS
C_BIAS0 = B_BIAS0 + B_QHEADS
D_BIAS0 = C_BIAS0 + len(C_PATTERNS) * C_HEADS
N_BIAS_HEADS = D_BIAS0 + D_HEADS
N_BRANCH = 4
BRANCH_WIDTH = 256
N_EXPERTS = 16
N_GROUPS = 4
EXPERTS_PER_GROUP = N_EXPERTS // N_GROUPS
TOP_K = 2
GROUP_SCORE_TOPK = 2
D_FF_EXPERT = 256
MOE_BLOCK = 128
DEEPNORM_ALPHA = (2 * DEPTH) ** 0.25
DEEPNORM_BETA = (8 * DEPTH) ** -0.25

IN_SPLITS = (
    ('a_q', A_HEADS * 2 * A_QK), ('a_k', A_HEADS * 2 * A_QK), ('a_v', A_HEADS * A_V),
    ('b_q', B_QHEADS * HEAD_DIM), ('b_k', B_KVHEADS * HEAD_DIM), ('b_v', B_KVHEADS * HEAD_DIM),
    ('c_q', len(C_PATTERNS) * C_HEADS * HEAD_DIM), ('c_k', len(C_PATTERNS) * C_HEADS * HEAD_DIM),
    ('c_v', len(C_PATTERNS) * C_HEADS * HEAD_DIM),
    ('d_q', D_HEADS * HEAD_DIM), ('d_k', HEAD_DIM), ('d_v', HEAD_DIM),
    ('i_q', IDX_HEADS * IDX_DIM), ('i_k', IDX_DIM), ('i_w', IDX_HEADS),
    ('gate', N_BRANCH * D_MODEL),
)
IN_WIDTH = sum(w for _, w in IN_SPLITS)

kernel_name = 'hybrid_gated_four_mixer_deepnorm_moe'

def layer_norm(x, g, b, eps=1e-5):
    xf = x.astype(jnp.float32)
    mu = jnp.mean(xf, axis=-1, keepdims=True)
    var = jnp.mean(jnp.square(xf - mu), axis=-1, keepdims=True)
    return ((xf - mu) * lax.rsqrt(var + eps)).astype(x.dtype) * g + b

def rms_norm(x, g, eps=1e-5):
    xf = x.astype(jnp.float32)
    return (xf * lax.rsqrt(jnp.mean(jnp.square(xf), axis=-1, keepdims=True) + eps)).astype(x.dtype) * g

def t5_bucket(n):
    max_exact = REL_BUCKETS // 2
    nf = jnp.maximum(n, 1).astype(jnp.float32)
    log_ratio = jnp.log(nf / max_exact) / math.log(REL_MAX_DIST / max_exact)
    large = max_exact + (log_ratio * (REL_BUCKETS - max_exact)).astype(jnp.int32)
    large = jnp.minimum(large, REL_BUCKETS - 1)
    return jnp.where(n < max_exact, n, large)

def rel_bias(rel_table, dist, h0, nh):
    return rel_table[:, h0:h0 + nh].astype(jnp.float32)[t5_bucket(jnp.maximum(dist, 0))]

def split_in(h):
    parts = {}
    off = 0
    for name, width in IN_SPLITS:
        parts[name] = h[..., off:off + width]
        off += width
    return parts

def diff_attention(q, k, v, lam_q, lam_k, subln_g, rel_table, layer_idx):
    bsz, seq, _ = q.shape
    nb = seq // BLOCK
    qb = jnp.moveaxis(q.reshape(bsz, nb, BLOCK, A_HEADS, 2, A_QK), 1, 0)
    k = k.reshape(bsz, seq, A_HEADS, 2, A_QK)
    v = v.reshape(bsz, seq, A_HEADS, A_V)
    lam_init = 0.8 - 0.6 * math.exp(-0.3 * layer_idx)
    lq = lam_q.astype(jnp.float32)
    lk = lam_k.astype(jnp.float32)
    lam = jnp.exp(jnp.sum(lq[0] * lk[0])) - jnp.exp(jnp.sum(lq[1] * lk[1])) + lam_init
    kpos = jnp.arange(seq)
    scale = A_QK ** -0.5

    def block(args):
        q_blk, i = args
        qpos = i * BLOCK + jnp.arange(BLOCK)
        dist = qpos[:, None] - kpos[None, :]
        bias = jnp.moveaxis(rel_bias(rel_table, dist, A_BIAS0, A_HEADS), -1, 0)
        s = jnp.einsum('bqhmd,bkhmd->bhmqk', q_blk, k).astype(jnp.float32) * scale + bias[None, :, None]
        s = jnp.where(dist >= 0, s, -jnp.inf)
        p = jax.nn.softmax(s, axis=-1)
        w = p[:, :, 0] - lam * p[:, :, 1]
        return jnp.einsum('bhqk,bkhe->bqhe', w.astype(v.dtype), v)

    o = lax.map(block, (qb, jnp.arange(nb)))
    o = jnp.moveaxis(o, 0, 1).reshape(bsz, seq, A_HEADS, A_V)
    o = rms_norm(o, subln_g) * (1.0 - lam_init)
    return o.reshape(bsz, seq, A_HEADS * A_V)

def sliding_sink_attention(q, k, v, sinks, rel_table):
    bsz, seq, _ = q.shape
    nb = seq // BLOCK
    rep = B_QHEADS // B_KVHEADS
    q = q.reshape(bsz, nb, BLOCK, B_KVHEADS, rep, HEAD_DIM)

    def band(a):
        a = a.reshape(bsz, nb, BLOCK, B_KVHEADS, HEAD_DIM)
        prev = jnp.pad(a[:, :-1], ((0, 0), (1, 0), (0, 0), (0, 0), (0, 0)))
        return jnp.concatenate([prev, a], axis=2)

    kb, vb = band(k), band(v)
    ql = jnp.arange(BLOCK)
    kl = jnp.arange(2 * BLOCK)
    dist = ql[:, None] + BLOCK - kl[None, :]
    bias = rel_bias(rel_table, dist, B_BIAS0, B_QHEADS).reshape(BLOCK, 2 * BLOCK, B_KVHEADS, rep)
    bias = jnp.transpose(bias, (2, 3, 0, 1))
    kpos = jnp.arange(nb)[:, None] * BLOCK - BLOCK + kl[None, :]
    valid = ((dist >= 0) & (dist < B_WINDOW))[None] & (kpos >= 0)[:, None, :]
    s = jnp.einsum('bnqgrd,bnkgd->bngrqk', q, kb).astype(jnp.float32) * HEAD_DIM ** -0.5 + bias[None, None]
    s = jnp.where(valid[None, :, None, None], s, -jnp.inf)
    sink = jnp.broadcast_to(
        sinks.astype(jnp.float32).reshape(B_KVHEADS, rep)[None, None, :, :, None, None], s.shape[:-1] + (1,))
    p = jax.nn.softmax(jnp.concatenate([s, sink], axis=-1), axis=-1)[..., :-1]
    o = jnp.einsum('bngrqk,bnkgd->bnqgrd', p.astype(vb.dtype), vb)
    return o.reshape(bsz, seq, B_QHEADS * HEAD_DIM)

def dilated_attention(q, k, v, rel_table):
    bsz, seq, _ = q.shape
    nb = seq // BLOCK
    n_pat = len(C_PATTERNS)
    q = q.reshape(bsz, seq, n_pat, C_HEADS, HEAD_DIM)
    k = k.reshape(bsz, seq, n_pat, C_HEADS, HEAD_DIM)
    v = v.reshape(bsz, seq, n_pat, C_HEADS, HEAD_DIM)
    k_groups = [k[:, :, g] for g in range(n_pat)]
    v_groups = [v[:, :, g] for g in range(n_pat)]
    scale = HEAD_DIM ** -0.5

    def block(i):
        qpos = i * BLOCK + jnp.arange(BLOCK)
        q_blk = lax.dynamic_slice_in_dim(q, i * BLOCK, BLOCK, axis=1)
        outs, lses = [], []
        for g, (window, dil) in enumerate(C_PATTERNS):
            dist = dil * jnp.arange(window // dil + 1)
            idx = qpos[:, None] - dist[None, :]
            valid = idx >= 0
            idx = jnp.maximum(idx, 0)
            kg = k_groups[g][:, idx]
            vg = v_groups[g][:, idx]
            bias = rel_bias(rel_table, dist, C_BIAS0 + g * C_HEADS, C_HEADS).T
            s = jnp.einsum('bqhd,bqjhd->bqhj', q_blk[:, :, g], kg).astype(jnp.float32) * scale + bias
            s = jnp.where(valid[None, :, None, :], s, -jnp.inf)
            m = jnp.max(s, axis=-1, keepdims=True)
            e = jnp.exp(s - m)
            den = jnp.sum(e, axis=-1)
            outs.append(jnp.einsum('bqhj,bqjhd->bqhd', e, vg.astype(jnp.float32)) / den[..., None])
            lses.append(m[..., 0] + jnp.log(den))
        alpha = jax.nn.softmax(jnp.stack(lses, 0), axis=0)
        return jnp.sum(alpha[..., None] * jnp.stack(outs, 0), axis=0)

    o = lax.map(block, jnp.arange(nb))
    return jnp.moveaxis(o, 0, 1).reshape(bsz, seq, C_HEADS * HEAD_DIM).astype(v.dtype)

def indexed_sparse_attention(q, k, v, iq, ik, iw, rel_table):
    bsz, seq, _ = q.shape
    nb = seq // BLOCK
    k_sel = min(D_TOPK_MAX, seq // 4)
    q = q.reshape(bsz, seq, D_HEADS, HEAD_DIM)
    iq = iq.reshape(bsz, seq, IDX_HEADS, IDX_DIM)
    kpos = jnp.arange(seq)
    gather = jax.vmap(lambda a, idx: a[idx])
    scale = HEAD_DIM ** -0.5

    def block(i):
        qpos = i * BLOCK + jnp.arange(BLOCK)
        q_blk = lax.dynamic_slice_in_dim(q, i * BLOCK, BLOCK, axis=1)
        iq_blk = lax.dynamic_slice_in_dim(iq, i * BLOCK, BLOCK, axis=1)
        iw_blk = lax.dynamic_slice_in_dim(iw, i * BLOCK, BLOCK, axis=1)
        rel = jax.nn.relu(jnp.einsum('bqhd,bsd->bqhs', iq_blk, ik).astype(jnp.float32))
        index_score = jnp.einsum('bqhs,bqh->bqs', rel, iw_blk.astype(jnp.float32))
        index_score = jnp.where(kpos[None, None, :] <= qpos[None, :, None], index_score, -jnp.inf)
        _, sel = lax.top_k(index_score, k_sel)
        dist = qpos[None, :, None] - sel
        kg = gather(k, sel)
        vg = gather(v, sel)
        bias = jnp.moveaxis(rel_bias(rel_table, dist, D_BIAS0, D_HEADS), -1, 2)
        s = jnp.einsum('bqhd,bqkd->bqhk', q_blk, kg).astype(jnp.float32) * scale + bias
        s = jnp.where((dist >= 0)[:, :, None, :], s, -jnp.inf)
        p = jax.nn.softmax(s, axis=-1)
        return jnp.einsum('bqhk,bqkd->bqhd', p.astype(vg.dtype), vg)

    o = lax.map(block, jnp.arange(nb))
    return jnp.moveaxis(o, 0, 1).reshape(bsz, seq, D_HEADS * HEAD_DIM)

def hybrid_mixer(u, w_in, lam_q, lam_k, subln_g, sinks, w_branch, w_out, rel_table, layer_idx):
    bsz, seq, dm = u.shape
    parts = split_in(u @ w_in)
    o_a = diff_attention(parts['a_q'], parts['a_k'], parts['a_v'], lam_q, lam_k, subln_g, rel_table, layer_idx)
    o_b = sliding_sink_attention(parts['b_q'], parts['b_k'], parts['b_v'], sinks, rel_table)
    o_c = dilated_attention(parts['c_q'], parts['c_k'], parts['c_v'], rel_table)
    o_d = indexed_sparse_attention(parts['d_q'], parts['d_k'], parts['d_v'],
                                   parts['i_q'], parts['i_k'], parts['i_w'], rel_table)
    gates = jax.nn.sigmoid(parts['gate'].astype(jnp.float32)).reshape(bsz, seq, N_BRANCH, dm)
    branches = (o_a, o_b, o_c, o_d)
    merged = gates[:, :, 0] * (o_a @ w_branch[0])
    for i in range(1, N_BRANCH):
        merged = merged + gates[:, :, i] * (branches[i] @ w_branch[i])
    return (merged.astype(u.dtype) @ w_out).astype(u.dtype)

def routed_moe(v, w_router, b_router, w_exp_gate, w_exp_up, w_exp_down):
    bsz, seq, dm = v.shape
    n_tok = bsz * seq
    vf = v.reshape(n_tok, dm)
    probs = jax.nn.softmax((vf @ w_router).astype(jnp.float32), axis=-1)
    sel_score = probs + b_router.astype(jnp.float32)
    grp_score = jnp.sum(lax.top_k(sel_score.reshape(n_tok, N_GROUPS, EXPERTS_PER_GROUP), GROUP_SCORE_TOPK)[0], axis=-1)
    top_group = jnp.argmax(grp_score, axis=-1)
    in_group = (jnp.arange(N_EXPERTS) // EXPERTS_PER_GROUP)[None, :] == top_group[:, None]
    _, top_idx = lax.top_k(jnp.where(in_group, sel_score, -jnp.inf), TOP_K)
    top_w = jnp.take_along_axis(probs, top_idx, axis=-1)
    top_w = top_w / jnp.sum(top_w, axis=-1, keepdims=True)
    n_asg = n_tok * TOP_K
    e_a = top_idx.reshape(n_asg).astype(jnp.int32)
    tok_a = jnp.arange(n_asg, dtype=jnp.int32) // TOP_K
    w_a = top_w.reshape(n_asg)
    order = jnp.argsort(e_a)
    e_s, tok_s, w_s = e_a[order], tok_a[order], w_a[order]
    counts = jnp.zeros((N_EXPERTS,), jnp.int32).at[e_a].add(1)
    padded = (counts + MOE_BLOCK - 1) // MOE_BLOCK * MOE_BLOCK
    pad_end = jnp.cumsum(padded)
    pad_start = pad_end - padded
    start = jnp.cumsum(counts) - counts
    dest = pad_start[e_s] + jnp.arange(n_asg, dtype=jnp.int32) - start[e_s]
    n_blocks = -(-n_asg // MOE_BLOCK) + N_EXPERTS
    n_slots = n_blocks * MOE_BLOCK
    slot_tok = jnp.full((n_slots,), n_tok, jnp.int32).at[dest].set(tok_s)
    slot_w = jnp.zeros((n_slots,), jnp.float32).at[dest].set(w_s)
    block_e = jnp.minimum(jnp.searchsorted(pad_end, jnp.arange(n_blocks) * MOE_BLOCK, side='right'), N_EXPERTS - 1)
    vpad = jnp.concatenate([vf, jnp.zeros((1, dm), vf.dtype)], axis=0)
    xb = vpad[slot_tok].reshape(n_blocks, MOE_BLOCK, dm)

    def expert_block(args):
        x_blk, e = args
        h = jax.nn.silu(x_blk @ w_exp_gate[e]) * (x_blk @ w_exp_up[e])
        return h @ w_exp_down[e]

    yb = lax.map(expert_block, (xb, block_e)).reshape(n_slots, dm)
    y = jnp.zeros((n_tok + 1, dm), jnp.float32).at[slot_tok].add(yb.astype(jnp.float32) * slot_w[:, None])
    return y[:n_tok].reshape(bsz, seq, dm).astype(v.dtype)

def setup_inputs(seed: int = 0) -> dict:
    key = jax.random.key(seed)
    ks = jax.random.split(key, 21)
    L, D, E, F = DEPTH, D_MODEL, N_EXPERTS, D_FF_EXPERT

    def nrm(k, shape, s):
        return jax.random.normal(k, shape, jnp.float32) * s

    return {
        'x': nrm(ks[0], (BATCH, SEQ, D), 1.0),
        'c': nrm(ks[1], (BATCH, D), 1.0),
        'rel_table': nrm(ks[2], (REL_BUCKETS, N_BIAS_HEADS), 0.5),
        'w_router': nrm(ks[3], (D, E), D ** -0.5),
        'b_router': nrm(ks[4], (E,), 0.01),
        'w_ada': nrm(ks[5], (L, D, 6 * D), 0.1 * D ** -0.5),
        'b_ada': nrm(ks[6], (L, 6 * D), 0.01),
        'w_in': nrm(ks[7], (L, D, IN_WIDTH), D ** -0.5),
        'a_lambda_q': nrm(ks[8], (L, 2, A_QK), 0.1),
        'a_lambda_k': nrm(ks[9], (L, 2, A_QK), 0.1),
        'a_subln_g': 1.0 + nrm(ks[10], (L, A_V), 0.01),
        'b_sinks': nrm(ks[11], (L, B_QHEADS), 0.5),
        'w_branch': nrm(ks[12], (L, N_BRANCH, BRANCH_WIDTH, D), BRANCH_WIDTH ** -0.5),
        'w_out': nrm(ks[13], (L, D, D), DEEPNORM_BETA * D ** -0.5),
        'ln1_g': 1.0 + nrm(ks[14], (L, D), 0.01),
        'ln1_b': nrm(ks[15], (L, D), 0.01),
        'w_exp_gate': nrm(ks[16], (L, E, D, F), D ** -0.5),
        'w_exp_up': nrm(ks[17], (L, E, D, F), D ** -0.5),
        'w_exp_down': nrm(ks[18], (L, E, F, D), DEEPNORM_BETA * F ** -0.5),
        'ln2_g': 1.0 + nrm(ks[19], (L, D), 0.01),
        'ln2_b': nrm(ks[20], (L, D), 0.01),
    }

def reference(x, c, rel_table, w_router, b_router, w_ada, b_ada, w_in, a_lambda_q, a_lambda_k,
              a_subln_g, b_sinks, w_branch, w_out, ln1_g, ln1_b, w_exp_gate, w_exp_up, w_exp_down,
              ln2_g, ln2_b):
    cond = jax.nn.silu(c)
    for l in range(DEPTH):
        mod = (cond @ w_ada[l] + b_ada[l])[:, None, :]
        shift_a, scale_a, gate_a, shift_f, scale_f, gate_f = jnp.split(mod, 6, axis=-1)
        u = x * (1.0 + scale_a) + shift_a
        y = hybrid_mixer(u, w_in[l], a_lambda_q[l], a_lambda_k[l], a_subln_g[l], b_sinks[l],
                         w_branch[l], w_out[l], rel_table, l)
        x = layer_norm(DEEPNORM_ALPHA * x + (1.0 + gate_a) * y, ln1_g[l], ln1_b[l])
        v = x * (1.0 + scale_f) + shift_f
        y = routed_moe(v, w_router, b_router, w_exp_gate[l], w_exp_up[l], w_exp_down[l])
        x = layer_norm(DEEPNORM_ALPHA * x + (1.0 + gate_f) * y, ln2_g[l], ln2_b[l])
    return x


_drawn_inputs = setup_inputs


def setup_inputs(seed=0):
    import zlib

    import numpy as np

    out = dict(_drawn_inputs(seed))
    spreads = {}
    factors = {'a_subln_g': 7.229, 'b_sinks': 23.08, 'ln2_g': 32.247, 'ln2_b': 33.487}
    for name, (base, spread) in spreads.items():
        noise = np.random.default_rng([zlib.crc32(name.encode()), seed]).standard_normal(out[name].shape)
        drawn = base * np.exp(spread * noise) if base else spread * noise
        out[name] = __import__('jax').numpy.asarray(drawn.astype(out[name].dtype))
    for name, factor in factors.items():
        out[name] = (out[name] * factor).astype(out[name].dtype)
    return out
```

```python
import math
from contextlib import ExitStack

import numpy as np
import concourse.bass as bass
from concourse import mybir

F32 = mybir.dt.float32
ALU = mybir.AluOpType
ACT = mybir.ActivationFunctionType
AX = mybir.AxisListType

P = 128
D = 1024
S = 1024
KT = D // P
NT = S // P
HALF = 512
HD = 64
NE = 16
FF = 256
ALPHA = 2.0 ** 0.25
EPS = 1e-5
LAM0 = 0.8 - 0.6 * math.exp(0.0)
TOPK = 256
MASKED = -1.0e30
TAKEN = -3.0e38
LOWEST = -3.4e38

SPLITS = (("a_q", 256), ("a_k", 256), ("a_v", 256), ("b_q", 256), ("b_k", 128), ("b_v", 128),
          ("c_q", 768), ("c_k", 768), ("c_v", 768), ("d_q", 256), ("d_k", 64), ("d_v", 64),
          ("i_q", 256), ("i_k", 32), ("i_w", 8), ("gate", 4096))
COL = {}
for _n, _w in SPLITS:
    COL[_n] = sum(w for _, w in SPLITS[:len(COL)])
IN_WIDTH = sum(w for _, w in SPLITS)

TABLES = (("A", 0, 1024, 1023, 1, 1023), ("B", 4, 256, 255, 1, 127), ("C0", 8, 256, 255, 1, 128),
          ("C1", 12, 256, 255, 4, 128), ("C2", 16, 128, 127, 8, 127), ("D", 20, 1024, 1023, 1, 1023))
TAB_OFF, _o = {}, 0
for _t in TABLES:
    TAB_OFF[_t[0]] = _o
    _o += _t[2] + P
TAB_W = _o


def table_constants():
    onehot = np.zeros((32, TAB_W), np.float32)
    mask = np.zeros((4, TAB_W), np.float32)
    for name, _, width, d0, dil, most in TABLES:
        for x in range(width + P):
            steps = d0 - x
            if 0 <= steps <= most and not (name == "C2" and steps % 2):
                n = steps * dil
                b = n if n < 16 else min(31, 16 + int(math.log(n / 16) / math.log(2048 / 16) * 16))
                onehot[b, TAB_OFF[name] + x] = 1.0
            else:
                mask[:, TAB_OFF[name] + x] = MASKED
    sel = np.zeros((4, 2, P), np.float32)
    for h in range(4):
        sel[h, h // 2, (h % 2) * 64:(h % 2) * 64 + 64] = 1.0
    blockones = np.zeros((P, P), np.float32)
    blockones[:64, :64] = blockones[64:, 64:] = 1.0 / 64
    tri = np.where(np.arange(P)[None, :] <= np.arange(P)[:, None], 0.0, MASKED).astype(np.float32)
    iota = np.broadcast_to(np.arange(16, dtype=np.float32) - 99.0, (P, 16)).copy()
    return dict(onehot=onehot, tabmask=mask, headsel=sel.reshape(4, 256), blockones=blockones,
                ident=np.eye(P, dtype=np.float32), causal=tri, iota=iota)


N_TAB = sum(-(-(x[2] + P) // HALF) for x in TABLES)


def build(nc, t, out, scratch):
    ctx = ExitStack()
    with ctx:
        def sb(name, shape, dt=F32):
            return ctx.enter_context(nc.sbuf_tensor(name, shape, dt))

        def sem(name):
            return ctx.enter_context(nc.semaphore(name))

        KB = 256
        uT_ = sb("uT", [P, KT, S])
        oT_ = sb("oT", [P, 4, 2, S])
        ring_ = sb("ring", [P, 2, KT * HALF])
        qkv_ = sb("qkv", [P, 32 * KB])
        strips_ = sb("strips", [P, 30 * KB])
        SR = sb("SR", [P, 4, S])
        PT = sb("PT", [P, 2, S])
        isel = sb("isel", [P, 4224])
        ident = sb("ident_sb", [P, P])
        causal = sb("causal_sb", [P, P])
        bones = sb("bones_sb", [P, P])
        hsel = sb("hsel_sb", [4, 2, P])
        iota = sb("iota_sb", [P, 16])
        badaT = sb("badaT", [P, 48])
        modT = sb("modT", [P, 48])
        cT = sb("cT", [P, 2, KT])
        lamq = sb("lamq", [32, 2, 2])
        lam = sb("lam", [P, 4])
        subg = sb("subg", [P, 1])
        sink = sb("sink", [P, 4])
        epsc = sb("epsc", [P, 1])
        lamw = sb("lamw", [P, 4])
        iw = sb("iw", [P, NT, 8])
        mx = sb("mx", [P, 224 + 8])
        negm = sb("negm", [P, 224 + 8])
        den = sb("den", [P, 224 + 8])
        rec = sb("rec", [P, 224 + 8])
        top8 = sb("top8", [P, 8])
        stats = sb("stats", [P, 2, 2, 6])
        mv = sb("mv", [P, 2, 2])
        sd = sb("sd", [P, 2])

        uT, oT = uT_, oT_
        ring = [ring_[:, i, :].rearrange("p (k n) -> p k n", k=KT) for i in range(2)]
        qT = qkv_[:, 0:2 * S].rearrange("p (a s) -> p a s", a=2)
        kT = qkv_[:, 2 * S:4 * S].rearrange("p (a s) -> p a s", a=2)
        V = qkv_[:, 4 * S:6 * S].rearrange("p (t n) -> p t n", t=NT)
        ikT = qkv_[:, 4 * S:5 * S]
        bm = qkv_[:, 6 * S:8 * S].rearrange("p (r s) -> p r s", r=2)
        xn = qkv_[:, 0:8 * S].rearrange("p (t n) -> p t n", t=NT)
        mrg = xn
        yacc = xn
        x1 = oT_[:, :, :, :].rearrange("p a b s -> p (a b) s")
        vT = uT_
        stripAD = strips_[:, 0:4 * S].rearrange("p (h s) -> p h s", h=4)
        stripB = strips_[:, 4 * S:5 * S].rearrange("p (h s) -> p h s", h=4)
        stripC = [strips_[:, 5 * S:6 * S].rearrange("p (h s) -> p h s", h=4),
                  strips_[:, 6 * S:7 * S].rearrange("p (h s) -> p h s", h=4),
                  strips_[:, 7 * S:7 * S + 512].rearrange("p (h s) -> p h s", h=4)]
        rows = strips_[:, 0:6 * S].rearrange("p (r s) -> p r s", r=6)

        pb = [ctx.enter_context(nc.psum_tensor(f"pb{i}", [P, HALF], F32)) for i in range(2)]
        psS = [ctx.enter_context(nc.psum_tensor(f"psS{i}", [P, S], F32)) for i in range(2)]
        psT = ctx.enter_context(nc.psum_tensor("psT", [P, S], F32))

        HSLOT = SR[:, 0:2, :].rearrange("p a (f s) -> p a f s", f=2)
        SIG = SR[:, 2:4, :].rearrange("p a (b s) -> p (a b) s", b=2)
        route = strips_[:, 6 * S:6 * S + 11 * P].rearrange("p (r t e) -> p r t e", r=11, t=NT)
        small = strips_[:, 6 * S + 11 * P:6 * S + 12 * P]
        pair = [(psT[:, 0:HALF], psT[:, HALF:S]), (pb[0][:], pb[1][:])]

        const_in = sem("const_in")
        x_in = sem("x_in")
        w_landed = [sem("w_landed0"), sem("w_landed1")]
        w_used = sem("w_used")
        cond_ready = sem("cond_ready")
        lam_ops = sem("lam_ops")
        lam_sum = sem("lam_sum")
        lam_exp = sem("lam_exp")
        mod_sum = sem("mod_sum")
        mod_ready = sem("mod_ready")
        out_ready, out_taken = sem("out_ready"), sem("out_taken")
        tab_ready, tab_taken, tab_out = sem("tab_ready"), sem("tab_taken"), sem("tab_out")
        shifted_out = sem("shifted_out")
        strip_in, stripAD_in = sem("strip_in"), sem("stripAD_in")
        scores_ready, scores_taken = sem("scores_ready"), sem("scores_taken")
        relu_taken = sem("relu_taken")
        relu_used = sem("relu_used")
        biased = sem("biased")
        probs_ready = sem("probs_ready")
        diff_ready = sem("diff_ready")
        pT_ready, pT_copied = sem("pT_ready"), sem("pT_copied")
        sel_ready, bm_ready = sem("sel_ready"), sem("bm_ready")
        a_biased = sem("a_biased")
        sink_exp = sem("sink_exp")
        cols_ready = sem("cols_ready")
        norm_ready, norm_taken = sem("norm_ready"), sem("norm_taken")
        shift_ready, shift_exp = sem("shift_ready"), sem("shift_exp")
        sq_ready, ms_ready, rms_ready = sem("sq_ready"), sem("ms_ready"), sem("rms_ready")
        sum_done = sem("sum_done")
        gate_ready, sig_ready, proj_ready, proj_taken = (sem(n) for n in ("gate_ready", "sig_ready", "proj_ready", "proj_taken"))
        wb_in, wb_used = [sem("wb_in0"), sem("wb_in1")], sem("wb_used")
        gcols_out, rows_in = sem("gcols_out"), sem("rows_in")
        wo_in, router_in = sem("wo_in"), sem("router_in")
        xr_in = [sem("xr_in0"), sem("xr_in1")]
        y_ready, y_taken, x1_ready = sem("y_ready"), sem("y_taken"), sem("x1_ready")
        var_ready, sd_ready = sem("var_ready"), sem("sd_ready")
        logit_ready, logit_max, logit_exp, route_ready = (sem(n) for n in ("logit_ready", "logit_max", "logit_exp", "route_ready"))
        e_in, e_used = [sem("e_in0"), sem("e_in1")], sem("e_used")
        gu_ready, gu_taken, gsig_ready = sem("gu_ready"), sem("gu_taken"), sem("gsig_ready")
        h_ready, h_used = sem("h_ready"), sem("h_used")
        down_ready, down_taken = sem("down_ready"), sem("down_taken")
        fin_ready, out_done = sem("fin_ready"), sem("out_done")
        phase = sem("phase")
        dve_step, act_step = sem("dve_step"), sem("act_step")

        w = t["w_in"][0]
        chunks = [[(t["w_ada"][0], HALF * c, HALF, 0)] for c in range(12)]
        chunks.append([(w, COL["i_q"], 256, 0)] + [(w, COL["i_k"], 32, 256 + 32 * r) for r in range(4)]
                      + [(w, COL["i_w"], 8, 384)])
        PROJ = {}

        def branch_chunks(name, q, k, v):
            PROJ[name] = len(chunks)
            chunks.append([(w, q, 256, 0)] + k)
            chunks.append([v])

        bk, dk = COL["b_k"], COL["d_k"]
        branch_chunks("B", COL["b_q"], [(w, bk, 64, 256), (w, bk, 64, 320), (w, bk + 64, 64, 384),
                                        (w, bk + 64, 64, 448)], (w, COL["b_v"], 128, 0))
        for g in range(3):
            branch_chunks(f"C{g}", COL["c_q"] + 256 * g, [(w, COL["c_k"] + 256 * g, 256, 256)],
                          (w, COL["c_v"] + 256 * g, 256, 0))
        branch_chunks("A", COL["a_q"], [(w, COL["a_k"], 256, 256)], (w, COL["a_v"], 256, 0))
        branch_chunks("D", COL["d_q"], [(w, dk, 64, 256), (w, dk, 64, 320)], (w, COL["d_v"], 64, 0))
        ORDER = ("B", "C0", "C1", "C2", "A", "D")
        VCOLS = {"A": 256, "B": 128, "C0": 256, "C1": 256, "C2": 256, "D": 64}
        KCOLS = {"A": 2, "B": 2, "C0": 2, "C1": 2, "C2": 2, "D": 1}
        BASE = {"B": 0, "C0": 32, "C1": 64, "C2": 96, "A": 128, "D": 192}
        N_IDX = 8 * (NT - 2)

        def units(name):
            for j in range(NT):
                for h in range(4):
                    if name in "AD":
                        yield h, j, 0, j + 1
                    elif name == "C1":
                        yield h, j, j - j % 2, j + 1
                    elif name == "C2":
                        yield h, j, j, j + 1
                    else:
                        yield h, j, max(0, j - 1), j + 1

        def pt_banks(k0, k1):
            return -(-(k1 - k0) // 4)

        BANKS, _n = {}, 0
        for _name in ORDER:
            for _i, (_, _, _k0, _k1) in enumerate(units(_name)):
                _n += pt_banks(_k0, _k1)
                for _m in range(2 if _name == "A" else 1):
                    BANKS[BASE[_name] + (2 * _i + _m if _name == "A" else _i)] = _n

        def bias_strip(name, h, n):
            if name in "AD":
                return stripAD[:, h, S - n:S]
            if name == "B":
                return stripB[:, h, 256 - n:256]
            g = int(name[1])
            return stripC[g][:, h, 256 - n:256] if g < 2 else stripC[g][:, h, 0:P]

        def idx_tile(j):
            at = sum((i + 1) * P for i in range(2, j))
            return isel[:, at:at + (j + 1) * P]

        def tile_tokens(ap, name, j):
            if name == "C1":
                return ap.rearrange("p (a r) -> p r a", r=4)[:, j // 2, (j % 2) * P:(j % 2) * P + P]
            if name == "C2":
                return ap.rearrange("p (a r) -> p r a", r=8)[:, j, :]
            return ap[:, j * P:(j + 1) * P]

        def half_in_order(dst, src, name, hf):
            if name in ("C1", "C2"):
                r = 4 if name == "C1" else 8
                n = HALF // r
                return (dst.rearrange("p (r a) -> p r a", r=r)[:, :, hf * n:(hf + 1) * n],
                        src.rearrange("p (a r) -> p r a", r=r))
            return dst[:, hf * HALF:(hf + 1) * HALF], src

        def rows_to_tokens(dst, src, name, hf):
            if name in ("C1", "C2"):
                r = 4 if name == "C1" else 8
                return (dst.rearrange("p (a r) -> p r a", r=r)[:, hf * r // 2:(hf + 1) * r // 2, :],
                        src.rearrange("p (r a) -> p r a", r=r // 2))
            return dst[:, hf * HALF:(hf + 1) * HALF], src

        RAW = {"A": 0, "B": 1, "C0": 2, "C1": 0, "C2": 3, "D": 3}

        def stand(eng, n):
            eng.drain().then_inc(phase, 1)
            eng.wait_ge(phase, 5 * n)

        onehot = SR[0:32, :, :].rearrange("p r s -> p (r s)")[:, 0:TAB_W]
        relt = PT[0:32, 0, 0:24]
        bcols = SR[:, 0:2, :].rearrange("p r (c n) -> p (r c n)", n=64)
        fac = [SR[0:4, g, :] for g in range(3)]
        fmax = SR[0:4, 3, :]
        fden = [PT[0:4, 0, :], PT[0:4, 1, :], bm[0:4, 0, :]]
        N_CONST = 15

        def down_w(e):
            return isel[:, (e % 2) * 2 * S:(e % 2 + 1) * 2 * S].rearrange("p (k n) -> p k n", k=2)

        OUTS = {"A": 16 + 6 + NT + 5 * (8 + NT + 32)}

        block = ctx.enter_context(nc.Block())

        @block.sync
        def _(sp):
            for a, b in ((ident[:], t["ident"]), (causal[:], t["causal"]), (bones[:], t["blockones"]),
                         (hsel[:], t["headsel"].rearrange("h (a p) -> h a p", a=2)), (iota[:], t["iota"]),
                         (onehot, t["onehot"]), (relt, t["rel_table"]),
                         (isel[0:4, 0:TAB_W], t["tabmask"]),
                         (cT[:, 0, :], t["c"][0].rearrange("(k p) -> p k", p=P)),
                         (badaT[:], t["b_ada"][0].rearrange("(k p) -> p k", p=P)),
                         (lamq[:, 0, :], t["a_lambda_q"][0].rearrange("m d -> d m")),
                         (lamq[:, 1, :], t["a_lambda_k"][0].rearrange("m d -> d m")),
                         (subg[0:64, :], t["a_subln_g"][0].rearrange("(d a) -> d a", a=1)),
                         (subg[64:128, :], t["a_subln_g"][0].rearrange("(d a) -> d a", a=1)),
                         (sink[:], t["b_sinks"][0:1, :].broadcast_to([P, 4]))):
                sp.dma_start(a, b, allow_slow_non_contiguous=True).then_inc(const_in, 16)

            def chunk(n):
                if n >= 2:
                    sp.wait_ge(w_used, n - 1)
                for src, c0, wd, at in chunks[n]:
                    sp.dma_start(ring[n % 2][:, :, at:at + wd],
                                 src[:, c0:c0 + wd].rearrange("(k p) n -> p k n", p=P)).then_inc(w_landed[n % 2], 16)

            chunk(0)
            chunk(1)
            for j in range(NT):
                sp.dma_start(xn[:, j, :], t["x"][0, j * P:(j + 1) * P, :]).then_inc(x_in, 16)
            sp.wait_ge(tab_taken, N_TAB)
            sp.dma_start(scratch["gtab"], isel[0:4, 0:TAB_W]).then_inc(tab_out, 16)
            sp.wait_ge(tab_out, 16)
            for h in range(4):
                sp.dma_start(scratch["shifted"][h, 0:P * (TAB_W + P + 1)].rearrange("(p n) -> p n", p=P)[:, 0:TAB_W],
                             scratch["gtab"][h:h + 1, :].broadcast_to([P, TAB_W])).then_inc(shifted_out, 16)
            sp.wait_ge(shifted_out, 64)

            def strip(dst, name, h, s):
                width = {x[0]: x[2] for x in TABLES}[name]
                c0 = TAB_OFF[name] + P - 1
                src = scratch["shifted"][h, 0:P * (TAB_W + P)].rearrange("(p n) -> p n", p=P)[:, c0:c0 + width]
                sp.dma_start(dst, src).then_inc(s, 16)

            for h in range(4):
                strip(stripB[:, h, :], "B", h, strip_in)
                for g in range(3):
                    strip(stripC[g][:, h, :], f"C{g}", h, strip_in)
                strip(stripAD[:, h, :], "A", h, stripAD_in)
            for n in range(2, PROJ["D"]):
                chunk(n)
                if n == 13:
                    sp.wait_ge(mod_ready, 1)
                    for r, c0 in ((0, 16), (1, 40)):
                        sp.dma_start(scratch["gates"][r].rearrange("(k p) -> p k", p=P), modT[:, c0:c0 + 8],
                                     allow_slow_non_contiguous=True).then_inc(gcols_out, 16)
            sp.wait_ge(a_biased, 1)
            for h in range(4):
                strip(stripAD[:, h, :], "D", h, stripAD_in)
            for n in range(PROJ["D"], len(chunks)):
                chunk(n)
            stand(sp, 1)
            sp.wait_ge(gcols_out, 32)
            for r, src in enumerate((scratch["gates"][0:1, :], t["ln1_g"], t["ln1_b"],
                                     scratch["gates"][1:2, :], t["ln2_g"], t["ln2_b"])):
                sp.dma_start(rows[:, r, :], src.broadcast_to([P, D])).then_inc(rows_in, 16)
            for d in range(KT):
                if d >= 2:
                    sp.wait_ge(wb_used, d - 1)
                for b in range(4):
                    c0 = COL["gate"] + b * D + d * P
                    sp.dma_start(ring[d % 2][:, :, b * P:(b + 1) * P],
                                 w[:, c0:c0 + P].rearrange("(k p) n -> p k n", p=P)).then_inc(wb_in[d % 2], 16)
                    sp.dma_start(PT[:, d % 2, b * 256:(b + 1) * 256].rearrange("p (k n) -> p k n", k=2),
                                 t["w_branch"][0, b, :, d * P:(d + 1) * P].rearrange("(k p) n -> p k n", p=P)
                                 ).then_inc(wb_in[d % 2], 16)
            stand(sp, 2)
            for hf in range(2):
                sp.dma_start(ring[hf], t["w_out"][0][:, hf * HALF:(hf + 1) * HALF]
                             .rearrange("(k p) n -> p k n", p=P)).then_inc(wo_in, 16)
            for j in range(NT):
                if j >= 2:
                    sp.wait_ge(x1_ready, j - 1)
                sp.dma_start(SR[:, j % 2, :], t["x"][0, j * P:(j + 1) * P, :]).then_inc(xr_in[j % 2], 16)
            stand(sp, 3)
            sp.dma_start(PT[:, 0, 0:P].rearrange("p (k e) -> p k e", k=KT),
                         t["w_router"].rearrange("(k p) e -> p k e", p=P)).then_inc(router_in, 16)
            sp.dma_start(PT[:, 0, P:P + NE], t["b_router"].rearrange("(a n) -> a n", a=1).broadcast_to([P, NE])
                         ).then_inc(router_in, 16)
            for e in range(NE):
                if e >= 2:
                    sp.wait_ge(e_used, e - 1)
                for at, name in ((0, "w_exp_gate"), (FF, "w_exp_up")):
                    sp.dma_start(ring[e % 2][:, :, at:at + FF],
                                 t[name][0, e].rearrange("(k p) n -> p k n", p=P)).then_inc(e_in[e % 2], 16)
                sp.dma_start(down_w(e), t["w_exp_down"][0, e].rearrange("(k p) n -> p k n", p=P)
                             ).then_inc(e_in[e % 2], 16)
            for j in range(NT):
                sp.wait_ge(fin_ready, j + 1)
                sp.dma_start(out[0, j * P:(j + 1) * P, :], yacc[:, j, :]).then_inc(out_done, 16)
            sp.wait_ge(out_done, 16 * NT)

        @block.tensor
        def _(pe):
            mm = nc.tensor.matmul
            n_out = 0
            n_norm = 0
            s = 0
            n_pt = 0
            n_diff = 0
            last_pt = {0: 0, 1: 0}

            def landed(n):
                pe.wait_ge(w_landed[n % 2], 16 * sum(len(chunks[i]) for i in range(n % 2, n + 1, 2)))

            def bank():
                if n_out >= 2:
                    pe.wait_ge(out_taken, n_out - 1)
                return pb[n_out % 2]

            def norm_bank():
                if n_norm >= 2:
                    pe.wait_ge(norm_taken, n_norm - 1)
                return psT[:, (n_norm % 2) * HALF:(n_norm % 2 + 1) * HALF]

            pe.wait_ge(const_in, 16 * N_CONST)
            n = 0
            for name, h0, width, *_ in TABLES:
                for c in range(0, width + P, HALF):
                    wd = min(HALF, width + P - c)
                    if n >= 2:
                        pe.wait_ge(tab_taken, n - 1)
                    at = TAB_OFF[name] + c
                    mm(psS[n % 2][0:4, 0:wd], PT[0:32, 0, h0:h0 + 4], onehot[:, at:at + wd],
                       start=True, stop=True).then_inc(tab_ready, 1)
                    n += 1
            pe.wait_ge(lam_ops, 1)
            mm(psT[:, HALF:HALF + 2], PT[0:32, 1, 0:P], PT[0:32, 1, P:P + 2], start=True, stop=True).then_inc(lam_sum, 1)
            pe.wait_ge(cond_ready, 1)
            for c in range(12):
                landed(c)
                for m in range(4):
                    for k in range(KT):
                        last = mm(psT[:, 4 * c + m:4 * c + m + 1], ring[c % 2][:, k, m * P:(m + 1) * P],
                                  cT[:, 1, k:k + 1], start=(k == 0), stop=(k == KT - 1))
                last.then_inc(w_used, 1)
            pe.drain().then_inc(mod_sum, 1)
            pe.wait_ge(x_in, 16 * NT)
            for k in range(KT):
                for hf in range(2):
                    o = bank()
                    for q in range(4):
                        last = nc.tensor.transpose(o[:, q * P:(q + 1) * P], xn[:, 4 * hf + q, k * P:(k + 1) * P], ident[:])
                    last.then_inc(out_ready, 1)
                    n_out += 1
            pe.wait_ge(out_taken, n_out)

            def project_T(n, cols):
                nonlocal n_out
                for c in range(cols):
                    for hf in range(2):
                        o = bank()
                        for k in range(KT):
                            last = mm(o[:], ring[n % 2][:, k, c * P:(c + 1) * P], uT[:, k, hf * HALF:(hf + 1) * HALF],
                                      start=(k == 0), stop=(k == KT - 1))
                        last.then_inc(out_ready, 1)
                        n_out += 1

            def project_V(n, name, cols, at=0):
                nonlocal n_out
                for j in range(NT):
                    o = bank()
                    for k in range(KT):
                        last = mm(o[:, 0:cols], tile_tokens(uT[:, k, :], name, j), ring[n % 2][:, k, at:at + cols],
                                  start=(k == 0), stop=(k == KT - 1))
                    last.then_inc(out_ready, 1)
                    n_out += 1

            landed(12)
            project_T(12, 3)
            project_V(12, "I", 8, 384)
            pe.drain().then_inc(w_used, 1)
            pe.wait_ge(out_taken, n_out)
            for j in range(2, NT):
                for h in range(8):
                    if s >= 2:
                        pe.wait_ge(relu_taken, s - 1)
                    r = 32 * (h % 4)
                    for c in range(0, (j + 1) * P, HALF):
                        wd = min(HALF, (j + 1) * P - c)
                        last = mm(psS[s % 2][:, c:c + wd], qT[r:r + 32, h // 4, j * P:(j + 1) * P],
                                  ikT[r:r + 32, c:c + wd], start=True, stop=True)
                    last.then_inc(scores_ready, 1)
                    s += 1
            pe.wait_ge(relu_taken, s)

            for name in ORDER:
                n = PROJ[name]
                landed(n)
                project_T(n, 2 + KCOLS[name])
                pe.drain().then_inc(w_used, 1)
                landed(n + 1)
                project_V(n + 1, name, VCOLS[name])
                pe.drain().then_inc(w_used, 1)
                pe.wait_ge(out_taken, n_out)
                todo = list(units(name))

                def score(i):
                    nonlocal s
                    h, j, k0, k1 = todo[i]
                    for m in range(2 if name == "A" else 1):
                        if s >= N_IDX + 2:
                            pe.wait_ge(scores_taken, s - N_IDX - 1)
                        r, K = ((h % 2) * 64 + 32 * m, 32) if name == "A" else ((h % 2) * 64, 64)
                        keys = kT[:, 0 if name == "D" else h // 2, :]
                        for c in range(k0 * P, k1 * P, HALF):
                            wd = min(HALF, k1 * P - c)
                            last = mm(psS[s % 2][:, c - k0 * P:c - k0 * P + wd],
                                      qT[r:r + K, h // 2, j * P:(j + 1) * P], keys[r:r + K, c:c + wd],
                                      start=True, stop=True)
                        last.then_inc(scores_ready, 1)
                        s += 1

                def transpose_probs(i):
                    nonlocal n_pt, n_diff
                    h, j, k0, k1 = todo[i]
                    if name == "A":
                        n_diff += 1
                        pe.wait_ge(diff_ready, n_diff)
                        slot = (BASE["A"] + 2 * i) % 4
                    else:
                        pe.wait_ge(probs_ready, BASE[name] + i + 1)
                        slot = (BASE[name] + i) % 4
                    for b, c in enumerate(range(k0, k1, 4)):
                        if last_pt[b]:
                            pe.wait_ge(pT_copied, last_pt[b])
                        for q in range(c, min(c + 4, k1)):
                            last = nc.tensor.transpose(psT[:, (q - k0) * P:(q - k0 + 1) * P],
                                                       SR[:, slot, (q - k0) * P:(q - k0 + 1) * P], ident[:])
                        last.then_inc(pT_ready, 1)
                        n_pt += 1
                        last_pt[b] = n_pt

                def weigh_values(i):
                    nonlocal n_out
                    h, j, k0, k1 = todo[i]
                    u = ORDER.index(name) * 32 + i
                    pe.wait_ge(pT_copied, BANKS[BASE[name] + (2 * i if name == "A" else i)])
                    o = bank()
                    vh = {"B": h // 2, "D": 0}.get(name, h)
                    for q in range(k0, k1):
                        last = mm(o[0:64, 0:P], V[:, q, vh * HD:(vh + 1) * HD],
                                  PT[:, u % 2, (q - k0) * P:(q - k0 + 1) * P], start=(q == k0), stop=(q == k1 - 1))
                    last.then_inc(out_ready, 1)
                    n_out += 1

                for i in range(-2, len(todo)):
                    if i + 2 < len(todo):
                        score(i + 2)
                    if 0 <= i + 1 < len(todo):
                        transpose_probs(i + 1)
                    if i >= 0:
                        weigh_values(i)
                pe.wait_ge(pT_copied, n_pt)
                pe.wait_ge(out_taken, n_out)
                if name in ("B", "D"):
                    pe.wait_ge(cols_ready, 1 if name == "B" else 3)
                    for pr in range(2):
                        for hf in range(2):
                            o = norm_bank()
                            for q in range(4):
                                c0 = (4 * (4 * hf + q) + 2 * pr) * 64
                                last = nc.tensor.transpose(o[:, q * P:(q + 1) * P], bcols[:, c0:c0 + P], ident[:])
                            last.then_inc(norm_ready, 1)
                            n_norm += 1
                if name == "C2":
                    for g in range(3):
                        for stat in (mx, den):
                            for hf in range(2):
                                o = norm_bank()
                                for q in range(4):
                                    c0 = BASE[f"C{g}"] + 4 * (4 * hf + q)
                                    last = nc.tensor.transpose(o[0:4, q * P:(q + 1) * P], stat[:, c0:c0 + 4], ident[:])
                                last.then_inc(norm_ready, 1)
                                n_norm += 1
                    pe.wait_ge(cols_ready, 2)
                    for g in range(3):
                        for pr in range(2):
                            for hf in range(2):
                                mm(norm_bank(), hsel[:, pr, :], fac[g][:, hf * HALF:(hf + 1) * HALF],
                                   start=True, stop=True).then_inc(norm_ready, 1)
                                n_norm += 1
                if name == "A":
                    for i in range(4):
                        pe.wait_ge(sq_ready, i + 1)
                        mm(norm_bank(), bones[:], bm[:, i % 2, 0:HALF], start=True, stop=True).then_inc(norm_ready, 1)
                        n_norm += 1
                if n_norm:
                    pe.wait_ge(norm_taken, n_norm)
            stand(pe, 1)

            n = 0
            for d in range(KT):
                pe.wait_ge(wb_in[d % 2], 16 * 8 * (d // 2 + 1))
                for b in range(4):
                    if n >= 2:
                        pe.wait_ge(sig_ready, n - 1)
                    for hf in range(2):
                        for k in range(KT):
                            last = mm(psS[n % 2][:, hf * HALF:(hf + 1) * HALF], ring[d % 2][:, k, b * P:(b + 1) * P],
                                      uT[:, k, hf * HALF:(hf + 1) * HALF], start=(k == 0), stop=(k == KT - 1))
                    last.then_inc(gate_ready, 1)
                    if n >= 2:
                        pe.wait_ge(proj_taken, n - 1)
                    for hf in range(2):
                        for k in range(2):
                            last = mm(pair[n % 2][hf], PT[:, d % 2, b * 256 + k * P:b * 256 + (k + 1) * P],
                                      oT[:, b, k, hf * HALF:(hf + 1) * HALF], start=(k == 0), stop=(k == 1))
                    last.then_inc(proj_ready, 1)
                    n += 1
                pe.drain().then_inc(wb_used, 1)
            stand(pe, 2)

            pe.wait_ge(wo_in, 32)

            def to_vT(j):
                nonlocal n_out
                pe.wait_ge(x1_ready, j + 1)
                for hf in range(2):
                    o = bank()
                    for q in range(4):
                        k = 4 * hf + q
                        last = nc.tensor.transpose(o[:, q * P:(q + 1) * P], x1[:, j, k * P:(k + 1) * P], ident[:])
                    last.then_inc(out_ready, 1)
                    n_out += 1

            for j in range(NT):
                if j >= 2:
                    pe.wait_ge(y_taken, j - 1)
                for hf in range(2):
                    for k in range(KT):
                        last = mm(psS[j % 2][:, hf * HALF:(hf + 1) * HALF], mrg[:, k, j * P:(j + 1) * P], ring[hf][:, k, :],
                                  start=(k == 0), stop=(k == KT - 1))
                last.then_inc(y_ready, 1)
                if j >= 2:
                    to_vT(j - 2)
            to_vT(NT - 2)
            to_vT(NT - 1)
            pe.wait_ge(out_taken, n_out)
            stand(pe, 3)

            pe.wait_ge(router_in, 32)
            for j in range(NT):
                for k in range(KT):
                    last = mm(psT[:, j * NE:(j + 1) * NE], vT[:, k, j * P:(j + 1) * P],
                              PT[:, 0, k * NE:(k + 1) * NE], start=(k == 0), stop=(k == KT - 1))
            last.then_inc(logit_ready, 1)
            n = m = 0
            for e in range(NE):
                pe.wait_ge(e_in[e % 2], 48 * (e // 2 + 1))
                for hf in range(2):
                    for f in range(2):
                        if n >= 2:
                            pe.wait_ge(gu_taken, n - 1)
                        for g in range(2):
                            for k in range(KT):
                                last = mm(psS[n % 2][:, g * HALF:(g + 1) * HALF],
                                          ring[e % 2][:, k, g * FF + f * P:g * FF + (f + 1) * P],
                                          vT[:, k, hf * HALF:(hf + 1) * HALF], start=(k == 0), stop=(k == KT - 1))
                        last.then_inc(gu_ready, 1)
                        n += 1
                if e == 0:
                    pe.wait_ge(route_ready, 1)
                for hf in range(2):
                    pe.wait_ge(h_ready, 4 * e + 2 * hf + 2)
                    for j in range(4 * hf, 4 * hf + 4):
                        if m >= 2:
                            pe.wait_ge(down_taken, m - 1)
                        for c in range(2):
                            for f in range(2):
                                last = mm(pair[m % 2][c], HSLOT[:, hf, f, (j % 4) * P:(j % 4 + 1) * P],
                                          down_w(e)[:, f, c * HALF:(c + 1) * HALF], start=(f == 0), stop=(f == 1))
                        last.then_inc(down_ready, 1)
                        m += 1
                    pe.drain().then_inc(h_used, 1)
                pe.drain().then_inc(e_used, 1)

        @block.scalar
        def _(act):
            fn = nc.scalar.activation
            n_out = n_self = n_pt = n_vT = 0

            def take(dst, src, scale=1.0, bias=None):
                nonlocal n_out
                act.wait_ge(out_ready, n_out + 1)
                if bias is None:
                    ins = fn(dst, src, ACT.Copy, scale=scale)
                else:
                    ins = fn(dst, src, ACT.Identity, scale=scale, bias=bias)
                ins.then_inc(out_taken, 1)
                n_out += 1

            def nxt():
                return pb[n_out % 2]

            act.wait_ge(const_in, 16 * N_CONST)
            fn(cT[:, 1, :], cT[:, 0, :], ACT.Exp, scale=-1.0).then_inc(act_step, 1)
            act.wait_ge(lam_sum, 1)
            fn(lam[:, 0:2], psT[:, HALF:HALF + 2], ACT.Exp).then_inc(lam_exp, 1)
            act.wait_ge(mod_ready, 1)
            for k in range(KT):
                for hf in range(2):
                    take(uT[:, k, hf * HALF:(hf + 1) * HALF], nxt()[:], scale=modT[:, 8 + k:9 + k], bias=modT[:, k:k + 1])
            for c in range(3):
                for hf in range(2):
                    dst = qT[:, c, :] if c < 2 else ikT
                    take(dst[:, hf * HALF:(hf + 1) * HALF], nxt()[:])
            for j in range(NT):
                take(iw[:, j, :], nxt()[:, 0:8])
            s = 0
            for j in range(2, NT):
                for h in range(8):
                    act.wait_ge(scores_ready, s + 1)
                    if s >= 4:
                        act.wait_ge(relu_used, s - 3)
                    fn(SR[:, s % 4, 0:(j + 1) * P], psS[s % 2][:, 0:(j + 1) * P], ACT.Relu).then_inc(relu_taken, 1)
                    s += 1

            for name in ORDER:
                scale = (32 if name == "A" else 64) ** -0.5
                for c in range(2 + KCOLS[name]):
                    for hf in range(2):
                        dst, src = half_in_order(qT[:, c, :] if c < 2 else kT[:, c - 2, :], nxt()[:], name, hf)
                        take(dst, src, scale=scale if c < 2 else 1.0)
                for j in range(NT):
                    take(V[:, j, 0:VCOLS[name]], nxt()[:, 0:VCOLS[name]])
                todo = list(units(name))

                def exps(i):
                    h, j, k0, k1 = todo[i]
                    n = (k1 - k0) * P
                    for m in range(2 if name == "A" else 1):
                        a = BASE[name] + (2 * i + m if name == "A" else i)
                        act.wait_ge(biased, a + 1)
                        fn(SR[:, a % 4, 0:n], SR[:, a % 4, 0:n], ACT.Exp, bias=negm[:, a:a + 1],
                           accum_out=den[:, a:a + 1]).then_inc(probs_ready, 1)

                def copy_probs(i):
                    nonlocal n_pt
                    h, j, k0, k1 = todo[i]
                    u = ORDER.index(name) * 32 + i
                    if u >= 2 and i < 2:
                        pass
                    elif i >= 2:
                        act.wait_ge(out_ready, n_out)
                    for b, c in enumerate(range(k0, k1, 4)):
                        wd = (min(c + 4, k1) - c) * P
                        act.wait_ge(pT_ready, n_pt + 1)
                        fn(PT[:, u % 2, b * HALF:b * HALF + wd], psT[:, b * HALF:b * HALF + wd], ACT.Copy).then_inc(pT_copied, 1)
                        n_pt += 1

                def take_output(i):
                    h, j, k0, k1 = todo[i]
                    dst = tile_tokens(oT[:, RAW[name], h // 2, :], name, j)
                    take(dst[(h % 2) * 64:(h % 2) * 64 + 64], nxt()[0:64, 0:P])

                for i in range(-2, len(todo)):
                    if i + 2 < len(todo):
                        exps(i + 2)
                    if 0 <= i + 1 < len(todo):
                        copy_probs(i + 1)
                    if i >= 0:
                        take_output(i)
                if name == "B":
                    for h in range(4):
                        ins = fn(rec[:, h:32:4], negm[:, h:32:4], ACT.Exp, bias=sink[:, h:h + 1])
                    ins.then_inc(sink_exp, 1)
                if name == "C2":
                    for g in range(3):
                        act.wait_ge(shift_ready, g + 1)
                        fn(fac[g], fac[g], ACT.Exp).then_inc(shift_exp, 1)
                if name == "A":
                    for i in range(4):
                        act.wait_ge(ms_ready, i + 1)
                        fn(bm[:, i % 2, 0:HALF], bm[:, i % 2, 0:HALF], ACT.Sqrt, bias=epsc[:]).then_inc(rms_ready, 1)
            stand(act, 1)

            for n in range(4 * KT):
                act.wait_ge(gate_ready, n + 1)
                if n >= 4:
                    act.wait_ge(proj_taken, n - 3)
                fn(SR[:, n % 4, :], psS[n % 2][:], ACT.Sigmoid).then_inc(sig_ready, 1)
            stand(act, 2)

            def take_vT(j):
                nonlocal n_out
                for hf in range(2):
                    act.wait_ge(out_ready, n_out + 1)
                    for q in range(4):
                        k = 4 * hf + q
                        ins = fn(vT[:, k, j * P:(j + 1) * P], pb[n_out % 2][:, q * P:(q + 1) * P], ACT.Identity,
                                 scale=modT[:, 32 + k:33 + k], bias=modT[:, 24 + k:25 + k])
                    ins.then_inc(out_taken, 1)
                    n_out += 1

            for j in range(NT):
                act.wait_ge(var_ready, j + 1)
                fn(sd[:, 0:1], mv[:, 0, 1:2], ACT.Sqrt, bias=epsc[:]).then_inc(sd_ready, 1)
                if j >= 2:
                    take_vT(j - 2)
            take_vT(NT - 2)
            take_vT(NT - 1)
            stand(act, 3)

            act.wait_ge(logit_max, 1)
            fn(route[:, 0], route[:, 0], ACT.Exp).then_inc(logit_exp, 1)
            for n in range(4 * NE):
                act.wait_ge(gu_ready, n + 1)
                if n >= 2:
                    act.wait_ge(gu_taken, n - 1)
                fn(SIG[:, n % 2, :], psS[n % 2][:, 0:HALF], ACT.Sigmoid).then_inc(gsig_ready, 1)
            for j in range(NT):
                act.wait_ge(var_ready, NT + j + 1)
                fn(sd[:, 0:1], mv[:, 0, 1:2], ACT.Sqrt, bias=epsc[:]).then_inc(sd_ready, 1)

        @block.gpsimd
        def _(pool):
            pool.wait_ge(stripAD_in, 128)
            n = 0
            for j in range(2, NT):
                pool.wait_ge(sel_ready, j - 1)
                for h in range(4):
                    if n >= 2:
                        pool.wait_ge(biased, BASE["D"] + 8 + n - 1)
                    elif n == 0:
                        pool.wait_ge(norm_taken, 4 + 24 + 4)
                        pool.wait_ge(sum_done, 2)
                    wd = (j + 1) * P
                    nc.gpsimd.tensor_tensor(bm[:, n % 2, 0:wd], stripAD[:, h, S - wd:S], idx_tile(j), ALU.add
                                            ).then_inc(bm_ready, 1)
                    n += 1
            stand(pool, 1)
            stand(pool, 2)
            stand(pool, 3)

        @block.vector
        def _(dve):
            v = nc.vector
            n_self = 0

            def step(ins):
                nonlocal n_self
                n_self += 1
                ins.then_inc(dve_step, 1)
                dve.wait_ge(dve_step, n_self)

            v.memset(epsc[:], EPS)
            dve.wait_ge(const_in, 16 * N_CONST)
            v.memset(PT[0:32, 1, 0:P], 1.0)
            v.tensor_tensor(PT[0:32, 1, P:P + 2], lamq[:, 0, :], lamq[:, 1, :], ALU.mult).then_inc(lam_ops, 1)
            dve.wait_ge(act_step, 1)
            step(v.tensor_scalar(cT[:, 1, :], cT[:, 1, :], 1.0, None, ALU.add))
            step(v.reciprocal(cT[:, 1, :], cT[:, 1, :]))
            v.tensor_tensor(cT[:, 1, :], cT[:, 1, :], cT[:, 0, :], ALU.mult).then_inc(cond_ready, 1)
            n = 0
            for name, h0, width, *_ in TABLES:
                for c in range(0, width + P, HALF):
                    wd = min(HALF, width + P - c)
                    at = TAB_OFF[name] + c
                    dve.wait_ge(tab_ready, n + 1)
                    v.tensor_tensor(isel[0:4, at:at + wd], psS[n % 2][0:4, 0:wd], isel[0:4, at:at + wd], ALU.add
                                    ).then_inc(tab_taken, 1)
                    n += 1
            dve.wait_ge(lam_exp, 1)
            step(v.tensor_tensor(lam[:, 2:3], lam[:, 1:2], lam[:, 0:1], ALU.subtract))
            step(v.tensor_scalar(lam[:, 3:4], lam[:, 2:3], -LAM0, None, ALU.add))
            step(v.tensor_scalar(subg[:], subg[:], 1.0 - LAM0, None, ALU.mult))
            dve.wait_ge(mod_sum, 1)
            step(v.tensor_tensor(modT[:], psT[:, 0:48], badaT[:], ALU.add))
            for c0 in (8, 16, 32):
                step(v.tensor_scalar(modT[:, c0:c0 + 8], modT[:, c0:c0 + 8], 1.0, None, ALU.add))
            v.tensor_scalar(modT[:, 40:48], modT[:, 40:48], 1.0, None, ALU.add).then_inc(mod_ready, 1)

            dve.wait_ge(tab_out, 16)
            s = 0
            for j in range(2, NT):
                acc = idx_tile(j)
                wd = (j + 1) * P
                for h in range(8):
                    dve.wait_ge(relu_taken, s + 1)
                    if h == 0:
                        ins = v.tensor_scalar(acc, SR[:, s % 4, 0:wd], iw[:, j, 0:1], None, ALU.mult)
                    else:
                        ins = v.scalar_tensor_tensor(acc, SR[:, s % 4, 0:wd], iw[:, j, h:h + 1], acc, ALU.mult, ALU.add)
                    ins.then_inc(relu_used, 1)
                    s += 1
                    dve.wait_ge(relu_used, s)
                step(v.tensor_tensor(acc[:, j * P:], acc[:, j * P:], causal[:], ALU.add))

            def top_k(j):
                acc = idx_tile(j)
                for _ in range(TOPK // 8):
                    step(v.max(top8[:], acc))
                    step(v.match_replace(acc, top8[:], acc, TAKEN))
                v.tensor_scalar(acc, acc, TAKEN, MASKED, ALU.not_equal, ALU.mult).then_inc(sel_ready, 1)

            n_norm = n_diff = 0

            def norm_src():
                nonlocal n_norm
                dve.wait_ge(norm_ready, n_norm + 1)
                n_norm += 1
                return psT[:, ((n_norm - 1) % 2) * HALF:((n_norm - 1) % 2 + 1) * HALF]

            TOPS = {"B": (2, 3), "C0": (4,), "C1": (5,), "C2": (6,), "A": (7,), "D": ()}
            for name in ORDER:
                for j in TOPS[name]:
                    top_k(j)
                if name == "B":
                    dve.wait_ge(strip_in, 16 * 16)
                if name == "A":
                    dve.wait_ge(stripAD_in, 64)
                if name == "D":
                    dve.wait_ge(stripAD_in, 128)
                for i, (h, j, k0, k1) in enumerate(units(name)):
                    wd = (k1 - k0) * P
                    maps = 2 if name == "A" else 1
                    for m in range(maps):
                        a = BASE[name] + maps * i + m
                        dve.wait_ge(scores_ready, N_IDX + a + 1)
                        if a >= 4:
                            dve.wait_ge(pT_ready, BANKS[a - 4])
                        if name == "D" and j >= 2:
                            n = 4 * (j - 2) + h
                            dve.wait_ge(bm_ready, n + 1)
                            bias = bm[:, n % 2, 0:wd]
                        else:
                            bias = bias_strip(name, h, wd)
                        v.tensor_tensor_reduce(out=SR[:, a % 4, 0:wd], in0=psS[a % 2][:, 0:wd], in1=bias, scale=1.0,
                                               scalar=sink[:, h:h + 1] if name == "B" else LOWEST,
                                               op0=ALU.add, op1=ALU.max, accum_out=mx[:, a:a + 1]).then_inc(scores_taken, 1)
                        dve.wait_ge(scores_taken, a + 1)
                        v.tensor_scalar(negm[:, a:a + 1], mx[:, a:a + 1], -1.0, None, ALU.mult).then_inc(biased, 1)
                    if name == "A":
                        if i == 31:
                            dve.wait_ge(biased, a + 1)
                            dve.sem_inc(a_biased, 1)
                        for q in ([i - 1] if i else []) + ([31] if i == 31 else []):
                            hh, jj = q % 4, q // 4
                            wq = (jj + 1) * P
                            a0 = BASE["A"] + 2 * q
                            dve.wait_ge(probs_ready, a0 + 2)
                            step(v.reciprocal(rec[:, a0:a0 + 2], den[:, a0:a0 + 2]))
                            step(v.tensor_tensor(rec[:, a0 + 1:a0 + 2], rec[:, a0 + 1:a0 + 2], lam[:, 3:4], ALU.mult))
                            s0, s1 = a0 % 4, (a0 + 1) % 4
                            step(v.tensor_scalar(SR[:, s1, 0:wq], SR[:, s1, 0:wq], rec[:, a0 + 1:a0 + 2], None, ALU.mult))
                            v.scalar_tensor_tensor(SR[:, s0, 0:wq], SR[:, s0, 0:wq], rec[:, a0:a0 + 1], SR[:, s1, 0:wq],
                                                   ALU.mult, ALU.add).then_inc(diff_ready, 1)
                if name in ("B", "D"):
                    a0 = BASE[name]
                    dve.wait_ge(probs_ready, a0 + 32)
                    if name == "B":
                        dve.wait_ge(sink_exp, 1)
                        step(v.tensor_tensor(den[:, 0:32], den[:, 0:32], rec[:, 0:32], ALU.add))
                    step(v.reciprocal(rec[:, a0:a0 + 32], den[:, a0:a0 + 32]))
                    dve.wait_ge(pT_ready, BANKS[a0 + 31])
                    v.tensor_copy(bcols.rearrange("p (c n) -> p c n", n=64),
                                  rec[:, a0:a0 + 32].unsqueeze(2).broadcast_to([P, 32, 64])).then_inc(cols_ready, 1)
                    for pr in range(2):
                        for hf in range(2):
                            o = oT[:, RAW[name], pr, hf * HALF:(hf + 1) * HALF]
                            v.tensor_tensor(o, norm_src(), o, ALU.mult).then_inc(norm_taken, 1)
                if name == "C2":
                    for g in range(3):
                        for st in (fac[g], fden[g]):
                            for hf in range(2):
                                dst, src = rows_to_tokens(st, norm_src()[0:4, :], f"C{g}", hf)
                                v.tensor_copy(dst, src).then_inc(norm_taken, 1)
                    dve.wait_ge(norm_taken, n_norm)
                    step(v.tensor_tensor(fmax, fac[0], fac[1], ALU.max))
                    step(v.tensor_tensor(fmax, fmax, fac[2], ALU.max))
                    for g in range(3):
                        v.tensor_tensor(fac[g], fac[g], fmax, ALU.subtract).then_inc(shift_ready, 1)
                    dve.wait_ge(shift_ready, 3)
                    for g in range(3):
                        dve.wait_ge(shift_exp, g + 1)
                        step(v.tensor_tensor(fden[g], fden[g], fac[g], ALU.mult))
                        if g:
                            step(v.tensor_tensor(fden[0], fden[0], fden[g], ALU.add))
                    step(v.reciprocal(fden[0], fden[0]))
                    for g in range(3):
                        ins = v.tensor_tensor(fac[g], fac[g], fden[0], ALU.mult)
                        if g < 2:
                            step(ins)
                    ins.then_inc(cols_ready, 1)
                    for g in range(3):
                        for pr in range(2):
                            for hf in range(2):
                                o = oT[:, RAW[f"C{g}"], pr, hf * HALF:(hf + 1) * HALF]
                                v.tensor_tensor(o, norm_src(), o, ALU.mult).then_inc(norm_taken, 1)
                                dve.wait_ge(norm_taken, n_norm)
                                if g:
                                    o0 = oT[:, 2, pr, hf * HALF:(hf + 1) * HALF]
                                    step(v.tensor_tensor(o0, o0, o, ALU.add))
                    dve.sem_inc(sum_done, 1)
                if name == "A":
                    for i in range(4):
                        if i == 0:
                            dve.wait_ge(out_taken, OUTS["A"])
                        o = oT[:, 0, i // 2, (i % 2) * HALF:(i % 2 + 1) * HALF]
                        v.tensor_tensor(bm[:, i % 2, 0:HALF], o, o, ALU.mult).then_inc(sq_ready, 1)
                        v.tensor_copy(bm[:, i % 2, 0:HALF], norm_src()).then_inc(norm_taken, 1)
                        dve.wait_ge(norm_taken, n_norm)
                        dve.sem_inc(ms_ready, 1)
                        dve.wait_ge(rms_ready, i + 1)
                        step(v.reciprocal(bm[:, i % 2, 0:HALF], bm[:, i % 2, 0:HALF]))
                        step(v.scalar_tensor_tensor(o, o, subg[:], bm[:, i % 2, 0:HALF], ALU.mult, ALU.mult))
                    dve.sem_inc(sum_done, 1)
            stand(dve, 1)

            for n in range(4 * KT):
                d, b = n // 4, n % 4
                dve.wait_ge(sig_ready, n + 1)
                dve.wait_ge(proj_ready, n + 1)
                for hf in range(2):
                    o = mrg[:, d, hf * HALF:(hf + 1) * HALF]
                    g = SR[:, n % 4, hf * HALF:(hf + 1) * HALF]
                    ins = v.tensor_tensor(g if b else o, pair[n % 2][hf], g, ALU.mult)
                ins.then_inc(proj_taken, 1)
                dve.wait_ge(proj_taken, n + 1)
                if b:
                    step(v.tensor_tensor(mrg[:, d, :], mrg[:, d, :], SR[:, n % 4, :], ALU.add))
            stand(dve, 2)

            def layer_norm(dst, tmp, r, n):
                for hf in range(2):
                    ins = v.bn_stats(stats[:, 0, hf, :], tmp[:, hf * HALF:(hf + 1) * HALF])
                    step(ins)
                step(v.bn_aggr(mv[:, 0, :], stats[:, 0, :, :].rearrange("p a b -> p (a b)")))
                dve.sem_inc(var_ready, 1)
                dve.wait_ge(sd_ready, n + 1)
                step(v.reciprocal(sd[:, 1:2], sd[:, 0:1]))
                step(v.tensor_scalar(dst, tmp, mv[:, 0, 0:1], sd[:, 1:2], ALU.subtract, ALU.mult))
                step(v.tensor_tensor(dst, dst, rows[:, r, :], ALU.mult))
                return v.tensor_tensor(dst, dst, rows[:, r + 1, :], ALU.add)

            dve.wait_ge(rows_in, 96)
            tmp = SR[:, 2, :]
            for j in range(NT):
                dve.wait_ge(y_ready, j + 1)
                v.tensor_tensor(tmp, psS[j % 2][:], rows[:, 0, :], ALU.mult).then_inc(y_taken, 1)
                dve.wait_ge(y_taken, j + 1)
                dve.wait_ge(xr_in[j % 2], 16 * (j // 2 + 1))
                step(v.scalar_tensor_tensor(tmp, SR[:, j % 2, :], ALPHA, tmp, ALU.mult, ALU.add))
                layer_norm(x1[:, j, :], tmp, 1, j).then_inc(x1_ready, 1)
            stand(dve, 3)

            dve.wait_ge(logit_ready, 1)
            dve.wait_ge(router_in, 32)
            b3 = lambda ap: ap.unsqueeze(2).broadcast_to([P, NT, NE])
            R = [route[:, i] for i in range(11)]
            c1 = small[:, 0:8]
            step(v.tensor_copy(R[0], psT[:, 0:P].rearrange("p (t e) -> p t e", t=NT)))
            step(v.tensor_reduce(c1, R[0], AX.X, ALU.max))
            step(v.tensor_tensor(R[0], R[0], b3(c1), ALU.subtract))
            dve.sem_inc(logit_max, 1)
            dve.wait_ge(logit_exp, 1)
            step(v.tensor_reduce(c1, R[0], AX.X, ALU.add))
            step(v.reciprocal(c1, c1))
            step(v.tensor_tensor(R[0], R[0], b3(c1), ALU.mult))
            step(v.tensor_tensor(R[1], R[0], PT[:, 0, P:P + NE].unsqueeze(1).broadcast_to([P, NT, NE]), ALU.add))
            grp = R[1].rearrange("p t (g m) -> p t g m", g=4)
            gs, ps_ = R[2][:, :, 0:4], R[2][:, :, 4:8]
            first = True
            for a in range(4):
                for b in range(a + 1, 4):
                    step(v.tensor_tensor(gs if first else ps_, grp[:, :, :, a], grp[:, :, :, b], ALU.add))
                    if not first:
                        step(v.tensor_tensor(gs, gs, ps_, ALU.max))
                    first = False

            def first_best(mask, vals, n, tmp_):
                iot = iota[:, 0:n].unsqueeze(1).broadcast_to([P, NT, n])
                spread = c1.unsqueeze(2).broadcast_to([P, NT, n])
                step(v.tensor_reduce(c1, vals, AX.X, ALU.max))
                step(v.tensor_tensor(tmp_, vals, spread, ALU.is_equal))
                step(v.tensor_tensor(tmp_, tmp_, iot, ALU.mult))
                step(v.tensor_reduce(c1, tmp_, AX.X, ALU.min))
                step(v.tensor_tensor(mask, iot, spread, ALU.is_equal))

            first_best(R[3][:, :, 0:4], gs, 4, R[4][:, :, 0:4])
            step(v.tensor_scalar(R[3][:, :, 4:8], R[3][:, :, 0:4], 0.0, MASKED, ALU.is_equal, ALU.mult))
            for m in range(4):
                step(v.tensor_tensor(R[5].rearrange("p t (g m) -> p t g m", g=4)[:, :, :, m],
                                     grp[:, :, :, m], R[3][:, :, 4:8], ALU.add))
            first_best(R[6], R[5], NE, R[4])
            step(v.tensor_scalar(R[7], R[6], 2.0 * MASKED, None, ALU.mult))
            step(v.tensor_tensor(R[5], R[5], R[7], ALU.add))
            first_best(R[8], R[5], NE, R[4])
            step(v.tensor_tensor(R[6], R[6], R[8], ALU.add))
            step(v.tensor_tensor(R[6], R[6], R[0], ALU.mult))
            step(v.tensor_reduce(c1, R[6], AX.X, ALU.add))
            step(v.reciprocal(c1, c1))
            v.tensor_tensor(R[9], R[6], b3(c1), ALU.mult).then_inc(route_ready, 1)
            dve.wait_ge(route_ready, 1)

            m = 0

            def hidden(n):
                e, hf, f = n // 4, n // 2 % 2, n % 2
                dve.wait_ge(gsig_ready, n + 1)
                dve.wait_ge(gu_ready, n + 1)
                if e >= 1:
                    dve.wait_ge(h_used, 2 * (e - 1) + hf + 1)
                step(v.tensor_tensor(SIG[:, n % 2, :], psS[n % 2][:, 0:HALF], SIG[:, n % 2, :], ALU.mult))
                v.tensor_tensor(HSLOT[:, hf, f, :], psS[n % 2][:, HALF:S], SIG[:, n % 2, :], ALU.mult).then_inc(gu_taken, 1)
                dve.wait_ge(gu_taken, n + 1)
                dve.sem_inc(h_ready, 1)

            for e in range(NE):
                for n in range(4 * e, 4 * e + 4):
                    hidden(n)
                for j in range(NT):
                    dve.wait_ge(down_ready, m + 1)
                    for c in range(2):
                        y = yacc[:, j, c * HALF:(c + 1) * HALF]
                        if e == 0:
                            ins = v.tensor_scalar(y, pair[m % 2][c], R[9][:, j, e:e + 1], None, ALU.mult)
                        else:
                            ins = v.scalar_tensor_tensor(y, pair[m % 2][c], R[9][:, j, e:e + 1], y, ALU.mult, ALU.add)
                    ins.then_inc(down_taken, 1)
                    m += 1
            dve.wait_ge(down_taken, m)
            for j in range(NT):
                step(v.tensor_tensor(yacc[:, j, :], yacc[:, j, :], rows[:, 3, :], ALU.mult))
                step(v.scalar_tensor_tensor(tmp, x1[:, j, :], ALPHA, yacc[:, j, :], ALU.mult, ALU.add))
                layer_norm(yacc[:, j, :], tmp, 4, NT + j).then_inc(fin_ready, 1)


_INS = ['x', 'c', 'rel_table', 'w_router', 'b_router', 'w_ada', 'b_ada', 'w_in', 'a_lambda_q', 'a_lambda_k',
        'a_subln_g', 'b_sinks', 'w_branch', 'w_out', 'ln1_g', 'ln1_b', 'w_exp_gate', 'w_exp_up', 'w_exp_down',
        'ln2_g', 'ln2_b']


def kernel(**inputs):
    import concourse.bacc as bacc
    from concourse.bass_utils import run_bass_kernel_spmd

    nc = bacc.Bacc("TRN2", target_bir_lowering=False, num_devices=1)
    arrays = {name: np.ascontiguousarray(inputs[name]) for name in _INS}
    arrays.update(table_constants())
    t = {name: nc.dram_tensor(f"in_{name}", a.shape, mybir.dt.from_np(a.dtype), kind="ExternalInput").ap()
         for name, a in arrays.items()}
    out = nc.dram_tensor("out", (1, S, D), F32, kind="ExternalOutput").ap()
    scratch = {"gtab": nc.dram_tensor("gtab", (4, TAB_W), F32, kind="Internal").ap(),
               "shifted": nc.dram_tensor("shifted", (4, P * (TAB_W + P + 1)), F32, kind="Internal").ap(),
               "gates": nc.dram_tensor("gate_rows", (2, D), F32, kind="Internal").ap()}
    build(nc, t, out, scratch)
    r = run_bass_kernel_spmd(nc, [{f"in_{n}": a for n, a in arrays.items()}], core_ids=[0])
    return r.results[0]["out"]
```

```python
import math
from contextlib import ExitStack
from itertools import islice

import numpy as np
import concourse.bass as bass
from concourse import mybir

F32 = mybir.dt.float32
ALU = mybir.AluOpType
ACT = mybir.ActivationFunctionType
AX = mybir.AxisListType

P = 128
D = 1024
S = 1024
KT = D // P
NT = S // P
HALF = 512
HD = 64
NE = 16
FF = 256
NB = 2 * S // P + NE - 1
ALPHA = 2.0 ** 0.25
EPS = 1e-5
LAM0 = 0.8 - 0.6 * math.exp(0.0)
TOPK = 256
MASKED = -1.0e30
TAKEN = -3.0e38
LOWEST = -3.4e38

SPLITS = (("a_q", 256), ("a_k", 256), ("a_v", 256), ("b_q", 256), ("b_k", 128), ("b_v", 128),
          ("c_q", 768), ("c_k", 768), ("c_v", 768), ("d_q", 256), ("d_k", 64), ("d_v", 64),
          ("i_q", 256), ("i_k", 32), ("i_w", 8), ("gate", 4096))
COL = {}
for _n, _w in SPLITS:
    COL[_n] = sum(w for _, w in SPLITS[:len(COL)])
IN_WIDTH = sum(w for _, w in SPLITS)

TABLES = (("A", 0, 1024, 1023, 1, 1023), ("B", 4, 256, 255, 1, 127), ("C0", 8, 256, 255, 1, 128),
          ("C1", 12, 256, 255, 4, 128), ("C2", 16, 128, 127, 8, 127), ("D", 20, 1024, 1023, 1, 1023))
TAB_OFF, _o = {}, 0
for _t in TABLES:
    TAB_OFF[_t[0]] = _o
    _o += _t[2] + P
TAB_W = _o


def table_constants():
    onehot = np.zeros((32, TAB_W), np.float32)
    mask = np.zeros((4, TAB_W), np.float32)
    for name, _, width, d0, dil, most in TABLES:
        for x in range(width + P):
            steps = d0 - x
            if 0 <= steps <= most and not (name == "C2" and steps % 2):
                n = steps * dil
                b = n if n < 16 else min(31, 16 + int(math.log(n / 16) / math.log(2048 / 16) * 16))
                onehot[b, TAB_OFF[name] + x] = 1.0
            else:
                mask[:, TAB_OFF[name] + x] = MASKED
    sel = np.zeros((4, 2, P), np.float32)
    for h in range(4):
        sel[h, h // 2, (h % 2) * 64:(h % 2) * 64 + 64] = 1.0
    blockones = np.zeros((P, P), np.float32)
    blockones[:64, :64] = blockones[64:, 64:] = 1.0 / 64
    tri = np.where(np.arange(P)[None, :] <= np.arange(P)[:, None], 0.0, MASKED).astype(np.float32)
    iota = np.broadcast_to(np.arange(16, dtype=np.float32) - 99.0, (P, 16)).copy()
    p = np.arange(P, dtype=np.float32)
    return dict(before=(p[:, None] < p[None, :]).astype(np.float32), ones=np.ones((P, P), np.float32),
                iota_row=np.broadcast_to(p, (P, P)).copy(),
                token_id=(p[:, None] + P * np.arange(NT, dtype=np.float32)[None, :]), onehot=onehot, tabmask=mask, headsel=sel.reshape(4, 256), blockones=blockones,
                ident=np.eye(P, dtype=np.float32), causal=tri, iota=iota)


N_TAB = sum(-(-(x[2] + P) // HALF) for x in TABLES)


def build(nc, t, out, scratch):
    ctx = ExitStack()
    with ctx:
        def sb(name, shape, dt=F32):
            return ctx.enter_context(nc.sbuf_tensor(name, shape, dt))

        def sem(name):
            return ctx.enter_context(nc.semaphore(name))

        KB = 256
        uT_ = sb("uT", [P, KT, S])
        oT_ = sb("oT", [P, 4, 2, S])
        ring_ = sb("ring", [P, 2, KT * HALF])
        qkv_ = sb("qkv", [P, 32 * KB])
        strips_ = sb("strips", [P, 30 * KB])
        SR = sb("SR", [P, 4, S])
        PT = sb("PT", [P, 2, S])
        isel = sb("isel", [P, 4224])
        ident = sb("ident_sb", [P, P])
        causal = sb("causal_sb", [P, P])
        bones = sb("bones_sb", [P, P])
        hsel = sb("hsel_sb", [4, 2, P])
        iota = sb("iota_sb", [P, 16])
        badaT = sb("badaT", [P, 48])
        modT = sb("modT", [P, 48])
        cT = sb("cT", [P, 2, KT])
        lamq = sb("lamq", [32, 2, 2])
        lam = sb("lam", [P, 4])
        subg = sb("subg", [P, 1])
        ones_col = sb("ones_col", [P, 1])
        sink = sb("sink", [P, 4])
        epsc = sb("epsc", [P, 1])
        lamw = sb("lamw", [P, 4])
        iw = sb("iw", [P, NT, 8])
        mx = sb("mx", [P, 224 + 8])
        negm = sb("negm", [P, 224 + 8])
        den = sb("den", [P, 224 + 8])
        rec = sb("rec", [P, 224 + 8])
        top8 = sb("top8", [P, 8])
        stats = sb("stats", [P, 2, 2, 6])
        mv = sb("mv", [P, 2, 2])
        sd = sb("sd", [P, 2])
        slot_idx = sb("slot_idx", [P, NB], mybir.dt.int32)
        slot_now = sb("slot_now", [P, 2], mybir.dt.int32)
        block_expert = sb("block_expert", [P, NB], mybir.dt.int32)
        block_new = sb("block_new", [P, NB], mybir.dt.int32)
        block_slot = sb("block_slot", [P, NB], mybir.dt.int32)
        dest_idx = sb("dest_idx", [P, 2 * NT], mybir.dt.int32)

        uT, oT = uT_, oT_
        ring = [ring_[:, i, :].rearrange("p (k n) -> p k n", k=KT) for i in range(2)]
        qT = qkv_[:, 0:2 * S].rearrange("p (a s) -> p a s", a=2)
        kT = qkv_[:, 2 * S:4 * S].rearrange("p (a s) -> p a s", a=2)
        V = qkv_[:, 4 * S:6 * S].rearrange("p (t n) -> p t n", t=NT)
        ikT = qkv_[:, 4 * S:5 * S]
        bm = qkv_[:, 6 * S:8 * S].rearrange("p (r s) -> p r s", r=2)
        iwT = qkv_[0:8, 6 * S:7 * S]
        xn = qkv_[:, 0:8 * S].rearrange("p (t n) -> p t n", t=NT)
        mrg = xn
        yacc = xn
        x1 = oT_[:, :, :, :].rearrange("p a b s -> p (a b) s")
        vT = uT_
        stripAD = strips_[:, 0:4 * S].rearrange("p (h s) -> p h s", h=4)
        stripB = strips_[:, 4 * S:5 * S].rearrange("p (h s) -> p h s", h=4)
        stripC = [strips_[:, 5 * S:6 * S].rearrange("p (h s) -> p h s", h=4),
                  strips_[:, 6 * S:7 * S].rearrange("p (h s) -> p h s", h=4),
                  strips_[:, 7 * S:7 * S + 512].rearrange("p (h s) -> p h s", h=4)]
        rows = strips_[:, 0:6 * S].rearrange("p (r s) -> p r s", r=6)

        pb = [ctx.enter_context(nc.psum_tensor(f"pb{i}", [P, HALF], F32)) for i in range(2)]
        psS = [ctx.enter_context(nc.psum_tensor(f"psS{i}", [P, S], F32)) for i in range(2)]
        psT = ctx.enter_context(nc.psum_tensor("psT", [P, S], F32))

        XG, XT, YB = (qkv_[:, 2 * i * S:2 * (i + 1) * S].rearrange("p (r s) -> p r s", r=2) for i in range(3))
        SIG, HN, HT = (qkv_[:, 6 * S + i * HALF:6 * S + (i + 1) * HALF].rearrange("p (r s) -> p r s", r=2) for i in range(3))
        before, ones, iota_row = (SR[:, 3, i * P:(i + 1) * P] for i in range(3))
        token_id = SR[:, 3, 3 * P:3 * P + NT]
        onehots = SR[:, 0:2, :].rearrange("p r s -> p (r s)")
        block_hot = SR[:, 2, 0:2 * NT * NB].rearrange("p (c b) -> p c b", b=NB)
        route = strips_[:, 6 * S:6 * S + 11 * P].rearrange("p (r t e) -> p r t e", r=11, t=NT)
        small = strips_[:, 6 * S + 11 * P:6 * S + 12 * P]
        pair = [(psT[:, 0:HALF], psT[:, HALF:S]), (pb[0][:], pb[1][:])]

        const_in = sem("const_in")
        x_in = sem("x_in")
        piece_step, piece_summed = sem("piece_step"), sem("piece_summed")
        vecs_in, vecs_T, c_ready = sem("vecs_in"), sem("vecs_T"), sem("c_ready")
        w_landed = [sem("w_landed0"), sem("w_landed1")]
        ada_uT_in = [sem("ada_uT_in0"), sem("ada_uT_in1")]
        ada_used = sem("ada_used")
        ada_summed = sem("ada_summed")
        w_used = sem("w_used")
        cond_ready = sem("cond_ready")
        lam_ops = sem("lam_ops")
        lam_sum = sem("lam_sum")
        lam_exp = sem("lam_exp")
        mod_sum = sem("mod_sum")
        mod_ready = sem("mod_ready")
        out_ready, out_taken = sem("out_ready"), sem("out_taken")
        tab_ready, tab_taken, tab_out = sem("tab_ready"), sem("tab_taken"), sem("tab_out")
        stripD_in = sem("stripD_in")
        ada_in = [sem("ada_in0"), sem("ada_in1")]
        shifted_out = sem("shifted_out")
        strip_in, stripAD_in = sem("strip_in"), sem("stripAD_in")
        scores_ready, scores_taken = sem("scores_ready"), sem("scores_taken")
        relu_taken = sem("relu_taken")
        relu_used = sem("relu_used")
        biased = sem("biased")
        probs_ready = sem("probs_ready")
        diff_ready = sem("diff_ready")
        pT_ready, pT_copied = sem("pT_ready"), sem("pT_copied")
        sel_ready, bm_ready = sem("sel_ready"), sem("bm_ready")
        a_biased = sem("a_biased")
        sink_exp = sem("sink_exp")
        cols_ready = sem("cols_ready")
        norm_ready, norm_taken = sem("norm_ready"), sem("norm_taken")
        shift_ready, shift_exp = sem("shift_ready"), sem("shift_exp")
        sq_ready, ms_ready, rms_ready = sem("sq_ready"), sem("ms_ready"), sem("rms_ready")
        sum_done = sem("sum_done")
        gate_ready, sig_ready, proj_ready, proj_taken = (sem(n) for n in ("gate_ready", "sig_ready", "proj_ready", "proj_taken"))
        wb_in, wb_used = [sem("wb_in0"), sem("wb_in1")], sem("wb_used")
        gcols_out, rows_in = sem("gcols_out"), sem("rows_in")
        wo_in, router_in = sem("wo_in"), sem("router_in")
        xr_in = [sem("xr_in0"), sem("xr_in1")]
        y_ready, y_taken, x1_ready = sem("y_ready"), sem("y_taken"), sem("x1_ready")
        var_ready, sd_ready = sem("var_ready"), sem("sd_ready")
        logit_ready, logit_max, logit_exp, route_ready = (sem(n) for n in ("logit_ready", "logit_max", "logit_exp", "route_ready"))
        moe_const_in = sem("moe_const_in")
        counts_in, ranks = sem("counts_in"), sem("ranks")
        hots_ready, slot_sum = sem("hots_ready"), sem("slot_sum")
        slots_ready = sem("slots_ready")
        e_in = [sem("e_in0"), sem("e_in1")]
        xg_in = [sem("xg_in0"), sem("xg_in1")]
        x1_out = sem("x1_out")
        xt_ready, xt_taken = sem("xt_ready"), sem("xt_taken")
        gu_ready, gsig_ready, h_ready = sem("gu_ready"), sem("gsig_ready"), sem("h_ready")
        ht_ready, ht_taken = sem("ht_ready"), sem("ht_taken")
        down_ready, yb_ready = sem("down_ready"), sem("yb_ready")
        yb_out = [sem("yb_out0"), sem("yb_out1")]
        pick_in = [sem(f"pick_in{i}") for i in range(4)]
        y_added = sem("y_added")
        fin_ready = sem("fin_ready")
        out_done = [sem("out_done0"), sem("out_done1")]
        silu_ready, pool_step, gather_go = sem("silu_ready"), sem("pool_step"), sem("gather_go")
        phase = sem("phase")
        dve_step, act_step = sem("dve_step"), sem("act_step")

        w = t["w_in"][0]
        def ada(c):
            return [(t["w_ada"][0], HALF * c, HALF, 0)]

        chunks = [ada(0), ada(1)]
        chunks.append([(w, COL["i_q"], 256, 0)] + [(w, COL["i_k"], 32, 256 + 32 * r) for r in range(4)]
                      + [(w, COL["i_w"], 8, 384)])
        PROJ = {}
        WITH_ADA = ("C0", "C1", "C2", "A")

        def branch_chunks(name, q, k, v):
            PROJ[name] = len(chunks)
            chunks.append([(w, q, 256, 0)] + k)
            chunks.append([v])

        bk, dk = COL["b_k"], COL["d_k"]
        branch_chunks("B", COL["b_q"], [(w, bk, 64, 256), (w, bk, 64, 320), (w, bk + 64, 64, 384),
                                        (w, bk + 64, 64, 448)], (w, COL["b_v"], 128, 0))
        for g in range(3):
            branch_chunks(f"C{g}", COL["c_q"] + 256 * g, [(w, COL["c_k"] + 256 * g, 256, 256)],
                          (w, COL["c_v"] + 256 * g, 256, 0))
        branch_chunks("A", COL["a_q"], [(w, COL["a_k"], 256, 256)], (w, COL["a_v"], 256, 0))
        branch_chunks("D", COL["d_q"], [(w, dk, 64, 256), (w, dk, 64, 320)], (w, COL["d_v"], 64, 0))
        ORDER = ("B", "C0", "C1", "C2", "A", "D")
        VCOLS = {"A": 256, "B": 128, "C0": 256, "C1": 256, "C2": 256, "D": 64}
        KCOLS = {"A": 2, "B": 2, "C0": 2, "C1": 2, "C2": 2, "D": 1}
        BASE = {"B": 0, "C0": 32, "C1": 64, "C2": 96, "A": 128, "D": 192}
        N_IDX = 8 * (NT - 2)

        def units(name):
            for j in range(NT):
                for h in range(4):
                    if name in "AD":
                        yield h, j, 0, j + 1
                    elif name == "C1":
                        yield h, j, j - j % 2, j + 1
                    elif name == "C2":
                        yield h, j, j, j + 1
                    else:
                        yield h, j, max(0, j - 1), j + 1

        def pt_banks(k0, k1):
            return -(-(k1 - k0) // 4)

        BANKS, _n = {}, 0
        for _name in ORDER:
            for _i, (_, _, _k0, _k1) in enumerate(units(_name)):
                _n += pt_banks(_k0, _k1)
                for _m in range(2 if _name == "A" else 1):
                    BANKS[BASE[_name] + (2 * _i + _m if _name == "A" else _i)] = _n

        def bias_strip(name, h, n):
            if name in "AD":
                return stripAD[:, h, S - n:S]
            if name == "B":
                return stripB[:, h, 256 - n:256]
            g = int(name[1])
            return stripC[g][:, h, 256 - n:256] if g < 2 else stripC[g][:, h, 0:P]

        def idx_tile(j):
            at = sum((i + 1) * P for i in range(2, j))
            return isel[:, at:at + (j + 1) * P]

        def tile_tokens(ap, name, j):
            if name == "C1":
                return ap.rearrange("p (a r) -> p r a", r=4)[:, j // 2, (j % 2) * P:(j % 2) * P + P]
            if name == "C2":
                return ap.rearrange("p (a r) -> p r a", r=8)[:, j, :]
            return ap[:, j * P:(j + 1) * P]

        def half_in_order(dst, src, name, hf):
            if name in ("C1", "C2"):
                r = 4 if name == "C1" else 8
                n = HALF // r
                return (dst.rearrange("p (r a) -> p r a", r=r)[:, :, hf * n:(hf + 1) * n],
                        src.rearrange("p (a r) -> p r a", r=r))
            return dst[:, hf * HALF:(hf + 1) * HALF], src

        def rows_to_tokens(dst, src, name, hf):
            if name in ("C1", "C2"):
                r = 4 if name == "C1" else 8
                return (dst.rearrange("p (a r) -> p r a", r=r)[:, hf * r // 2:(hf + 1) * r // 2, :],
                        src.rearrange("p (r a) -> p r a", r=r // 2))
            return dst[:, hf * HALF:(hf + 1) * HALF], src

        RAW = {"A": 0, "B": 1, "C0": 2, "C1": 0, "C2": 3, "D": 3}

        def stand(eng, n):
            eng.drain().then_inc(phase, 1)
            eng.wait_ge(phase, 5 * n)

        picks = qkv_[:, 0:4 * S].rearrange("p (r s) -> p r s", r=4)
        ytmp = SR[:, 0:2, :]
        yout = qkv_[:, 4 * S:6 * S].rearrange("p (r s) -> p r s", r=2)
        picked = strips_[:, 6 * S + 7 * P:6 * S + 8 * P]
        earlier = PT[:, 1, 0:(NT + 1) * NE]
        topw, rank, blk, moved = (PT[:, 1, 2 * P + 2 * NT * i:2 * P + 2 * NT * (i + 1)] for i in range(4))
        blk_sum = PT[:, 1, 3 * P:3 * P + NB]
        blk_new = PT[:, 1, 3 * P + 32:3 * P + 32 + NB]
        blk_tmp = PT[:, 1, 3 * P + 64:3 * P + 64 + NB]
        blk_cmp = PT[:, 1, HALF:HALF + NB * NE].rearrange("p (b e) -> p b e", e=NE)

        ada_uT = [uT_[:, 4 * i:4 * i + 4, :].rearrange("p a (b n) -> p (a b) n", n=HALF) for i in range(2)]
        ada_acc = oT_[:, 0, :, :].rearrange("p a s -> p (a s)")
        ada_w = [PT[:, i, :].rearrange("p (k n) -> p k n", n=P) for i in range(2)]

        onehot = SR[0:32, :, :].rearrange("p r s -> p (r s)")[:, 0:TAB_W]
        relt = PT[0:32, 0, 0:24]
        bcols = SR[:, 0:2, :].rearrange("p r (c n) -> p (r c n)", n=64)
        fac = [SR[0:4, g, :] for g in range(3)]
        fmax = SR[0:4, 3, :]
        fden = [PT[0:4, 0, :], PT[0:4, 1, :], bm[0:4, 0, :]]
        N_CONST = 12
        vecs = PT[0:56, 1, HALF:HALF + P]

        down_all = isel[:, 0:4 * S].rearrange("p (r n) -> p r n", r=2)

        def refill(b):
            return not isinstance(b, int) or b >= 2

        def blocks(eng, step_of):
            step_of(0, 0, 0)
            step_of(1, 1, 1)
            step_of(2, 0, 2)
            step_of(3, 1, 3)
            with eng.Fori(2, NB // 2) as i:
                step_of(i * 2, 0, 2)
                step_of(i * 2 + 1, 1, 3)
            step_of(NB - 1, 0, NB - 1)

        OUTS = {"A": 16 + 6 + 3 + 32 + 5 * (8 + NT + 32)}
        ADA_AT = {name: 16 + 6 + 3 + 8 * i + (i + 1) * (8 + NT + 32) for i, name in enumerate(WITH_ADA)}

        def strip(eng, dst, name, h, s):
            width = {x[0]: x[2] for x in TABLES}[name]
            c0 = TAB_OFF[name] + P - 1
            src = scratch["shifted"][h, 0:P * (TAB_W + P)].rearrange("(p n) -> p n", p=P)[:, c0:c0 + width]
            eng.dma_start(dst, src).then_inc(s, 16)

        block = ctx.enter_context(nc.Block())

        @block.sync
        def _(sp):
            def chunk(n):
                if 2 <= n < 4:
                    sp.wait_ge(ada_used, n - 1)
                elif n >= 4:
                    sp.wait_ge(w_used, n - 3)
                for src, c0, wd, at in chunks[n]:
                    sp.dma_start(ring[n % 2][:, :, at:at + wd],
                                 src[:, c0:c0 + wd].rearrange("(k p) n -> p k n", p=P)).then_inc(w_landed[n % 2], 16)

            sp.dma_start(vecs[0:48, :], t["b_ada"][0].rearrange("(k p) -> k p", p=P)).then_inc(vecs_in, 16)
            sp.dma_start(vecs[48:56, :], t["c"][0].rearrange("(k p) -> k p", p=P)).then_inc(vecs_in, 16)
            sp.dma_start(ident[:], t["ident"]).then_inc(vecs_in, 16)
            chunk(0)
            chunk(1)
            for i in range(2):
                sp.dma_start(ada_uT[i], ada(2 + i)[0][0][:, (2 + i) * HALF:(3 + i) * HALF]
                             .rearrange("(k p) n -> p k n", p=P)).then_inc(ada_uT_in[i], 16)
            chunk(2)
            chunk(3)
            sp.wait_ge(tab_taken, N_TAB)
            sp.dma_start(scratch["gtab"], isel[0:4, 0:TAB_W]).then_inc(tab_out, 16)
            sp.wait_ge(tab_out, 16)
            for h in range(4):
                sp.dma_start(scratch["shifted"][h, 0:P * (TAB_W + P + 1)].rearrange("(p n) -> p n", p=P)[:, 0:TAB_W],
                             scratch["gtab"][h:h + 1, :].broadcast_to([P, TAB_W])).then_inc(shifted_out, 16)
            sp.wait_ge(shifted_out, 64)

            for h in range(4):
                strip(sp, stripB[:, h, :], "B", h, strip_in)
                for g in range(3):
                    strip(sp, stripC[g][:, h, :], f"C{g}", h, strip_in)
                strip(sp, stripAD[:, h, :], "A", h, stripAD_in)
            for n in range(4, PROJ["C0"] + 2):
                chunk(n)
            for i, name in enumerate(WITH_ADA):
                for m in range(8):
                    sp.wait_ge(out_ready, ADA_AT[name] + max(0, 2 * m - 2))
                    if name == "A" and m == 0:
                        sp.wait_ge(norm_taken, 4 + 24)
                    c0 = 2 * D + (8 * i + m) * P
                    sp.dma_start(ada_w[m % 2], t["w_ada"][0][:, c0:c0 + P].rearrange("(k p) n -> p k n", p=P)
                                 ).then_inc(ada_in[m % 2], 16)
                for n in range(PROJ[name] + 2, PROJ[name] + 4):
                    chunk(n)
            stand(sp, 1)
            sp.wait_ge(gcols_out, 32)
            for r, src in enumerate((scratch["gates"][0:1, :], t["ln1_g"], t["ln1_b"],
                                     scratch["gates"][1:2, :], t["ln2_g"], t["ln2_b"])):
                sp.dma_start(rows[:, r, :], src.broadcast_to([P, D])).then_inc(rows_in, 16)
            for d in range(KT):
                if d >= 2:
                    sp.wait_ge(wb_used, d - 1)
                for b in range(4):
                    c0 = COL["gate"] + b * D + d * P
                    sp.dma_start(ring[d % 2][:, :, b * P:(b + 1) * P],
                                 w[:, c0:c0 + P].rearrange("(k p) n -> p k n", p=P)).then_inc(wb_in[d % 2], 16)
                    sp.dma_start(PT[:, d % 2, b * 256:(b + 1) * 256].rearrange("p (k n) -> p k n", k=2),
                                 t["w_branch"][0, b, :, d * P:(d + 1) * P].rearrange("(k p) n -> p k n", p=P)
                                 ).then_inc(wb_in[d % 2], 16)
            stand(sp, 2)
            for dst, name in ((before, "before"), (ones, "ones"), (iota_row, "iota_row"), (token_id, "token_id")):
                sp.dma_start(dst, t[name]).then_inc(moe_const_in, 16)
            for hf in range(2):
                sp.dma_start(ring[hf], t["w_out"][0][:, hf * HALF:(hf + 1) * HALF]
                             .rearrange("(k p) n -> p k n", p=P)).then_inc(wo_in, 16)
            for j in range(NT):
                if j >= 2:
                    sp.wait_ge(x1_ready, j - 1)
                    sp.dma_start(scratch["x1"][(j - 2) * P:(j - 1) * P, :], x1[:, j - 2, :]).then_inc(x1_out, 16)
                sp.dma_start(SR[:, j % 2, :], t["x"][0, j * P:(j + 1) * P, :]).then_inc(xr_in[j % 2], 16)
            for j in (NT - 2, NT - 1):
                sp.wait_ge(x1_ready, j + 1)
                sp.dma_start(scratch["x1"][j * P:(j + 1) * P, :], x1[:, j, :]).then_inc(x1_out, 16)
            stand(sp, 3)
            sp.dma_start(PT[:, 0, 0:P].rearrange("p (k e) -> p k e", k=KT),
                         t["w_router"].rearrange("(k p) e -> p k e", p=P)).then_inc(router_in, 16)
            sp.dma_start(PT[:, 0, P:P + NE], t["b_router"].rearrange("(a n) -> a n", a=1).broadcast_to([P, NE])
                         ).then_inc(router_in, 16)
            sp.wait_ge(slots_ready, 1)

            def load_weights(b, r, least):
                at = bass.ds(b, 1)
                new = 1 if isinstance(b, int) and b == 0 else sp.value_load(block_new[0:1, at], min_val=0, max_val=1)
                e = sp.value_load(block_expert[0:1, at], min_val=0, max_val=NE - 1)
                slot = sp.value_load(block_slot[0:1, at], min_val=0, max_val=1)
                if refill(b):
                    sp.wait_ge(gu_ready, b - 1)
                for c0, name in ((0, "w_exp_gate"), (FF, "w_exp_up")):
                    sp.dma_start(ring_[:, bass.ds(slot, 1), :].rearrange("p a (k n) -> p (a k) n", k=KT)[:, :, c0:c0 + FF],
                                 t[name][0, bass.ds(e, 1), :, :].rearrange("e (k p) n -> p (e k) n", p=P),
                                 cond=new).then_inc(e_in[r], 16)
                if refill(b):
                    sp.wait_ge(down_ready, b - 1)
                sp.dma_start(down_all[:, bass.ds(slot, 1), :].rearrange("p a (k n) -> p (a k) n", k=2),
                             t["w_exp_down"][0, bass.ds(e, 1), :, :].rearrange("e (k p) n -> p (e k) n", p=P),
                             cond=new).then_inc(e_in[r], 16)

            blocks(sp, load_weights)
            for j in range(NT):
                sp.wait_ge(fin_ready, j + 1)
                sp.dma_start(out[0, j * P:(j + 1) * P, :], yout[:, j % 2, :]).then_inc(out_done[j % 2], 16)
            for o in out_done:
                sp.wait_ge(o, 16 * NT // 2)

        @block.tensor
        def _(pe):
            mm = nc.tensor.matmul
            n_out = 0
            n_norm = 0
            s = 0
            n_pt = 0
            n_diff = 0
            n_ada = 0
            last_pt = {0: 0, 1: 0}

            def landed(n):
                pe.wait_ge(w_landed[n % 2], 16 * sum(len(chunks[i]) for i in range(n % 2, n + 1, 2)))

            def bank():
                if n_out >= 2:
                    pe.wait_ge(out_taken, n_out - 1)
                return pb[n_out % 2]

            def norm_bank():
                if n_norm >= 2:
                    pe.wait_ge(norm_taken, n_norm - 1)
                return psT[:, (n_norm % 2) * HALF:(n_norm % 2 + 1) * HALF]

            pe.wait_ge(vecs_in, 48)
            nc.tensor.transpose(psT[:, 0:56], vecs, ident[0:56, 0:56]).then_inc(vecs_T, 1)
            for m in range(2 * KT):
                if m % 4 == 0:
                    pe.wait_ge(ada_summed, m // 4 + 1)
                last = mm(psT[:, m:m + 1], ada_acc[:, m * P:(m + 1) * P], ones_col[:], start=True, stop=True)
            last.then_inc(mod_sum, 1)
            pe.wait_ge(x_in, 16 * NT)
            for k in range(KT):
                for hf in range(2):
                    o = bank()
                    for q in range(4):
                        last = nc.tensor.transpose(o[:, q * P:(q + 1) * P], xn[:, 4 * hf + q, k * P:(k + 1) * P], ident[:])
                    last.then_inc(out_ready, 1)
                    n_out += 1
            pe.wait_ge(out_taken, n_out)

            def project_T(n, cols, with_ada=False, between=()):
                nonlocal n_out, n_ada
                for c in range(cols):
                    for hf in range(2):
                        o = bank()
                        for k in range(KT):
                            last = mm(o[:], ring[n % 2][:, k, c * P:(c + 1) * P], uT[:, k, hf * HALF:(hf + 1) * HALF],
                                      start=(k == 0), stop=(k == KT - 1))
                        last.then_inc(out_ready, 1)
                        n_out += 1
                        for _ in islice(between, 2):
                            pass
                        if with_ada:
                            i = n_ada % 2
                            pe.wait_ge(piece_summed, n_ada + 1)
                            mm(bank()[:, 0:1], ada_w[i][:, 0, :], ones_col[:], start=True, stop=True).then_inc(out_ready, 1)
                            n_out += 1
                            n_ada += 1

            def project_V(n, name, cols, at=0):
                nonlocal n_out
                for j in range(NT):
                    o = bank()
                    for k in range(KT):
                        last = mm(o[:, 0:cols], tile_tokens(uT[:, k, :], name, j), ring[n % 2][:, k, at:at + cols],
                                  start=(k == 0), stop=(k == KT - 1))
                    last.then_inc(out_ready, 1)
                    n_out += 1

            def tables():
                n = 0
                for name, h0, width, *_ in TABLES:
                    for c in range(0, width + P, HALF):
                        wd = min(HALF, width + P - c)
                        if n >= 2:
                            pe.wait_ge(tab_taken, n - 1)
                        at = TAB_OFF[name] + c
                        mm(psS[n % 2][0:4, 0:wd], PT[0:32, 0, h0:h0 + 4], onehot[:, at:at + wd],
                           start=True, stop=True).then_inc(tab_ready, 1)
                        n += 1
                        yield

            landed(2)
            pe.wait_ge(const_in, 16 * N_CONST)
            pe.wait_ge(lam_ops, 1)
            mm(psT[:, HALF:HALF + 2], PT[0:32, 1, 0:P], PT[0:32, 1, P:P + 2], start=True, stop=True).then_inc(lam_sum, 1)
            tab = tables()
            project_T(2, 3, between=tab)
            for _ in tab:
                pass
            for hf in range(2):
                o = bank()
                for k in range(KT):
                    last = mm(o[0:8, :], ring[0][:, k, 384:392], uT[:, k, hf * HALF:(hf + 1) * HALF],
                              start=(k == 0), stop=(k == KT - 1))
                last.then_inc(out_ready, 1)
                n_out += 1
            pe.drain().then_inc(w_used, 1)
            pe.wait_ge(out_taken, n_out)
            o = bank()
            for j in range(NT):
                last = nc.tensor.transpose(o[:, 8 * j:8 * j + 8], iwT[:, j * P:(j + 1) * P], ident[0:8, 0:8])
            last.then_inc(out_ready, 1)
            n_out += 1
            pe.wait_ge(tab_taken, N_TAB)
            for j in range(2, NT):
                for h in range(8):
                    if s >= 2:
                        pe.wait_ge(relu_taken, s - 1)
                    r = 32 * (h % 4)
                    for c in range(0, (j + 1) * P, HALF):
                        wd = min(HALF, (j + 1) * P - c)
                        last = mm(psS[s % 2][:, c:c + wd], qT[r:r + 32, h // 4, j * P:(j + 1) * P],
                                  ikT[r:r + 32, c:c + wd], start=True, stop=True)
                    last.then_inc(scores_ready, 1)
                    s += 1
            pe.wait_ge(relu_taken, s)

            for name in ORDER:
                n = PROJ[name]
                landed(n)
                project_T(n, 2 + KCOLS[name], name in WITH_ADA)
                pe.drain().then_inc(w_used, 1)
                landed(n + 1)
                project_V(n + 1, name, VCOLS[name])
                pe.drain().then_inc(w_used, 1)
                pe.wait_ge(out_taken, n_out)
                todo = list(units(name))

                def score(i):
                    nonlocal s
                    h, j, k0, k1 = todo[i]
                    for m in range(2 if name == "A" else 1):
                        if s >= N_IDX + 2:
                            pe.wait_ge(scores_taken, s - N_IDX - 1)
                        r, K = ((h % 2) * 64 + 32 * m, 32) if name == "A" else ((h % 2) * 64, 64)
                        keys = kT[:, 0 if name == "D" else h // 2, :]
                        for c in range(k0 * P, k1 * P, HALF):
                            wd = min(HALF, k1 * P - c)
                            last = mm(psS[s % 2][:, c - k0 * P:c - k0 * P + wd],
                                      qT[r:r + K, h // 2, j * P:(j + 1) * P], keys[r:r + K, c:c + wd],
                                      start=True, stop=True)
                        last.then_inc(scores_ready, 1)
                        s += 1

                def transpose_probs(i):
                    nonlocal n_pt, n_diff
                    h, j, k0, k1 = todo[i]
                    if name == "A":
                        n_diff += 1
                        pe.wait_ge(diff_ready, n_diff)
                        slot = (BASE["A"] + 2 * i) % 4
                    else:
                        pe.wait_ge(probs_ready, BASE[name] + i + 1)
                        slot = (BASE[name] + i) % 4
                    for b, c in enumerate(range(k0, k1, 4)):
                        if last_pt[b]:
                            pe.wait_ge(pT_copied, last_pt[b])
                        for q in range(c, min(c + 4, k1)):
                            last = nc.tensor.transpose(psT[:, (q - k0) * P:(q - k0 + 1) * P],
                                                       SR[:, slot, (q - k0) * P:(q - k0 + 1) * P], ident[:])
                        last.then_inc(pT_ready, 1)
                        n_pt += 1
                        last_pt[b] = n_pt

                def weigh_values(i):
                    nonlocal n_out
                    h, j, k0, k1 = todo[i]
                    u = ORDER.index(name) * 32 + i
                    pe.wait_ge(pT_copied, BANKS[BASE[name] + (2 * i if name == "A" else i)])
                    o = bank()
                    vh = {"B": h // 2, "D": 0}.get(name, h)
                    for q in range(k0, k1):
                        last = mm(o[0:64, 0:P], V[:, q, vh * HD:(vh + 1) * HD],
                                  PT[:, u % 2, (q - k0) * P:(q - k0 + 1) * P], start=(q == k0), stop=(q == k1 - 1))
                    last.then_inc(out_ready, 1)
                    n_out += 1

                for i in range(-2, len(todo)):
                    if i + 2 < len(todo):
                        score(i + 2)
                    if i >= 0:
                        weigh_values(i)
                    if 0 <= i + 1 < len(todo):
                        transpose_probs(i + 1)
                pe.wait_ge(pT_copied, n_pt)
                pe.wait_ge(out_taken, n_out)
                if name in ("B", "D"):
                    pe.wait_ge(cols_ready, 1 if name == "B" else 3)
                    for pr in range(2):
                        for hf in range(2):
                            o = norm_bank()
                            for q in range(4):
                                c0 = (4 * (4 * hf + q) + 2 * pr) * 64
                                last = nc.tensor.transpose(o[:, q * P:(q + 1) * P], bcols[:, c0:c0 + P], ident[:])
                            last.then_inc(norm_ready, 1)
                            n_norm += 1
                if name == "C2":
                    for g in range(3):
                        for stat in (mx, den):
                            for hf in range(2):
                                o = norm_bank()
                                for q in range(4):
                                    c0 = BASE[f"C{g}"] + 4 * (4 * hf + q)
                                    last = nc.tensor.transpose(o[0:4, q * P:(q + 1) * P], stat[:, c0:c0 + 4], ident[:])
                                last.then_inc(norm_ready, 1)
                                n_norm += 1
                    pe.wait_ge(cols_ready, 2)
                    for g in range(3):
                        for pr in range(2):
                            for hf in range(2):
                                mm(norm_bank(), hsel[:, pr, :], fac[g][:, hf * HALF:(hf + 1) * HALF],
                                   start=True, stop=True).then_inc(norm_ready, 1)
                                n_norm += 1
                if name == "A":
                    for i in range(4):
                        pe.wait_ge(sq_ready, i + 1)
                        mm(norm_bank(), bones[:], bm[:, i % 2, 0:HALF], start=True, stop=True).then_inc(norm_ready, 1)
                        n_norm += 1
                if n_norm:
                    pe.wait_ge(norm_taken, n_norm)
            stand(pe, 1)

            n = 0
            for d in range(KT):
                pe.wait_ge(wb_in[d % 2], 16 * 8 * (d // 2 + 1))
                for b in range(4):
                    if n >= 2:
                        pe.wait_ge(sig_ready, n - 1)
                    for hf in range(2):
                        for k in range(KT):
                            last = mm(psS[n % 2][:, hf * HALF:(hf + 1) * HALF], ring[d % 2][:, k, b * P:(b + 1) * P],
                                      uT[:, k, hf * HALF:(hf + 1) * HALF], start=(k == 0), stop=(k == KT - 1))
                    last.then_inc(gate_ready, 1)
                    if n >= 2:
                        pe.wait_ge(proj_taken, n - 1)
                    for hf in range(2):
                        for k in range(2):
                            last = mm(pair[n % 2][hf], PT[:, d % 2, b * 256 + k * P:b * 256 + (k + 1) * P],
                                      oT[:, b, k, hf * HALF:(hf + 1) * HALF], start=(k == 0), stop=(k == 1))
                    last.then_inc(proj_ready, 1)
                    n += 1
                pe.drain().then_inc(wb_used, 1)
            stand(pe, 2)

            pe.wait_ge(wo_in, 32)

            def to_vT(j):
                nonlocal n_out
                pe.wait_ge(x1_ready, j + 1)
                for hf in range(2):
                    o = bank()
                    for q in range(4):
                        k = 4 * hf + q
                        last = nc.tensor.transpose(o[:, q * P:(q + 1) * P], x1[:, j, k * P:(k + 1) * P], ident[:])
                    last.then_inc(out_ready, 1)
                    n_out += 1

            for j in range(NT):
                if j >= 2:
                    pe.wait_ge(y_taken, j - 1)
                for hf in range(2):
                    for k in range(KT):
                        last = mm(psS[j % 2][:, hf * HALF:(hf + 1) * HALF], mrg[:, k, j * P:(j + 1) * P], ring[hf][:, k, :],
                                  start=(k == 0), stop=(k == KT - 1))
                last.then_inc(y_ready, 1)
                if j >= 2:
                    to_vT(j - 2)
            to_vT(NT - 2)
            to_vT(NT - 1)
            pe.wait_ge(out_taken, n_out)
            stand(pe, 3)

            pe.wait_ge(router_in, 32)
            for j in range(NT):
                for k in range(KT):
                    last = mm(psT[:, j * NE:(j + 1) * NE], vT[:, k, j * P:(j + 1) * P],
                              PT[:, 0, k * NE:(k + 1) * NE], start=(k == 0), stop=(k == KT - 1))
            last.then_inc(logit_ready, 1)
            pe.wait_ge(moe_const_in, 64)
            pe.wait_ge(counts_in, 1)
            mm(pb[0][:, 0:P], before, picked, start=True, stop=False)
            mm(pb[0][:, 0:P], ones, earlier[:, 0:P], start=False, stop=True)
            mm(pb[0][:, P:P + NE], ones, earlier[:, P:P + NE], start=True, stop=True).then_inc(ranks, 1)
            pe.wait_ge(hots_ready, 1)
            for c in range(2 * NT):
                last = mm(pb[1][:, 0:NB], onehots[:, c * P:(c + 1) * P], block_hot[:, c, :],
                          start=(c == 0), stop=(c == 2 * NT - 1))
            last.then_inc(slot_sum, 1)
            pe.wait_ge(slots_ready, 1)

            def rows_T(b, r, least):
                pe.wait_ge(xg_in[r], (b // 2 + 1) * 16 if isinstance(b, int) else b * 8 + (16 - 8 * r))
                if refill(b + 1):
                    pe.wait_ge(xt_taken, b)
                for k in range(KT):
                    last = nc.tensor.transpose(psT[:, k * P:(k + 1) * P], XG[:, r, k * P:(k + 1) * P], ident[:])
                last.then_inc(xt_ready, 1)

            def pe_slot(b):
                return bass.ds(pe.value_load(block_slot[0:1, bass.ds(b, 1)], min_val=0, max_val=1), 1)

            def gate_up(b, r, slot):
                pe.wait_ge(e_in[r], (b // 2 + 1) * 48 if isinstance(b, int) else b * 24 + (48 - 24 * r))
                pe.wait_ge(xt_taken, b + 1)
                if refill(b):
                    pe.wait_ge(ht_taken, b - 1)
                for k in range(KT):
                    last = mm(pb[r][:], XT[:, r, k * P:(k + 1) * P], ring_[:, slot, k * HALF:(k + 1) * HALF],
                              start=(k == 0), stop=(k == KT - 1))
                last.then_inc(gu_ready, 1)

            def hidden_T(b, r):
                pe.wait_ge(h_ready, b + 1)
                for f in range(2):
                    last = nc.tensor.transpose(pb[r][:, f * P:(f + 1) * P], HN[:, r, f * P:(f + 1) * P], ident[:])
                last.then_inc(ht_ready, 1)

            def down(b, r, slot):
                pe.wait_ge(ht_taken, b + 1)
                if refill(b):
                    pe.wait_ge(yb_ready, b - 1)
                for c in range(2):
                    for f in range(2):
                        last = mm(psS[r][:, c * HALF:(c + 1) * HALF], HT[:, r, f * P:(f + 1) * P],
                                  down_all[:, slot, f * S + c * HALF:f * S + (c + 1) * HALF], start=(f == 0), stop=(f == 1))
                last.then_inc(down_ready, 1)

            def pe_block(b, r, least):
                slot = pe_slot(b)
                slot_before = pe_slot(b - 1) if least >= 1 else None
                if least < NB - 1:
                    rows_T(b + 1, 1 - r, least + 1)
                gate_up(b, r, slot)
                if least >= 1:
                    down(b - 1, 1 - r, slot_before)
                hidden_T(b, r)

            rows_T(0, 0, 0)
            blocks(pe, pe_block)
            down(NB - 1, 0, pe_slot(NB - 1))

        @block.scalar
        def _(act):
            fn = nc.scalar.activation
            n_out = n_self = n_pt = n_vT = 0

            def take(dst, src, scale=1.0, bias=None):
                nonlocal n_out
                act.wait_ge(out_ready, n_out + 1)
                if bias is None:
                    ins = fn(dst, src, ACT.Copy, scale=scale)
                else:
                    ins = fn(dst, src, ACT.Identity, scale=scale, bias=bias)
                ins.then_inc(out_taken, 1)
                n_out += 1

            def nxt():
                return pb[n_out % 2]

            for a, b in ((lamq[:, 0, :], t["a_lambda_q"][0].rearrange("m d -> d m")),
                         (lamq[:, 1, :], t["a_lambda_k"][0].rearrange("m d -> d m")),
                         (onehot, t["onehot"]), (relt, t["rel_table"]), (isel[0:4, 0:TAB_W], t["tabmask"]),
                         (causal[:], t["causal"]), (bones[:], t["blockones"]),
                         (hsel[:], t["headsel"].rearrange("h (a p) -> h a p", a=2)), (iota[:], t["iota"]),
                         (subg[0:64, :], t["a_subln_g"][0].rearrange("(d a) -> d a", a=1)),
                         (subg[64:128, :], t["a_subln_g"][0].rearrange("(d a) -> d a", a=1)),
                         (sink[:], t["b_sinks"][0:1, :].broadcast_to([P, 4]))):
                act.dma_start(a, b, allow_slow_non_contiguous=True).then_inc(const_in, 16)
            for j in range(NT):
                act.dma_start(xn[:, j, :], t["x"][0, j * P:(j + 1) * P, :]).then_inc(x_in, 16)
            act.wait_ge(c_ready, 1)
            fn(cT[:, 1, :], cT[:, 0, :], ACT.Exp, scale=-1.0).then_inc(act_step, 1)
            act.wait_ge(mod_ready, 1)
            for k in range(KT):
                for hf in range(2):
                    take(uT[:, k, hf * HALF:(hf + 1) * HALF], nxt()[:], scale=modT[:, 8 + k:9 + k], bias=modT[:, k:k + 1])
            act.wait_ge(lam_sum, 1)
            fn(lam[:, 0:2], psT[:, HALF:HALF + 2], ACT.Exp).then_inc(lam_exp, 1)
            for c in range(3):
                for hf in range(2):
                    dst = qT[:, c, :] if c < 2 else ikT
                    take(dst[:, hf * HALF:(hf + 1) * HALF], nxt()[:])
            for hf in range(2):
                take(iwT[:, hf * HALF:(hf + 1) * HALF], nxt()[0:8, :])
            take(iw[:, :, :].rearrange("p t h -> p (t h)"), nxt()[:, 0:8 * NT])
            s = 0
            for j in range(2, NT):
                for h in range(8):
                    act.wait_ge(scores_ready, s + 1)
                    if s >= 4:
                        act.wait_ge(relu_used, s - 3)
                    fn(SR[:, s % 4, 0:(j + 1) * P], psS[s % 2][:, 0:(j + 1) * P], ACT.Relu).then_inc(relu_taken, 1)
                    s += 1

            for name in ORDER:
                scale = (32 if name == "A" else 64) ** -0.5
                for c in range(2 + KCOLS[name]):
                    for hf in range(2):
                        dst, src = half_in_order(qT[:, c, :] if c < 2 else kT[:, c - 2, :], nxt()[:], name, hf)
                        take(dst, src, scale=scale if c < 2 else 1.0)
                        if name in WITH_ADA:
                            c0 = 16 + 8 * WITH_ADA.index(name) + 2 * c + hf
                            take(modT[:, c0:c0 + 1], nxt()[:, 0:1])
                for j in range(NT):
                    take(V[:, j, 0:VCOLS[name]], nxt()[:, 0:VCOLS[name]])
                todo = list(units(name))

                def exps(i):
                    h, j, k0, k1 = todo[i]
                    n = (k1 - k0) * P
                    for m in range(2 if name == "A" else 1):
                        a = BASE[name] + (2 * i + m if name == "A" else i)
                        act.wait_ge(biased, a + 1)
                        fn(SR[:, a % 4, 0:n], SR[:, a % 4, 0:n], ACT.Exp, bias=negm[:, a:a + 1],
                           accum_out=den[:, a:a + 1]).then_inc(probs_ready, 1)

                def copy_probs(i):
                    nonlocal n_pt
                    h, j, k0, k1 = todo[i]
                    u = ORDER.index(name) * 32 + i
                    if u >= 2 and i < 2:
                        pass
                    elif i >= 2:
                        act.wait_ge(out_ready, n_out)
                    for b, c in enumerate(range(k0, k1, 4)):
                        wd = (min(c + 4, k1) - c) * P
                        act.wait_ge(pT_ready, n_pt + 1)
                        fn(PT[:, u % 2, b * HALF:b * HALF + wd], psT[:, b * HALF:b * HALF + wd], ACT.Copy).then_inc(pT_copied, 1)
                        n_pt += 1

                def take_output(i):
                    h, j, k0, k1 = todo[i]
                    dst = tile_tokens(oT[:, RAW[name], h // 2, :], name, j)
                    take(dst[(h % 2) * 64:(h % 2) * 64 + 64], nxt()[0:64, 0:P])

                for i in range(-2, len(todo)):
                    if i + 2 < len(todo):
                        exps(i + 2)
                    if 0 <= i + 1 < len(todo):
                        copy_probs(i + 1)
                    if i >= 0:
                        take_output(i)
                if name == "B":
                    for h in range(4):
                        ins = fn(rec[:, h:32:4], negm[:, h:32:4], ACT.Exp, bias=sink[:, h:h + 1])
                    ins.then_inc(sink_exp, 1)
                if name == "C2":
                    for g in range(3):
                        act.wait_ge(shift_ready, g + 1)
                        fn(fac[g], fac[g], ACT.Exp).then_inc(shift_exp, 1)
                if name == "A":
                    for i in range(4):
                        act.wait_ge(ms_ready, i + 1)
                        fn(bm[:, i % 2, 0:HALF], bm[:, i % 2, 0:HALF], ACT.Sqrt, bias=epsc[:]).then_inc(rms_ready, 1)
            act.wait_ge(mod_ready, 2)
            for r, c0 in ((0, 16), (1, 40)):
                act.dma_start(scratch["gates"][r].rearrange("(k p) -> p k", p=P), modT[:, c0:c0 + 8],
                              allow_slow_non_contiguous=True).then_inc(gcols_out, 16)
            stand(act, 1)

            for n in range(4 * KT):
                act.wait_ge(gate_ready, n + 1)
                if n >= 4:
                    act.wait_ge(proj_taken, n - 3)
                fn(SR[:, n % 4, :], psS[n % 2][:], ACT.Sigmoid).then_inc(sig_ready, 1)
            stand(act, 2)

            def take_vT(j):
                nonlocal n_out
                for hf in range(2):
                    act.wait_ge(out_ready, n_out + 1)
                    for q in range(4):
                        k = 4 * hf + q
                        ins = fn(vT[:, k, j * P:(j + 1) * P], pb[n_out % 2][:, q * P:(q + 1) * P], ACT.Identity,
                                 scale=modT[:, 32 + k:33 + k], bias=modT[:, 24 + k:25 + k])
                    ins.then_inc(out_taken, 1)
                    n_out += 1

            for j in range(NT):
                act.wait_ge(var_ready, j + 1)
                fn(sd[:, 0:1], mv[:, 0, 1:2], ACT.Sqrt, bias=epsc[:]).then_inc(sd_ready, 1)
                if j >= 2:
                    take_vT(j - 2)
            take_vT(NT - 2)
            take_vT(NT - 1)
            stand(act, 3)

            act.wait_ge(logit_max, 1)
            fn(route[:, 0], route[:, 0], ACT.Exp).then_inc(logit_exp, 1)

            def take_rows(b, r, least):
                act.wait_ge(xt_ready, b + 1)
                if refill(b):
                    act.wait_ge(gu_ready, b - 1)
                for k in range(KT):
                    ins = fn(XT[:, r, k * P:(k + 1) * P], psT[:, k * P:(k + 1) * P], ACT.Identity,
                             scale=modT[:, 32 + k:33 + k], bias=modT[:, 24 + k:25 + k])
                ins.then_inc(xt_taken, 1)

            def store_results(b, r):
                act.wait_ge(yb_ready, b + 1)
                act.dma_start(scratch["yb"][bass.ds(b * P, P), :] if not isinstance(b, int) else
                              scratch["yb"][b * P:(b + 1) * P, :], YB[:, r, :]).then_inc(yb_out[r], 16)

            def act_block(b, r, least):
                if least < NB - 1:
                    take_rows(b + 1, 1 - r, least + 1)
                act.wait_ge(gu_ready, b + 1)
                if refill(b):
                    act.wait_ge(h_ready, b - 1)
                fn(SIG[:, r, :], pb[r][:, 0:FF], ACT.Sigmoid).then_inc(gsig_ready, 1)
                act.wait_ge(ht_ready, b + 1)
                if refill(b):
                    act.wait_ge(down_ready, b - 1)
                fn(HT[:, r, :], pb[r][:, 0:FF], ACT.Copy).then_inc(ht_taken, 1)
                if least >= 1:
                    store_results(b - 1, 1 - r)

            take_rows(0, 0, 0)
            blocks(act, act_block)
            store_results(NB - 1, 0)
            for j in range(NT):
                act.wait_ge(var_ready, NT + j + 1)
                fn(sd[:, 0:1], mv[:, 0, 1:2], ACT.Sqrt, bias=epsc[:]).then_inc(sd_ready, 1)

        @block.gpsimd
        def _(pool):
            pool.wait_ge(cond_ready, 1)
            for m in range(32):
                piece = ada_w[m % 2]
                pool.wait_ge(ada_in[m % 2], 16 * (m // 2 + 1))
                nc.gpsimd.tensor_tensor(piece, piece, cT[:, 1, :].unsqueeze(2).broadcast_to([P, KT, P]), ALU.mult
                                        ).then_inc(piece_step, 1)
                for i, n in enumerate((4, 2, 1)):
                    pool.wait_ge(piece_step, 3 * m + i + 1)
                    nc.gpsimd.tensor_tensor(piece[:, 0:n, :], piece[:, 0:n, :], piece[:, n:2 * n, :], ALU.add
                                            ).then_inc(piece_step if n > 1 else piece_summed, 1)
            pool.wait_ge(a_biased, 1)
            for h in range(4):
                strip(pool, stripAD[:, h, :], "D", h, stripD_in)
            pool.wait_ge(stripD_in, 64)
            n = 0
            for j in range(2, NT):
                pool.wait_ge(sel_ready, j - 1)
                for h in range(4):
                    if n >= 2:
                        pool.wait_ge(biased, BASE["D"] + 8 + n - 1)
                    elif n == 0:
                        pool.wait_ge(norm_taken, 4 + 24 + 4)
                        pool.wait_ge(sum_done, 2)
                    wd = (j + 1) * P
                    nc.gpsimd.tensor_tensor(bm[:, n % 2, 0:wd], stripAD[:, h, S - wd:S], idx_tile(j), ALU.add
                                            ).then_inc(bm_ready, 1)
                    n += 1
            stand(pool, 1)
            stand(pool, 2)
            stand(pool, 3)
            pool.wait_ge(x1_out, 16 * NT)
            pool.wait_ge(slots_ready, 1)

            def gather_rows(b, r, least):
                if refill(b):
                    pool.wait_ge(xt_ready, b - 1)
                idx = slot_idx[:, b:b + 1] if isinstance(b, int) else slot_idx[:, bass.ds(b, 1)]
                nc.gpsimd.tensor_copy(slot_now[:, r:r + 1], idx).then_inc(pool_step, 1)
                pool.wait_ge(pool_step, b + 1)
                pool.sem_inc(gather_go, 1)
                nc.gpsimd.indirect_dma_start(XG[:, r, :], None, scratch["x1"],
                                             bass.IndirectOffsetOnAxis(ap=slot_now[:, r:r + 1], axis=0)
                                             ).then_inc(xg_in[r], 16)

            blocks(pool, gather_rows)
            pool.wait_ge(yb_out[0], 16 * (NB // 2 + 1))
            pool.wait_ge(yb_out[1], 16 * (NB // 2))
            for c in range(2 * NT):
                j, m = c // 2, c % 2
                if c >= 4:
                    pool.wait_ge(y_added, c // 2 - 1)
                nc.gpsimd.indirect_dma_start(picks[:, c % 4, :], None, scratch["yb"],
                                             bass.IndirectOffsetOnAxis(ap=dest_idx[:, 8 * m + j:8 * m + j + 1], axis=0)
                                             ).then_inc(pick_in[c % 4], 16)

        @block.vector
        def _(dve):
            v = nc.vector
            n_self = 0

            def step(ins):
                nonlocal n_self
                n_self += 1
                ins.then_inc(dve_step, 1)
                dve.wait_ge(dve_step, n_self)

            v.memset(epsc[:], EPS)
            v.memset(ones_col[:], 1.0)
            dve.wait_ge(vecs_T, 1)
            v.tensor_copy(badaT[:], psT[:, 0:48])
            v.tensor_copy(cT[:, 0, :], psT[:, 48:56]).then_inc(c_ready, 1)
            dve.wait_ge(act_step, 1)
            step(v.tensor_scalar(cT[:, 1, :], cT[:, 1, :], 1.0, None, ALU.add))
            step(v.reciprocal(cT[:, 1, :], cT[:, 1, :]))
            v.tensor_tensor(cT[:, 1, :], cT[:, 1, :], cT[:, 0, :], ALU.mult).then_inc(cond_ready, 1)
            dve.wait_ge(cond_ready, 1)
            for n in range(4):
                acc = ada_acc[:, n * HALF:(n + 1) * HALF]
                src = ring[n] if n < 2 else ada_uT[n - 2]
                dve.wait_ge(w_landed[n] if n < 2 else ada_uT_in[n - 2], 16)
                step(v.tensor_scalar(acc, src[:, 0, :], cT[:, 1, 0:1], None, ALU.mult))
                for k in range(1, KT):
                    step(v.scalar_tensor_tensor(acc, src[:, k, :], cT[:, 1, k:k + 1], acc, ALU.mult, ALU.add))
                dve.sem_inc(ada_used, 1)
                dve.sem_inc(ada_summed, 1)
            dve.wait_ge(mod_sum, 1)
            step(v.tensor_tensor(modT[:, 0:16], psT[:, 0:16], badaT[:, 0:16], ALU.add))
            v.tensor_scalar(modT[:, 8:16], modT[:, 8:16], 1.0, None, ALU.add).then_inc(mod_ready, 1)
            dve.wait_ge(const_in, 16 * N_CONST)
            v.memset(PT[0:32, 1, 0:P], 1.0)
            v.tensor_tensor(PT[0:32, 1, P:P + 2], lamq[:, 0, :], lamq[:, 1, :], ALU.mult).then_inc(lam_ops, 1)
            n = 0
            for name, h0, width, *_ in TABLES:
                for c in range(0, width + P, HALF):
                    wd = min(HALF, width + P - c)
                    at = TAB_OFF[name] + c
                    dve.wait_ge(tab_ready, n + 1)
                    v.tensor_tensor(isel[0:4, at:at + wd], psS[n % 2][0:4, 0:wd], isel[0:4, at:at + wd], ALU.add
                                    ).then_inc(tab_taken, 1)
                    n += 1
            dve.wait_ge(lam_exp, 1)
            step(v.tensor_tensor(lam[:, 2:3], lam[:, 1:2], lam[:, 0:1], ALU.subtract))
            step(v.tensor_scalar(lam[:, 3:4], lam[:, 2:3], -LAM0, None, ALU.add))
            step(v.tensor_scalar(subg[:], subg[:], 1.0 - LAM0, None, ALU.mult))

            dve.wait_ge(tab_out, 16)
            s = 0
            for j in range(2, NT):
                acc = idx_tile(j)
                wd = (j + 1) * P
                for h in range(8):
                    dve.wait_ge(relu_taken, s + 1)
                    if h == 0:
                        ins = v.tensor_scalar(acc, SR[:, s % 4, 0:wd], iw[:, j, 0:1], None, ALU.mult)
                    else:
                        ins = v.scalar_tensor_tensor(acc, SR[:, s % 4, 0:wd], iw[:, j, h:h + 1], acc, ALU.mult, ALU.add)
                    ins.then_inc(relu_used, 1)
                    s += 1
                    dve.wait_ge(relu_used, s)
                step(v.tensor_tensor(acc[:, j * P:], acc[:, j * P:], causal[:], ALU.add))

            def top_k(j, r0=0, r1=TOPK // 8):
                acc = idx_tile(j)
                for _ in range(r0, r1):
                    step(v.max(top8[:], acc))
                    step(v.match_replace(acc, top8[:], acc, TAKEN))
                if r1 == TOPK // 8:
                    v.tensor_scalar(acc, acc, TAKEN, MASKED, ALU.not_equal, ALU.mult).then_inc(sel_ready, 1)

            n_norm = n_diff = 0

            def norm_src():
                nonlocal n_norm
                dve.wait_ge(norm_ready, n_norm + 1)
                n_norm += 1
                return psT[:, ((n_norm - 1) % 2) * HALF:((n_norm - 1) % 2 + 1) * HALF]

            TOPS = {"B": ((2,), (3, 0, 16)), "C0": ((3, 16), (4,)), "C1": ((5,),), "C2": ((6,),), "A": ((7,),), "D": ()}
            for name in ORDER:
                for part in TOPS[name]:
                    top_k(*part)
                if name == "B":
                    dve.wait_ge(strip_in, 16 * 16)
                if name == "A":
                    dve.wait_ge(stripAD_in, 64)
                if name == "D":
                    step(v.tensor_tensor(modT[:, 16:48], modT[:, 16:48], badaT[:, 16:48], ALU.add))
                    for c0 in (16, 32):
                        step(v.tensor_scalar(modT[:, c0:c0 + 8], modT[:, c0:c0 + 8], 1.0, None, ALU.add))
                    v.tensor_scalar(modT[:, 40:48], modT[:, 40:48], 1.0, None, ALU.add).then_inc(mod_ready, 1)
                    dve.wait_ge(stripD_in, 64)
                for i, (h, j, k0, k1) in enumerate(units(name)):
                    wd = (k1 - k0) * P
                    maps = 2 if name == "A" else 1
                    for m in range(maps):
                        a = BASE[name] + maps * i + m
                        dve.wait_ge(scores_ready, N_IDX + a + 1)
                        if a >= 4:
                            dve.wait_ge(pT_ready, BANKS[a - 4])
                        if name == "D" and j >= 2:
                            n = 4 * (j - 2) + h
                            dve.wait_ge(bm_ready, n + 1)
                            bias = bm[:, n % 2, 0:wd]
                        else:
                            bias = bias_strip(name, h, wd)
                        v.tensor_tensor_reduce(out=SR[:, a % 4, 0:wd], in0=psS[a % 2][:, 0:wd], in1=bias, scale=1.0,
                                               scalar=sink[:, h:h + 1] if name == "B" else LOWEST,
                                               op0=ALU.add, op1=ALU.max, accum_out=mx[:, a:a + 1]).then_inc(scores_taken, 1)
                        dve.wait_ge(scores_taken, a + 1)
                        v.tensor_scalar(negm[:, a:a + 1], mx[:, a:a + 1], -1.0, None, ALU.mult).then_inc(biased, 1)
                    if name == "A":
                        if i == 31:
                            dve.wait_ge(biased, a + 1)
                            dve.sem_inc(a_biased, 1)
                        for q in ([i - 1] if i else []) + ([31] if i == 31 else []):
                            hh, jj = q % 4, q // 4
                            wq = (jj + 1) * P
                            a0 = BASE["A"] + 2 * q
                            dve.wait_ge(probs_ready, a0 + 2)
                            step(v.reciprocal(rec[:, a0:a0 + 2], den[:, a0:a0 + 2]))
                            step(v.tensor_tensor(rec[:, a0 + 1:a0 + 2], rec[:, a0 + 1:a0 + 2], lam[:, 3:4], ALU.mult))
                            s0, s1 = a0 % 4, (a0 + 1) % 4
                            step(v.tensor_scalar(SR[:, s1, 0:wq], SR[:, s1, 0:wq], rec[:, a0 + 1:a0 + 2], None, ALU.mult))
                            v.scalar_tensor_tensor(SR[:, s0, 0:wq], SR[:, s0, 0:wq], rec[:, a0:a0 + 1], SR[:, s1, 0:wq],
                                                   ALU.mult, ALU.add).then_inc(diff_ready, 1)
                if name in ("B", "D"):
                    a0 = BASE[name]
                    dve.wait_ge(probs_ready, a0 + 32)
                    if name == "B":
                        dve.wait_ge(sink_exp, 1)
                        step(v.tensor_tensor(den[:, 0:32], den[:, 0:32], rec[:, 0:32], ALU.add))
                    step(v.reciprocal(rec[:, a0:a0 + 32], den[:, a0:a0 + 32]))
                    dve.wait_ge(pT_ready, BANKS[a0 + 31])
                    v.tensor_copy(bcols.rearrange("p (c n) -> p c n", n=64),
                                  rec[:, a0:a0 + 32].unsqueeze(2).broadcast_to([P, 32, 64])).then_inc(cols_ready, 1)
                    for pr in range(2):
                        for hf in range(2):
                            o = oT[:, RAW[name], pr, hf * HALF:(hf + 1) * HALF]
                            v.tensor_tensor(o, norm_src(), o, ALU.mult).then_inc(norm_taken, 1)
                if name == "C2":
                    for g in range(3):
                        for st in (fac[g], fden[g]):
                            for hf in range(2):
                                dst, src = rows_to_tokens(st, norm_src()[0:4, :], f"C{g}", hf)
                                v.tensor_copy(dst, src).then_inc(norm_taken, 1)
                    dve.wait_ge(norm_taken, n_norm)
                    step(v.tensor_tensor(fmax, fac[0], fac[1], ALU.max))
                    step(v.tensor_tensor(fmax, fmax, fac[2], ALU.max))
                    for g in range(3):
                        v.tensor_tensor(fac[g], fac[g], fmax, ALU.subtract).then_inc(shift_ready, 1)
                    dve.wait_ge(shift_ready, 3)
                    for g in range(3):
                        dve.wait_ge(shift_exp, g + 1)
                        step(v.tensor_tensor(fden[g], fden[g], fac[g], ALU.mult))
                        if g:
                            step(v.tensor_tensor(fden[0], fden[0], fden[g], ALU.add))
                    step(v.reciprocal(fden[0], fden[0]))
                    for g in range(3):
                        ins = v.tensor_tensor(fac[g], fac[g], fden[0], ALU.mult)
                        if g < 2:
                            step(ins)
                    ins.then_inc(cols_ready, 1)
                    for g in range(3):
                        for pr in range(2):
                            for hf in range(2):
                                o = oT[:, RAW[f"C{g}"], pr, hf * HALF:(hf + 1) * HALF]
                                v.tensor_tensor(o, norm_src(), o, ALU.mult).then_inc(norm_taken, 1)
                                dve.wait_ge(norm_taken, n_norm)
                                if g:
                                    o0 = oT[:, 2, pr, hf * HALF:(hf + 1) * HALF]
                                    step(v.tensor_tensor(o0, o0, o, ALU.add))
                    dve.sem_inc(sum_done, 1)
                if name == "A":
                    for i in range(4):
                        if i == 0:
                            dve.wait_ge(out_taken, OUTS["A"])
                        o = oT[:, 0, i // 2, (i % 2) * HALF:(i % 2 + 1) * HALF]
                        v.tensor_tensor(bm[:, i % 2, 0:HALF], o, o, ALU.mult).then_inc(sq_ready, 1)
                        v.tensor_copy(bm[:, i % 2, 0:HALF], norm_src()).then_inc(norm_taken, 1)
                        dve.wait_ge(norm_taken, n_norm)
                        dve.sem_inc(ms_ready, 1)
                        dve.wait_ge(rms_ready, i + 1)
                        step(v.reciprocal(bm[:, i % 2, 0:HALF], bm[:, i % 2, 0:HALF]))
                        step(v.scalar_tensor_tensor(o, o, subg[:], bm[:, i % 2, 0:HALF], ALU.mult, ALU.mult))
                    dve.sem_inc(sum_done, 1)
            stand(dve, 1)

            for n in range(4 * KT):
                d, b = n // 4, n % 4
                dve.wait_ge(sig_ready, n + 1)
                dve.wait_ge(proj_ready, n + 1)
                for hf in range(2):
                    o = mrg[:, d, hf * HALF:(hf + 1) * HALF]
                    g = SR[:, n % 4, hf * HALF:(hf + 1) * HALF]
                    ins = v.tensor_tensor(g if b else o, pair[n % 2][hf], g, ALU.mult)
                ins.then_inc(proj_taken, 1)
                dve.wait_ge(proj_taken, n + 1)
                if b:
                    step(v.tensor_tensor(mrg[:, d, :], mrg[:, d, :], SR[:, n % 4, :], ALU.add))
            stand(dve, 2)

            def layer_norm(dst, tmp, r, n):
                for hf in range(2):
                    ins = v.bn_stats(stats[:, 0, hf, :], tmp[:, hf * HALF:(hf + 1) * HALF])
                    step(ins)
                step(v.bn_aggr(mv[:, 0, :], stats[:, 0, :, :].rearrange("p a b -> p (a b)")))
                dve.sem_inc(var_ready, 1)
                dve.wait_ge(sd_ready, n + 1)
                step(v.reciprocal(sd[:, 1:2], sd[:, 0:1]))
                step(v.tensor_scalar(dst, tmp, mv[:, 0, 0:1], sd[:, 1:2], ALU.subtract, ALU.mult))
                step(v.tensor_tensor(dst, dst, rows[:, r, :], ALU.mult))
                return v.tensor_tensor(dst, dst, rows[:, r + 1, :], ALU.add)

            dve.wait_ge(rows_in, 96)
            tmp = SR[:, 2, :]
            for j in range(NT):
                dve.wait_ge(y_ready, j + 1)
                v.tensor_tensor(tmp, psS[j % 2][:], rows[:, 0, :], ALU.mult).then_inc(y_taken, 1)
                dve.wait_ge(y_taken, j + 1)
                dve.wait_ge(xr_in[j % 2], 16 * (j // 2 + 1))
                step(v.scalar_tensor_tensor(tmp, SR[:, j % 2, :], ALPHA, tmp, ALU.mult, ALU.add))
                layer_norm(x1[:, j, :], tmp, 1, j).then_inc(x1_ready, 1)
            stand(dve, 3)

            dve.wait_ge(logit_ready, 1)
            dve.wait_ge(router_in, 32)
            b3 = lambda ap: ap.unsqueeze(2).broadcast_to([P, NT, NE])
            R = [route[:, i] for i in range(11)]
            c1 = small[:, 0:8]
            step(v.tensor_copy(R[0], psT[:, 0:P].rearrange("p (t e) -> p t e", t=NT)))
            step(v.tensor_reduce(c1, R[0], AX.X, ALU.max))
            step(v.tensor_tensor(R[0], R[0], b3(c1), ALU.subtract))
            dve.sem_inc(logit_max, 1)
            dve.wait_ge(logit_exp, 1)
            step(v.tensor_reduce(c1, R[0], AX.X, ALU.add))
            step(v.reciprocal(c1, c1))
            step(v.tensor_tensor(R[0], R[0], b3(c1), ALU.mult))
            step(v.tensor_tensor(R[1], R[0], PT[:, 0, P:P + NE].unsqueeze(1).broadcast_to([P, NT, NE]), ALU.add))
            grp = R[1].rearrange("p t (g m) -> p t g m", g=4)
            gs, ps_ = R[2][:, :, 0:4], R[2][:, :, 4:8]
            first = True
            for a in range(4):
                for b in range(a + 1, 4):
                    step(v.tensor_tensor(gs if first else ps_, grp[:, :, :, a], grp[:, :, :, b], ALU.add))
                    if not first:
                        step(v.tensor_tensor(gs, gs, ps_, ALU.max))
                    first = False

            def first_best(mask, vals, n, tmp_):
                iot = iota[:, 0:n].unsqueeze(1).broadcast_to([P, NT, n])
                spread = c1.unsqueeze(2).broadcast_to([P, NT, n])
                step(v.tensor_reduce(c1, vals, AX.X, ALU.max))
                step(v.tensor_tensor(tmp_, vals, spread, ALU.is_equal))
                step(v.tensor_tensor(tmp_, tmp_, iot, ALU.mult))
                step(v.tensor_reduce(c1, tmp_, AX.X, ALU.min))
                step(v.tensor_tensor(mask, iot, spread, ALU.is_equal))

            first_best(R[3][:, :, 0:4], gs, 4, R[4][:, :, 0:4])
            step(v.tensor_scalar(R[3][:, :, 4:8], R[3][:, :, 0:4], 0.0, MASKED, ALU.is_equal, ALU.mult))
            for m in range(4):
                step(v.tensor_tensor(R[5].rearrange("p t (g m) -> p t g m", g=4)[:, :, :, m],
                                     grp[:, :, :, m], R[3][:, :, 4:8], ALU.add))
            first_best(R[6], R[5], NE, R[4])
            step(v.tensor_scalar(R[7], R[6], 2.0 * MASKED, None, ALU.mult))
            step(v.tensor_tensor(R[5], R[5], R[7], ALU.add))
            first_best(R[8], R[5], NE, R[4])
            for m, mask in ((0, R[6]), (1, R[8])):
                step(v.tensor_tensor(R[4], mask, R[0], ALU.mult))
                step(v.tensor_reduce(topw[:, 8 * m:8 * m + 8], R[4], AX.X, ALU.add))
            step(v.tensor_tensor(c1, topw[:, 0:8], topw[:, 8:16], ALU.add))
            step(v.reciprocal(c1, c1))
            for m in range(2):
                step(v.tensor_tensor(topw[:, 8 * m:8 * m + 8], topw[:, 8 * m:8 * m + 8], c1, ALU.mult))
            step(v.tensor_tensor(R[7], R[6], R[8], ALU.add))
            step(v.memset(earlier[:, 0:NE], 0.0))
            for j in range(NT):
                ins = v.tensor_tensor(earlier[:, (j + 1) * NE:(j + 2) * NE], earlier[:, j * NE:(j + 1) * NE],
                                      R[7][:, j, :], ALU.add)
                if j < NT - 1:
                    step(ins)
            ins.then_inc(counts_in, 1)
            dve.wait_ge(moe_const_in, 64)
            dve.wait_ge(ranks, 1)
            step(v.tensor_copy(R[1], pb[0][:, 0:P].rearrange("p (t e) -> p t e", t=NT)))
            cnt, nblk, bend, tmp16 = (small[:, 16 * i:16 * i + 16] for i in range(1, 5))
            step(v.tensor_copy(cnt, pb[0][:, P:P + NE]))
            step(v.tensor_scalar(nblk, cnt, 0.0, None, ALU.is_gt))
            for m in range(1, NT):
                step(v.scalar_tensor_tensor(nblk, cnt, float(m * P), nblk, ALU.is_gt, ALU.add))
            src, dst = nblk, bend
            step(v.tensor_copy(bend, nblk))
            for sh in (1, 2, 4, 8):
                step(v.tensor_copy(tmp16, bend))
                step(v.tensor_tensor(bend[:, sh:NE], tmp16[:, sh:NE], tmp16[:, 0:NE - sh], ALU.add))
            step(v.tensor_tensor(blk_cmp, bend.unsqueeze(1).broadcast_to([P, NB, NE]),
                                 iota_row[:, 0:NB].unsqueeze(2).broadcast_to([P, NB, NE]), ALU.is_le))
            step(v.tensor_reduce(blk_sum, blk_cmp, AX.X, ALU.add))
            step(v.tensor_scalar(blk_sum, blk_sum, float(NE - 1), None, ALU.min))
            step(v.tensor_copy(block_expert[:], blk_sum))
            step(v.memset(blk_new, 1.0))
            step(v.tensor_tensor(blk_new[:, 1:NB], blk_sum[:, 1:NB], blk_sum[:, 0:NB - 1], ALU.not_equal))
            step(v.tensor_copy(block_new[:], blk_new))
            for sh in (1, 2, 4, 8, 16):
                step(v.tensor_copy(blk_tmp, blk_new))
                step(v.tensor_tensor(blk_new[:, sh:NB], blk_tmp[:, sh:NB], blk_tmp[:, 0:NB - sh], ALU.add))
            step(v.tensor_copy(block_slot[:], blk_new))
            step(v.tensor_scalar(block_slot[:], block_slot[:], 1, None, ALU.bitwise_and))
            step(v.tensor_tensor(tmp16, bend, nblk, ALU.subtract))
            for m, mask in ((0, R[6]), (1, R[8])):
                step(v.tensor_tensor(R[4], mask, R[1], ALU.mult))
                step(v.tensor_reduce(rank[:, 8 * m:8 * m + 8], R[4], AX.X, ALU.add))
                step(v.tensor_tensor(R[4], mask, tmp16.unsqueeze(1).broadcast_to([P, NT, NE]), ALU.mult))
                step(v.tensor_reduce(blk[:, 8 * m:8 * m + 8], R[4], AX.X, ALU.add))
            step(v.tensor_scalar(moved, rank, float(P), None, ALU.is_ge))
            for m in range(2, NT):
                step(v.scalar_tensor_tensor(moved, rank, float(m * P), moved, ALU.is_ge, ALU.add))
            step(v.scalar_tensor_tensor(rank, moved, -float(P), rank, ALU.mult, ALU.add))
            step(v.tensor_tensor(blk, blk, moved, ALU.add))
            step(v.scalar_tensor_tensor(moved, blk, float(P), rank, ALU.mult, ALU.add))
            step(v.tensor_copy(dest_idx[:], moved))
            for c in range(2 * NT):
                j = c % NT
                v.tensor_scalar(onehots[:, c * P:(c + 1) * P], iota_row, rank[:, c:c + 1], None, ALU.is_equal)
                ins = v.tensor_scalar(block_hot[:, c, :], iota_row[:, 0:NB], blk[:, c:c + 1], token_id[:, j:j + 1],
                                      ALU.is_equal, ALU.mult)
            ins.then_inc(hots_ready, 1)
            dve.wait_ge(slot_sum, 1)
            v.tensor_copy(slot_idx[:], pb[1][:, 0:NB]).then_inc(slots_ready, 1)

            def results(b, r, least):
                dve.wait_ge(down_ready, b + 1)
                if refill(b):
                    dve.wait_ge(yb_out[r], b // 2 * 16 if isinstance(b, int) else b * 8 - 8 * r)
                v.tensor_copy(YB[:, r, :], psS[r][:]).then_inc(yb_ready, 1)

            def dve_block(b, r, least):
                dve.wait_ge(gsig_ready, b + 1)
                v.tensor_tensor(SIG[:, r, :], pb[r][:, 0:FF], SIG[:, r, :], ALU.mult).then_inc(silu_ready, 1)
                dve.wait_ge(silu_ready, b + 1)
                if refill(b):
                    dve.wait_ge(ht_ready, b - 1)
                v.tensor_tensor(HN[:, r, :], pb[r][:, FF:2 * FF], SIG[:, r, :], ALU.mult).then_inc(h_ready, 1)
                if least >= 1:
                    results(b - 1, 1 - r, least - 1)

            blocks(dve, dve_block)
            results(NB - 1, 0, NB - 1)

            for j in range(NT):
                q = (2 * j) % 4
                y = ytmp[:, j % 2, :]
                dve.wait_ge(pick_in[q], 16 * (j // 2 + 1))
                step(v.tensor_scalar(y, picks[:, q, :], topw[:, j:j + 1], None, ALU.mult))
                dve.wait_ge(pick_in[q + 1], 16 * (j // 2 + 1))
                v.scalar_tensor_tensor(y, picks[:, q + 1, :], topw[:, 8 + j:9 + j], y, ALU.mult, ALU.add).then_inc(y_added, 1)
                dve.wait_ge(y_added, j + 1)
                step(v.tensor_tensor(y, y, rows[:, 3, :], ALU.mult))
                step(v.scalar_tensor_tensor(y, x1[:, j, :], ALPHA, y, ALU.mult, ALU.add))
                if j >= 2:
                    dve.wait_ge(out_done[j % 2], 16 * (j // 2))
                layer_norm(yout[:, j % 2, :], y, 4, NT + j).then_inc(fin_ready, 1)


_INS = ['x', 'c', 'rel_table', 'w_router', 'b_router', 'w_ada', 'b_ada', 'w_in', 'a_lambda_q', 'a_lambda_k',
        'a_subln_g', 'b_sinks', 'w_branch', 'w_out', 'ln1_g', 'ln1_b', 'w_exp_gate', 'w_exp_up', 'w_exp_down',
        'ln2_g', 'ln2_b']


def kernel(**inputs):
    import concourse.bacc as bacc
    from concourse.bass_utils import run_bass_kernel_spmd

    nc = bacc.Bacc("TRN2", target_bir_lowering=False, num_devices=1)
    arrays = {name: np.ascontiguousarray(inputs[name]) for name in _INS}
    arrays.update(table_constants())
    t = {name: nc.dram_tensor(f"in_{name}", a.shape, mybir.dt.from_np(a.dtype), kind="ExternalInput").ap()
         for name, a in arrays.items()}
    out = nc.dram_tensor("out", (1, S, D), F32, kind="ExternalOutput").ap()
    scratch = {"gtab": nc.dram_tensor("gtab", (4, TAB_W), F32, kind="Internal").ap(),
               "shifted": nc.dram_tensor("shifted", (4, P * (TAB_W + P + 1)), F32, kind="Internal").ap(),
               "x1": nc.dram_tensor("x1_rows", (S, D), F32, kind="Internal").ap(),
               "yb": nc.dram_tensor("block_results", (NB * P, D), F32, kind="Internal").ap(),
               "gates": nc.dram_tensor("gate_rows", (2, D), F32, kind="Internal").ap()}
    build(nc, t, out, scratch)
    r = run_bass_kernel_spmd(nc, [{f"in_{n}": a for n, a in arrays.items()}], core_ids=[0])
    return r.results[0]["out"]
```

```python
import math
from contextlib import ExitStack
from itertools import islice

import numpy as np
import concourse.bass as bass
from concourse import mybir

F32 = mybir.dt.float32
F32R = mybir.dt.float32r
ALU = mybir.AluOpType
ACT = mybir.ActivationFunctionType
AX = mybir.AxisListType

P = 128
D = 1024
S = 1024
KT = D // P
NT = S // P
HALF = 512
HD = 64
NE = 16
FF = 256
NB = 2 * S // P + NE - 1
ALPHA = 2.0 ** 0.25
EPS = 1e-5
LAM0 = 0.8 - 0.6 * math.exp(0.0)
TOPK = 256
MASKED = -1.0e30
TAKEN = -3.0e38
LOWEST = -3.4e38

SPLITS = (("a_q", 256), ("a_k", 256), ("a_v", 256), ("b_q", 256), ("b_k", 128), ("b_v", 128),
          ("c_q", 768), ("c_k", 768), ("c_v", 768), ("d_q", 256), ("d_k", 64), ("d_v", 64),
          ("i_q", 256), ("i_k", 32), ("i_w", 8), ("gate", 4096))
COL = {}
for _n, _w in SPLITS:
    COL[_n] = sum(w for _, w in SPLITS[:len(COL)])

TABLES = (("A", 0, 1024, 1023, 1, 1023), ("B", 4, 256, 255, 1, 127), ("C0", 8, 256, 255, 1, 128),
          ("C1", 12, 256, 255, 4, 128), ("C2", 16, 128, 127, 8, 127), ("D", 20, 1024, 1023, 1, 1023))
TAB_OFF, _o = {}, 0
for _t in TABLES:
    TAB_OFF[_t[0]] = _o
    _o += _t[2] + P
TAB_W = _o


def table_constants():
    onehot = np.zeros((32, TAB_W), np.float32)
    mask = np.zeros((4, TAB_W), np.float32)
    for name, _, width, d0, dil, most in TABLES:
        for x in range(width + P):
            steps = d0 - x
            if 0 <= steps <= most and not (name == "C2" and steps % 2):
                n = steps * dil
                b = n if n < 16 else min(31, 16 + int(math.log(n / 16) / math.log(2048 / 16) * 16))
                onehot[b, TAB_OFF[name] + x] = 1.0
            else:
                mask[:, TAB_OFF[name] + x] = MASKED
    sel = np.zeros((4, 2, P), np.float32)
    for h in range(4):
        sel[h, h // 2, (h % 2) * 64:(h % 2) * 64 + 64] = 1.0
    blockones = np.zeros((P, P), np.float32)
    blockones[:64, :64] = blockones[64:, 64:] = 1.0 / 64
    tri = np.where(np.arange(P)[None, :] <= np.arange(P)[:, None], 0.0, MASKED).astype(np.float32)
    iota = np.broadcast_to(np.arange(16, dtype=np.float32) - 99.0, (P, 16)).copy()
    p = np.arange(P, dtype=np.float32)
    return dict(before=(p[:, None] < p[None, :]).astype(np.float32), ones=np.ones((P, P), np.float32),
                iota_row=np.broadcast_to(p, (P, P)).copy(),
                token_id=(p[:, None] + P * np.arange(NT, dtype=np.float32)[None, :]), onehot=onehot, tabmask=mask,
                headsel=sel.reshape(4, 256), blockones=blockones,
                ident=np.eye(P, dtype=np.float32), causal=tri, iota=iota)


N_TAB = sum(-(-(x[2] + P) // HALF) for x in TABLES)


def build(nc, t, out, scratch):
    ctx = ExitStack()
    with ctx:
        def sb(name, shape, dt=F32):
            return ctx.enter_context(nc.sbuf_tensor(name, shape, dt))

        def sem(name):
            return ctx.enter_context(nc.semaphore(name))

        KB = 256
        shared = {"uT": [P, KT, S], "ring": [P, 2, KT * HALF], "strips": [P, 30 * KB], "isel": [P, 4224]}
        with ExitStack() as first:
            uT_, ring_, strips_, isel = (first.enter_context(nc.sbuf_tensor(n, shape, F32)) for n, shape in shared.items())
        uT_r, ring_r, strips_r, isel_r = (sb(n + "_r", shape, F32R) for n, shape in shared.items())
        oT_ = sb("oT", [P, 4, 2, S])
        qkv_ = sb("qkv", [P, 32 * KB])
        SR = sb("SR", [P, 4, S])
        PT = sb("PT", [P, 2, S])
        ident = sb("ident_sb", [P, P])
        causal = sb("causal_sb", [P, P])
        bones = sb("bones_sb", [P, P])
        hsel = sb("hsel_sb", [4, 2, P])
        iota = sb("iota_sb", [P, 16])
        badaT = sb("badaT", [P, 48])
        modT = sb("modT", [P, 48])
        cT = sb("cT", [P, 2, KT])
        lamq = sb("lamq", [32, 2, 2])
        lam = sb("lam", [P, 4])
        subg = sb("subg", [P, 1])
        ones_col = sb("ones_col", [P, 1])
        sink = sb("sink", [P, 4])
        epsc = sb("epsc", [P, 1])
        iw = sb("iw", [P, NT, 8])
        mx = sb("mx", [P, 224 + 8])
        negm = sb("negm", [P, 224 + 8])
        den = sb("den", [P, 224 + 8])
        rec = sb("rec", [P, 224 + 8])
        top8 = sb("top8", [P, 8])
        stats = sb("stats", [P, 2, 2, 6])
        mv = sb("mv", [P, 2, 2])
        sd = sb("sd", [P, 2])
        slot_idx = sb("slot_idx", [P, NB], mybir.dt.int32)
        slot_now = sb("slot_now", [P, 2], mybir.dt.int32)
        block_expert = sb("block_expert", [P, NB], mybir.dt.int32)
        block_new = sb("block_new", [P, NB], mybir.dt.int32)
        block_slot = sb("block_slot", [P, NB], mybir.dt.int32)
        dest_idx = sb("dest_idx", [P, 2 * NT], mybir.dt.int32)

        uT, oT = uT_, oT_
        ring = [ring_[:, i, :].rearrange("p (k n) -> p k n", k=KT) for i in range(2)]
        qT = qkv_[:, 0:2 * S].rearrange("p (a s) -> p a s", a=2)
        kT = qkv_[:, 2 * S:4 * S].rearrange("p (a s) -> p a s", a=2)
        V = qkv_[:, 4 * S:6 * S].rearrange("p (t n) -> p t n", t=NT)
        ikT = qkv_[:, 4 * S:5 * S]
        bm = qkv_[:, 6 * S:8 * S].rearrange("p (r s) -> p r s", r=2)
        iwT = qkv_[0:8, 6 * S:7 * S]
        xn = qkv_[:, 0:8 * S].rearrange("p (t n) -> p t n", t=NT)
        mrg = xn
        x1 = ring_[:, :, :].rearrange("p a (b s) -> p (a b) s", s=S)
        wo = oT_[:, :, :, :].rearrange("p a b s -> p (a b) s")
        expert_w = oT_[:, :, :, :].rearrange("p (c a) b s -> p c (a b s)", c=2)
        uhi = [isel_r[:, k * S:(k + 1) * S] if k < 4 else strips_r[:, (k - 1) * S:k * S] for k in range(KT)]
        graw = [ring_[:, 0, q * S:(q + 1) * S] for q in range(4)]
        glo, ghi = ([ring_r[:, i, q * S:(q + 1) * S] for q in range(4)] for i in range(2))
        vT = uT_
        stripAD = strips_[:, 0:4 * S].rearrange("p (h s) -> p h s", h=4)
        stripB = strips_[:, 4 * S:5 * S].rearrange("p (h s) -> p h s", h=4)
        stripC = [strips_[:, 5 * S:6 * S].rearrange("p (h s) -> p h s", h=4),
                  strips_[:, 6 * S:7 * S].rearrange("p (h s) -> p h s", h=4),
                  strips_[:, 7 * S:7 * S + 512].rearrange("p (h s) -> p h s", h=4)]
        rows = strips_[:, 0:6 * S].rearrange("p (r s) -> p r s", r=6)

        pb = [ctx.enter_context(nc.psum_tensor(f"pb{i}", [P, HALF], F32)) for i in range(2)]
        psS = [ctx.enter_context(nc.psum_tensor(f"psS{i}", [P, S], F32)) for i in range(2)]
        psT = ctx.enter_context(nc.psum_tensor("psT", [P, S], F32))

        XG, XT, YB = (qkv_[:, 2 * i * S:2 * (i + 1) * S].rearrange("p (r s) -> p r s", r=2) for i in range(3))
        SIG, HN, HT = (qkv_[:, 6 * S + i * HALF:6 * S + (i + 1) * HALF].rearrange("p (r s) -> p r s", r=2) for i in range(3))
        before, ones, iota_row = (SR[:, 3, i * P:(i + 1) * P] for i in range(3))
        token_id = SR[:, 3, 3 * P:3 * P + NT]
        onehots = SR[:, 0:2, :].rearrange("p r s -> p (r s)")
        block_hot = SR[:, 2, 0:2 * NT * NB].rearrange("p (c b) -> p c b", b=NB)
        route = strips_[:, 6 * S:6 * S + 11 * P].rearrange("p (r t e) -> p r t e", r=11, t=NT)
        small = strips_[:, 6 * S + 11 * P:6 * S + 12 * P]
        pair = [(psT[:, 0:HALF], psT[:, HALF:S]), (pb[0][:], pb[1][:])]

        const_in = sem("const_in")
        x_in = sem("x_in")
        piece_step, piece_summed = sem("piece_step"), sem("piece_summed")
        vecs_in, vecs_T, c_ready = sem("vecs_in"), sem("vecs_T"), sem("c_ready")
        w_landed = [sem("w_landed0"), sem("w_landed1")]
        ada_uT_in = [sem("ada_uT_in0"), sem("ada_uT_in1")]
        ada_used = sem("ada_used")
        ada_summed = sem("ada_summed")
        w_used = sem("w_used")
        cond_ready = sem("cond_ready")
        lam_ops = sem("lam_ops")
        lam_sum = sem("lam_sum")
        lam_exp = sem("lam_exp")
        mod_sum = sem("mod_sum")
        mod_ready = sem("mod_ready")
        out_ready, out_taken = sem("out_ready"), sem("out_taken")
        tab_ready, tab_taken, tab_out = sem("tab_ready"), sem("tab_taken"), sem("tab_out")
        stripD_in = sem("stripD_in")
        ada_in = [sem("ada_in0"), sem("ada_in1")]
        shifted_out = sem("shifted_out")
        strip_in, stripAD_in = sem("strip_in"), sem("stripAD_in")
        scores_ready, scores_taken = sem("scores_ready"), sem("scores_taken")
        relu_taken = sem("relu_taken")
        relu_used = sem("relu_used")
        biased = sem("biased")
        probs_ready = sem("probs_ready")
        diff_ready = sem("diff_ready")
        pT_ready, pT_copied = sem("pT_ready"), sem("pT_copied")
        sel_ready, bm_ready = sem("sel_ready"), sem("bm_ready")
        a_biased = sem("a_biased")
        sink_exp = sem("sink_exp")
        cols_ready = sem("cols_ready")
        norm_ready, norm_taken = sem("norm_ready"), sem("norm_taken")
        shift_ready, shift_exp = sem("shift_ready"), sem("shift_exp")
        sq_ready, ms_ready, rms_ready = sem("sq_ready"), sem("ms_ready"), sem("rms_ready")
        sum_done = sem("sum_done")
        gate_ready, proj_ready = sem("gate_ready"), sem("proj_ready")
        sig_ready, proj_taken = sem("sig_ready"), sem("proj_taken")
        wb_in, wb_used = [sem(f"wb_in{i}") for i in range(4)], sem("wb_used")
        w_hi, w_lo, u_hi, u_lo = (sem(n) for n in ("w_hi", "w_lo", "u_hi", "u_lo"))
        gcols_out, rows_in, rows2_in = sem("gcols_out"), sem("rows_in"), sem("rows2_in")
        wo_in, wo_last_in, router_in = sem("wo_in"), sem("wo_last_in"), sem("router_in")
        xr_in = [sem("xr_in0"), sem("xr_in1")]
        y_ready, y_taken, x1_ready = sem("y_ready"), sem("y_taken"), sem("x1_ready")
        var_ready, sd_ready = sem("var_ready"), sem("sd_ready")
        logitT_ready, logitT_taken = sem("logitT_ready"), sem("logitT_taken")
        logit_ready, logit_max, logit_exp = (sem(n) for n in ("logit_ready", "logit_max", "logit_exp"))
        moe_const_in = sem("moe_const_in")
        counts_in, ranks = sem("counts_in"), sem("ranks")
        hots_ready, slot_sum = sem("hots_ready"), sem("slot_sum")
        experts_ready = sem("experts_ready")
        slots_ready = sem("slots_ready")
        e_in = [sem("e_in0"), sem("e_in1")]
        down_in = [sem("down_in0"), sem("down_in1")]
        xg_in = [sem("xg_in0"), sem("xg_in1")]
        x1_out = sem("x1_out")
        xt_ready, xt_taken = sem("xt_ready"), sem("xt_taken")
        gu_ready, gsig_ready, h_ready = sem("gu_ready"), sem("gsig_ready"), sem("h_ready")
        ht_ready, ht_taken = sem("ht_ready"), sem("ht_taken")
        down_ready, yb_ready = sem("down_ready"), sem("yb_ready")
        yb_out = [sem("yb_out0"), sem("yb_out1")]
        pick_in = [sem(f"pick_in{i}") for i in range(4)]
        y_added = sem("y_added")
        first_weighed = sem("first_weighed")
        ln_var, ln_sd, ln_shift = sem("ln_var"), sem("ln_sd"), sem("ln_shift")
        normed, scaled = sem("normed"), sem("scaled")
        fin_ready = sem("fin_ready")
        out_done = [sem(f"out_done{i}") for i in range(4)]
        silu_ready, pool_step, gather_go = sem("silu_ready"), sem("pool_step"), sem("gather_go")
        phase = sem("phase")
        dve_step, act_step = sem("dve_step"), sem("act_step")

        w = t["w_in"][0]
        def ada(c):
            return [(t["w_ada"][0], HALF * c, HALF, 0)]

        chunks = [ada(0), ada(1)]
        chunks.append([(w, COL["i_q"], 256, 0)] + [(w, COL["i_k"], 32, 256 + 32 * r) for r in range(4)]
                      + [(w, COL["i_w"], 8, 384)])
        PROJ = {}
        WITH_ADA = ("C0", "C1", "C2", "A")

        def branch_chunks(name, q, k, v):
            PROJ[name] = len(chunks)
            chunks.append([(w, q, 256, 0)] + k)
            chunks.append([v])

        bk, dk = COL["b_k"], COL["d_k"]
        branch_chunks("B", COL["b_q"], [(w, bk, 64, 256), (w, bk, 64, 320), (w, bk + 64, 64, 384),
                                        (w, bk + 64, 64, 448)], (w, COL["b_v"], 128, 0))
        for g in range(3):
            branch_chunks(f"C{g}", COL["c_q"] + 256 * g, [(w, COL["c_k"] + 256 * g, 256, 256)],
                          (w, COL["c_v"] + 256 * g, 256, 0))
        branch_chunks("A", COL["a_q"], [(w, COL["a_k"], 256, 256)], (w, COL["a_v"], 256, 0))
        branch_chunks("D", COL["d_q"], [(w, dk, 64, 256), (w, dk, 64, 320)], (w, COL["d_v"], 64, 0))
        ORDER = ("B", "C0", "C1", "C2", "A", "D")
        VCOLS = {"A": 256, "B": 128, "C0": 256, "C1": 256, "C2": 256, "D": 64}
        KCOLS = {"A": 2, "B": 2, "C0": 2, "C1": 2, "C2": 2, "D": 1}
        BASE = {"B": 0, "C0": 32, "C1": 64, "C2": 96, "A": 128, "D": 192}
        N_IDX = 8 * (NT - 2)

        def units(name):
            for j in range(NT):
                for h in range(4):
                    if name in "AD":
                        yield h, j, 0, j + 1
                    elif name == "C1":
                        yield h, j, j - j % 2, j + 1
                    elif name == "C2":
                        yield h, j, j, j + 1
                    else:
                        yield h, j, max(0, j - 1), j + 1

        def score_place(name, a):
            return psS[a % 2][:] if name in "AD" else psS[a % 4 // 2][:, a % 2 * HALF:(a % 2 + 1) * HALF]

        def turned_place(name, i, b):
            return b if name in "AD" else i % 2

        def turned(name, i):
            u = ORDER.index(name) * 32 + i
            return PT[:, u % 2, :] if name in "AD" else PT[:, u % 2, u // 2 % 2 * HALF:(u // 2 % 2 + 1) * HALF]

        AHEAD = {name: 2 if name in "AD" else 4 for name in ORDER}
        EXP_AHEAD = {name: 2 if name in "AD" else 3 for name in ORDER}
        TURN_AHEAD = {name: 1 if name in "AD" else 2 for name in ORDER}
        PLACES = {name: 2 if name in "AD" else 4 for name in ORDER}

        def pt_banks(k0, k1):
            return -(-(k1 - k0) // 4)

        BANKS, _n = {}, 0
        for _name in ORDER:
            for _i, (_, _, _k0, _k1) in enumerate(units(_name)):
                _n += pt_banks(_k0, _k1)
                for _m in range(2 if _name == "A" else 1):
                    BANKS[BASE[_name] + (2 * _i + _m if _name == "A" else _i)] = _n

        def bias_strip(name, h, n):
            if name in "AD":
                return stripAD[:, h, S - n:S]
            if name == "B":
                return stripB[:, h, 256 - n:256]
            g = int(name[1])
            return stripC[g][:, h, 256 - n:256] if g < 2 else stripC[g][:, h, 0:P]

        def idx_tile(j):
            at = sum((i + 1) * P for i in range(2, j))
            return isel[:, at:at + (j + 1) * P]

        def tile_tokens(ap, name, j):
            if name == "C1":
                return ap.rearrange("p (a r) -> p r a", r=4)[:, j // 2, (j % 2) * P:(j % 2) * P + P]
            if name == "C2":
                return ap.rearrange("p (a r) -> p r a", r=8)[:, j, :]
            return ap[:, j * P:(j + 1) * P]

        def half_in_order(dst, src, name, hf):
            if name in ("C1", "C2"):
                r = 4 if name == "C1" else 8
                n = HALF // r
                return (dst.rearrange("p (r a) -> p r a", r=r)[:, :, hf * n:(hf + 1) * n],
                        src.rearrange("p (a r) -> p r a", r=r))
            return dst[:, hf * HALF:(hf + 1) * HALF], src

        def rows_to_tokens(dst, src, name, hf):
            if name in ("C1", "C2"):
                r = 4 if name == "C1" else 8
                return (dst.rearrange("p (a r) -> p r a", r=r)[:, hf * r // 2:(hf + 1) * r // 2, :],
                        src.rearrange("p (r a) -> p r a", r=r // 2))
            return dst[:, hf * HALF:(hf + 1) * HALF], src

        RAW = {"A": 0, "B": 1, "C0": 2, "C1": 0, "C2": 3, "D": 3}

        def stand(eng, n):
            eng.drain().then_inc(phase, 1)
            eng.wait_ge(phase, 5 * n)

        picks = qkv_[:, 0:4 * S].rearrange("p (r s) -> p r s", r=4)
        ln_cols = small[:, 80:80 + 32].rearrange("p (r n) -> p r n", r=4)
        picked = strips_[:, 6 * S + 7 * P:6 * S + 8 * P]
        earlier = PT[:, 1, 0:(NT + 1) * NE]
        topw, rank, blk, moved = (PT[:, 1, 2 * P + 2 * NT * i:2 * P + 2 * NT * (i + 1)] for i in range(4))
        blk_sum = PT[:, 1, 3 * P:3 * P + NB]
        blk_new = PT[:, 1, 3 * P + 32:3 * P + 32 + NB]
        blk_tmp = PT[:, 1, 3 * P + 64:3 * P + 64 + NB]
        blk_cmp = PT[:, 1, HALF:HALF + NB * NE].rearrange("p (b e) -> p b e", e=NE)

        logitT = PT[0:NE, 1, :]
        wbr = [PT[:, 0, q * 256:(q + 1) * 256].rearrange("p (k n) -> p k n", k=2) for q in range(4)]
        ada_uT = [uT_[:, 4 * i:4 * i + 4, :].rearrange("p a (b n) -> p (a b) n", n=HALF) for i in range(2)]
        ada_acc = oT_[:, 0, :, :].rearrange("p a s -> p (a s)")
        ada_w = [PT[:, i, :].rearrange("p (k n) -> p k n", n=P) for i in range(2)]

        onehot = SR[0:32, :, :].rearrange("p r s -> p (r s)")[:, 0:TAB_W]
        relt = PT[0:32, 0, 0:24]
        bcols = SR[:, 0:2, :].rearrange("p r (c n) -> p (r c n)", n=64)
        fac = [SR[0:4, g, :] for g in range(3)]
        fmax = SR[0:4, 3, :]
        fden = [strips_[0:4, (4 + g) * S:(5 + g) * S] for g in range(3)]
        N_CONST = 12
        vecs = PT[0:56, 1, HALF:HALF + P]

        down_all = isel[:, 0:4 * S].rearrange("p (r n) -> p r n", r=2)

        def refill(b):
            return not isinstance(b, int) or b >= 2

        def blocks(eng, step_of):
            step_of(0, 0, 0)
            step_of(1, 1, 1)
            step_of(2, 0, 2)
            step_of(3, 1, 3)
            with eng.Fori(2, NB // 2) as i:
                step_of(i * 2, 0, 2)
                step_of(i * 2 + 1, 1, 3)
            step_of(NB - 1, 0, NB - 1)

        OUTS = {"A": 16 + 6 + 3 + 32 + 5 * (8 + NT + 32)}
        ADA_AT = {name: 16 + 6 + 3 + 8 * i + (i + 1) * (8 + NT + 32) for i, name in enumerate(WITH_ADA)}

        def strip(eng, dst, name, h, s):
            width = {x[0]: x[2] for x in TABLES}[name]
            c0 = TAB_OFF[name] + P - 1
            src = scratch["shifted"][h, 0:P * (TAB_W + P)].rearrange("(p n) -> p n", p=P)[:, c0:c0 + width]
            eng.dma_start(dst, src).then_inc(s, 16)

        block = ctx.enter_context(nc.Block())

        @block.sync
        def _(sp):
            def chunk(n):
                if 2 <= n < 4:
                    sp.wait_ge(ada_used, n - 1)
                elif n >= 4:
                    sp.wait_ge(w_used, n - 3)
                for src, c0, wd, at in chunks[n]:
                    sp.dma_start(ring[n % 2][:, :, at:at + wd],
                                 src[:, c0:c0 + wd].rearrange("(k p) n -> p k n", p=P)).then_inc(w_landed[n % 2], 16)

            sp.dma_start(vecs[0:48, :], t["b_ada"][0].rearrange("(k p) -> k p", p=P)).then_inc(vecs_in, 16)
            sp.dma_start(vecs[48:56, :], t["c"][0].rearrange("(k p) -> k p", p=P)).then_inc(vecs_in, 16)
            sp.dma_start(ident[:], t["ident"]).then_inc(vecs_in, 16)
            chunk(0)
            chunk(1)
            for i in range(2):
                sp.dma_start(ada_uT[i], ada(2 + i)[0][0][:, (2 + i) * HALF:(3 + i) * HALF]
                             .rearrange("(k p) n -> p k n", p=P)).then_inc(ada_uT_in[i], 16)
            chunk(2)
            chunk(3)
            sp.wait_ge(tab_taken, N_TAB)
            sp.dma_start(scratch["gtab"], isel[0:4, 0:TAB_W]).then_inc(tab_out, 16)
            sp.wait_ge(tab_out, 16)
            for h in range(4):
                sp.dma_start(scratch["shifted"][h, 0:P * (TAB_W + P + 1)].rearrange("(p n) -> p n", p=P)[:, 0:TAB_W],
                             scratch["gtab"][h:h + 1, :].broadcast_to([P, TAB_W])).then_inc(shifted_out, 16)
            sp.wait_ge(shifted_out, 64)

            for h in range(4):
                strip(sp, stripB[:, h, :], "B", h, strip_in)
                for g in range(3):
                    strip(sp, stripC[g][:, h, :], f"C{g}", h, strip_in)
                strip(sp, stripAD[:, h, :], "A", h, stripAD_in)
            for n in range(4, PROJ["C0"] + 2):
                chunk(n)
            for i, name in enumerate(WITH_ADA):
                for m in range(8):
                    sp.wait_ge(out_ready, ADA_AT[name] + max(0, 2 * m - 2))
                    c0 = 2 * D + (8 * i + m) * P
                    sp.dma_start(ada_w[m % 2], t["w_ada"][0][:, c0:c0 + P].rearrange("(k p) n -> p k n", p=P)
                                 ).then_inc(ada_in[m % 2], 16)
                for n in range(PROJ[name] + 2, PROJ[name] + 4):
                    chunk(n)

            def gate_weights(n):
                b, d = n // KT, n % KT
                c0 = COL["gate"] + b * D + d * P
                sp.dma_start(graw[n % 4].rearrange("p (k n) -> p k n", k=KT),
                             w[:, c0:c0 + P].rearrange("(k p) n -> p k n", p=P)).then_inc(wb_in[n % 4], 16)

            def branch_weights(n):
                b, d = n // KT, n % KT
                sp.dma_start(wbr[n % 4], t["w_branch"][0, b, :, d * P:(d + 1) * P].rearrange("(k p) n -> p k n", p=P)
                             ).then_inc(wb_in[n % 4], 16)

            def out_weights(i, s):
                sp.dma_start(wo[:, 2 * i:2 * i + 2, :], t["w_out"][0][256 * i:256 * (i + 1), :]
                             .rearrange("(k p) n -> p k n", p=P)).then_inc(s, 16)

            sp.wait_ge(w_used, len(chunks) - 2)
            for n in range(4):
                gate_weights(n)
            stand(sp, 1)
            for n in range(4):
                branch_weights(n)
            sp.wait_ge(gcols_out, 32)
            row_sources = (scratch["gates"][0:1, :], t["ln1_g"], t["ln1_b"], scratch["gates"][1:2, :], t["ln2_g"], t["ln2_b"])
            for r in range(3):
                sp.dma_start(rows[:, r, :], row_sources[r].broadcast_to([P, D])).then_inc(rows_in, 16)
            for n in range(4, 4 * KT):
                sp.wait_ge(wb_used, n - 3)
                gate_weights(n)
                branch_weights(n)
                if n % KT == 3:
                    out_weights(n // KT - 1, wo_in)
            sp.wait_ge(wb_used, 4 * KT)
            out_weights(3, wo_last_in)
            stand(sp, 2)
            for dst, name in ((before, "before"), (ones, "ones"), (iota_row, "iota_row"), (token_id, "token_id")):
                sp.dma_start(dst, t[name]).then_inc(moe_const_in, 16)
            for j in range(NT):
                if j >= 2:
                    sp.wait_ge(x1_ready, j - 1)
                    sp.dma_start(scratch["x1"][(j - 2) * P:(j - 1) * P, :], x1[:, j - 2, :]).then_inc(x1_out, 16)
                sp.dma_start(SR[:, j % 2, :], t["x"][0, j * P:(j + 1) * P, :]).then_inc(xr_in[j % 2], 16)
            sp.dma_start(PT[:, 0, 0:P].rearrange("p (k e) -> p k e", k=KT),
                         t["w_router"].rearrange("(k p) e -> p k e", p=P)).then_inc(router_in, 16)
            sp.dma_start(PT[:, 0, P:P + NE], t["b_router"].rearrange("(a n) -> a n", a=1).broadcast_to([P, NE])
                         ).then_inc(router_in, 16)
            for r in range(3, 6):
                sp.dma_start(rows[:, r, :], row_sources[r].broadcast_to([P, D])).then_inc(rows2_in, 16)
            for j in (NT - 2, NT - 1):
                sp.wait_ge(x1_ready, j + 1)
                sp.dma_start(scratch["x1"][j * P:(j + 1) * P, :], x1[:, j, :]).then_inc(x1_out, 16)
            stand(sp, 3)
            sp.wait_ge(experts_ready, 1)

            def load_weights(b, r, least):
                at = bass.ds(b, 1)
                new = 1 if isinstance(b, int) and b == 0 else sp.value_load(block_new[0:1, at], min_val=0, max_val=1)
                e = sp.value_load(block_expert[0:1, at], min_val=0, max_val=NE - 1)
                slot = sp.value_load(block_slot[0:1, at], min_val=0, max_val=1)
                if refill(b):
                    sp.wait_ge(gu_ready, b - 1)
                for c0, name in ((0, "w_exp_gate"), (FF, "w_exp_up")):
                    sp.dma_start(expert_w[:, bass.ds(slot, 1), :].rearrange("p a (k n) -> p (a k) n", k=KT)[:, :, c0:c0 + FF],
                                 t[name][0, bass.ds(e, 1), :, :].rearrange("e (k p) n -> p (e k) n", p=P),
                                 cond=new).then_inc(e_in[r], 16)
                if refill(b):
                    sp.wait_ge(down_ready, b - 1)
                sp.dma_start(down_all[:, bass.ds(slot, 1), :].rearrange("p a (k n) -> p (a k) n", k=2),
                             t["w_exp_down"][0, bass.ds(e, 1), :, :].rearrange("e (k p) n -> p (e k) n", p=P),
                             cond=new).then_inc(down_in[r], 16)

            blocks(sp, load_weights)
            for j in range(NT):
                sp.wait_ge(fin_ready, j + 1)
                sp.dma_start(out[0, j * P:(j + 1) * P, :], SR[:, j % 4, :]).then_inc(out_done[j % 4], 16)
            for o in out_done:
                sp.wait_ge(o, 16 * NT // 4)

        @block.tensor
        def _(pe):
            mm = nc.tensor.matmul
            n_out = 0
            n_norm = 0
            s = 0
            n_pt = 0
            n_diff = 0
            n_ada = 0
            last_pt = {0: 0, 1: 0}

            def landed(n):
                pe.wait_ge(w_landed[n % 2], 16 * sum(len(chunks[i]) for i in range(n % 2, n + 1, 2)))

            def bank():
                if n_out >= 2:
                    pe.wait_ge(out_taken, n_out - 1)
                return pb[n_out % 2]

            def norm_bank():
                if n_norm >= 2:
                    pe.wait_ge(norm_taken, n_norm - 1)
                return psT[:, (n_norm % 2) * HALF:(n_norm % 2 + 1) * HALF]

            pe.wait_ge(vecs_in, 48)
            nc.tensor.transpose(psT[:, 0:56], vecs, ident[0:56, 0:56]).then_inc(vecs_T, 1)
            for m in range(2 * KT):
                if m % 4 == 0:
                    pe.wait_ge(ada_summed, m // 4 + 1)
                last = mm(psT[:, m:m + 1], ada_acc[:, m * P:(m + 1) * P], ones_col[:], start=True, stop=True)
            last.then_inc(mod_sum, 1)
            pe.wait_ge(x_in, 16 * NT)
            for k in range(KT):
                for hf in range(2):
                    o = bank()
                    for q in range(4):
                        last = nc.tensor.transpose(o[:, q * P:(q + 1) * P], xn[:, 4 * hf + q, k * P:(k + 1) * P], ident[:])
                    last.then_inc(out_ready, 1)
                    n_out += 1
            pe.wait_ge(out_taken, n_out)

            def project_T(n, cols, with_ada=False, between=(), steps=1):
                nonlocal n_out, n_ada
                for c in range(cols):
                    for hf in range(2):
                        o = bank()
                        for k in range(KT):
                            last = mm(o[:], ring[n % 2][:, k, c * P:(c + 1) * P], uT[:, k, hf * HALF:(hf + 1) * HALF],
                                      start=(k == 0), stop=(k == KT - 1))
                        last.then_inc(out_ready, 1)
                        n_out += 1
                        for _ in islice(between, steps):
                            pass
                        if with_ada:
                            i = n_ada % 2
                            pe.wait_ge(piece_summed, n_ada + 1)
                            mm(bank()[:, 0:1], ada_w[i][:, 0, :], ones_col[:], start=True, stop=True).then_inc(out_ready, 1)
                            n_out += 1
                            n_ada += 1

            def project_V(n, name, cols, at=0, between=()):
                nonlocal n_out
                for j in range(NT):
                    o = bank()
                    for k in range(KT):
                        last = mm(o[:, 0:cols], tile_tokens(uT[:, k, :], name, j), ring[n % 2][:, k, at:at + cols],
                                  start=(k == 0), stop=(k == KT - 1))
                    last.then_inc(out_ready, 1)
                    n_out += 1
                    for _ in islice(between, 2):
                        pass

            def tables():
                n = 0
                for name, h0, width, *_ in TABLES:
                    for c in range(0, width + P, HALF):
                        wd = min(HALF, width + P - c)
                        if n >= 2:
                            pe.wait_ge(tab_taken, n - 1)
                        at = TAB_OFF[name] + c
                        mm(psS[n % 2][0:4, 0:wd], PT[0:32, 0, h0:h0 + 4], onehot[:, at:at + wd],
                           start=True, stop=True).then_inc(tab_ready, 1)
                        n += 1
                        yield

            landed(2)
            pe.wait_ge(const_in, 16 * N_CONST)
            pe.wait_ge(lam_ops, 1)
            mm(psT[:, HALF:HALF + 2], PT[0:32, 1, 0:P], PT[0:32, 1, P:P + 2], start=True, stop=True).then_inc(lam_sum, 1)
            tab = tables()
            project_T(2, 3, between=tab, steps=2)
            for _ in tab:
                pass
            for hf in range(2):
                o = bank()
                for k in range(KT):
                    last = mm(o[0:8, :], ring[0][:, k, 384:392], uT[:, k, hf * HALF:(hf + 1) * HALF],
                              start=(k == 0), stop=(k == KT - 1))
                last.then_inc(out_ready, 1)
                n_out += 1
            pe.drain().then_inc(w_used, 1)
            pe.wait_ge(out_taken, n_out)
            o = bank()
            for j in range(NT):
                last = nc.tensor.transpose(o[:, 8 * j:8 * j + 8], iwT[:, j * P:(j + 1) * P], ident[0:8, 0:8])
            last.then_inc(out_ready, 1)
            n_out += 1
            pe.wait_ge(tab_taken, N_TAB)
            for j in range(2, NT):
                for h in range(8):
                    if s >= 2:
                        pe.wait_ge(relu_taken, s - 1)
                    r = 32 * (h % 4)
                    for c in range(0, (j + 1) * P, HALF):
                        wd = min(HALF, (j + 1) * P - c)
                        last = mm(psS[s % 2][:, c:c + wd], qT[r:r + 32, h // 4, j * P:(j + 1) * P],
                                  ikT[r:r + 32, c:c + wd], start=True, stop=True)
                    last.then_inc(scores_ready, 1)
                    s += 1
            pe.wait_ge(relu_taken, s)

            def norm_B_or_D(order):
                nonlocal n_norm
                pe.wait_ge(cols_ready, order)
                for pr in range(2):
                    for hf in range(2):
                        o = norm_bank()
                        for q in range(4):
                            c0 = (4 * (4 * hf + q) + 2 * pr) * 64
                            last = nc.tensor.transpose(o[:, q * P:(q + 1) * P], bcols[:, c0:c0 + P], ident[:])
                        last.then_inc(norm_ready, 1)
                        n_norm += 1
                        yield

            def norm_A():
                nonlocal n_norm
                for i in range(4):
                    pe.wait_ge(sq_ready, i + 1)
                    mm(norm_bank(), bones[:], bm[:, i % 2, 0:HALF], start=True, stop=True).then_inc(norm_ready, 1)
                    n_norm += 1
                    yield

            def combine_C():
                nonlocal n_norm
                for g in range(3):
                    for stat in (mx, den):
                        for hf in range(2):
                            o = norm_bank()
                            for q in range(4):
                                c0 = BASE[f"C{g}"] + 4 * (4 * hf + q)
                                last = nc.tensor.transpose(o[0:4, q * P:(q + 1) * P], stat[:, c0:c0 + 4], ident[:])
                            last.then_inc(norm_ready, 1)
                            n_norm += 1
                            yield
                for _ in range(6):
                    yield
                pe.wait_ge(cols_ready, 2)
                for g in range(3):
                    for pr in range(2):
                        for hf in range(2):
                            mm(norm_bank(), hsel[:, pr, :], fac[g][:, hf * HALF:(hf + 1) * HALF],
                               start=True, stop=True).then_inc(norm_ready, 1)
                            n_norm += 1
                            yield

            pending = iter(())
            for name in ORDER:
                n = PROJ[name]
                landed(n)
                project_T(n, 2 + KCOLS[name], name in WITH_ADA, between=pending, steps={"C0": 4, "A": 3}.get(name, 1))
                pe.drain().then_inc(w_used, 1)
                landed(n + 1)
                project_V(n + 1, name, VCOLS[name], between=pending)
                for _ in pending:
                    pass
                pe.drain().then_inc(w_used, 1)
                pe.wait_ge(out_taken, n_out)
                todo = list(units(name))

                def score(i):
                    nonlocal s
                    h, j, k0, k1 = todo[i]
                    for m in range(2 if name == "A" else 1):
                        a = s - N_IDX
                        if a >= PLACES[name]:
                            pe.wait_ge(scores_taken, a - PLACES[name] + 1)
                        r, K = ((h % 2) * 64 + 32 * m, 32) if name == "A" else ((h % 2) * 64, 64)
                        keys = kT[:, 0 if name == "D" else h // 2, :]
                        for c in range(k0 * P, k1 * P, HALF):
                            wd = min(HALF, k1 * P - c)
                            last = mm(score_place(name, a)[:, c - k0 * P:c - k0 * P + wd],
                                      qT[r:r + K, h // 2, j * P:(j + 1) * P], keys[r:r + K, c:c + wd],
                                      start=True, stop=True)
                        last.then_inc(scores_ready, 1)
                        s += 1

                def transpose_probs(i):
                    nonlocal n_pt, n_diff
                    h, j, k0, k1 = todo[i]
                    if name == "A":
                        n_diff += 1
                        pe.wait_ge(diff_ready, n_diff)
                        slot = (BASE["A"] + 2 * i) % 4
                    else:
                        pe.wait_ge(probs_ready, BASE[name] + i + 1)
                        slot = (BASE[name] + i) % 4
                    for b, c in enumerate(range(k0, k1, 4)):
                        at = turned_place(name, i, b)
                        if last_pt[at]:
                            pe.wait_ge(pT_copied, last_pt[at])
                        for q in range(c, min(c + 4, k1)):
                            last = nc.tensor.transpose(psT[:, at * HALF + (q - c) * P:at * HALF + (q - c + 1) * P],
                                                       SR[:, slot, (q - k0) * P:(q - k0 + 1) * P], ident[:])
                        last.then_inc(pT_ready, 1)
                        n_pt += 1
                        last_pt[at] = n_pt

                def weigh_values(i):
                    nonlocal n_out
                    h, j, k0, k1 = todo[i]
                    u = ORDER.index(name) * 32 + i
                    pe.wait_ge(pT_copied, BANKS[BASE[name] + (2 * i if name == "A" else i)])
                    o = bank()
                    vh = {"B": h // 2, "D": 0}.get(name, h)
                    for q in range(k0, k1):
                        last = mm(o[0:64, 0:P], V[:, q, vh * HD:(vh + 1) * HD],
                                  turned(name, i)[:, (q - k0) * P:(q - k0 + 1) * P], start=(q == k0), stop=(q == k1 - 1))
                    last.then_inc(out_ready, 1)
                    n_out += 1

                for i in range(-AHEAD[name], len(todo)):
                    if i + AHEAD[name] < len(todo):
                        score(i + AHEAD[name])
                    if i >= 0:
                        weigh_values(i)
                    if 0 <= i + TURN_AHEAD[name] < len(todo):
                        transpose_probs(i + TURN_AHEAD[name])
                pe.wait_ge(pT_copied, n_pt)
                pe.wait_ge(out_taken, n_out)
                if name == "B":
                    pending = norm_B_or_D(1)
                if name == "A":
                    pending = norm_A()
                if name == "D":
                    for _ in norm_B_or_D(3):
                        pass
                if name == "C2":
                    pending = combine_C()
                if name == "D":
                    pe.wait_ge(norm_taken, n_norm)
            stand(pe, 1)

            for n in range(4 * KT):
                b = n // KT
                pe.wait_ge(wb_in[n % 4], 32 * (n // 4 + 1))
                pe.wait_ge(w_lo, n + 1)
                if n >= 2:
                    pe.wait_ge(sig_ready, n - 1)
                for k in range(KT):
                    if n == 0:
                        pe.wait_ge(u_lo, k + 1)
                    whi, wlo = (x[n % 4][:, k * P:(k + 1) * P] for x in (ghi, glo))
                    for hf in range(2):
                        o = psS[n % 2][:, hf * HALF:(hf + 1) * HALF]
                        cols = slice(hf * HALF, (hf + 1) * HALF)
                        hi, lo = uhi[k][:, cols], uT_r[:, k, cols]
                        mm(o, whi, hi, start=(k == 0), stop=False)
                        mm(o, whi, lo, start=False, stop=False)
                        last = mm(o, wlo, hi, start=False, stop=(k == KT - 1))
                last.then_inc(gate_ready, 1)
                if n >= 2:
                    pe.wait_ge(proj_taken, n - 1)
                for hf in range(2):
                    for k in range(2):
                        last = mm(pair[n % 2][hf], wbr[n % 4][:, k, :],
                                  oT[:, b, k, hf * HALF:(hf + 1) * HALF], start=(k == 0), stop=(k == 1))
                last.then_inc(proj_ready, 1)
                pe.drain().then_inc(wb_used, 1)
            stand(pe, 2)

            pe.wait_ge(wo_in, 48)

            def to_vT(j):
                nonlocal n_out
                pe.wait_ge(x1_ready, j + 1)
                for hf in range(2):
                    o = bank()
                    for q in range(4):
                        k = 4 * hf + q
                        last = nc.tensor.transpose(o[:, q * P:(q + 1) * P], x1[:, j, k * P:(k + 1) * P], ident[:])
                    last.then_inc(out_ready, 1)
                    n_out += 1

            n_before = n_out

            def router(j0, j1):
                if j0 == 0:
                    pe.wait_ge(router_in, 32)
                pe.wait_ge(out_taken, n_before + 2 * j1)
                for k in range(KT):
                    last = mm(psT[0:NE, j0 * P:j1 * P], PT[:, 0, k * NE:(k + 1) * NE], vT[:, k, j0 * P:j1 * P],
                              start=(k == 0), stop=(k == KT - 1))
                last.then_inc(logitT_ready, 1)

            for j in range(NT):
                if j >= 2:
                    pe.wait_ge(y_taken, j - 1)
                for k in range(KT):
                    if j == 0 and k == 6:
                        pe.wait_ge(wo_last_in, 16)
                    for hf in range(2):
                        last = mm(psS[j % 2][:, hf * HALF:(hf + 1) * HALF], mrg[:, k, j * P:(j + 1) * P],
                                  wo[:, k, hf * HALF:(hf + 1) * HALF], start=(k == 0), stop=(k == KT - 1))
                last.then_inc(y_ready, 1)
                if j >= 2:
                    to_vT(j - 2)
                if j == NT - 2:
                    router(0, 4)
            to_vT(NT - 2)
            router(4, 6)
            to_vT(NT - 1)
            pe.wait_ge(logitT_taken, 2)
            router(6, 8)
            stand(pe, 3)
            pe.wait_ge(logitT_taken, 3)
            for j in range(NT):
                last = nc.tensor.transpose(pb[0][:, j * NE:(j + 1) * NE], logitT[:, j * P:(j + 1) * P], ident[0:NE, 0:NE])
            last.then_inc(logit_ready, 1)
            pe.wait_ge(moe_const_in, 64)
            pe.wait_ge(counts_in, 1)
            mm(pb[0][:, 0:P], before, picked, start=True, stop=False)
            mm(pb[0][:, 0:P], ones, earlier[:, 0:P], start=False, stop=True)
            mm(pb[0][:, P:P + NE], ones, earlier[:, P:P + NE], start=True, stop=True).then_inc(ranks, 1)
            for c in range(2 * NT):
                pe.wait_ge(hots_ready, c + 1)
                last = mm(pb[1][:, 0:NB], onehots[:, c * P:(c + 1) * P], block_hot[:, c, :],
                          start=(c == 0), stop=(c == 2 * NT - 1))
            last.then_inc(slot_sum, 1)
            pe.wait_ge(slots_ready, 1)

            def rows_T(b, r, least):
                pe.wait_ge(xg_in[r], (b // 2 + 1) * 16 if isinstance(b, int) else b * 8 + (16 - 8 * r))
                if refill(b + 1):
                    pe.wait_ge(xt_taken, b)
                for k in range(KT):
                    last = nc.tensor.transpose(psT[:, k * P:(k + 1) * P], XG[:, r, k * P:(k + 1) * P], ident[:])
                last.then_inc(xt_ready, 1)

            def pe_slot(b):
                return bass.ds(pe.value_load(block_slot[0:1, bass.ds(b, 1)], min_val=0, max_val=1), 1)

            def gate_up(b, r, slot):
                pe.wait_ge(e_in[r], (b // 2 + 1) * 32 if isinstance(b, int) else b * 16 + (32 - 16 * r))
                pe.wait_ge(xt_taken, b + 1)
                if refill(b):
                    pe.wait_ge(ht_taken, b - 1)
                for k in range(KT):
                    last = mm(pb[r][:], XT[:, r, k * P:(k + 1) * P], expert_w[:, slot, k * HALF:(k + 1) * HALF],
                              start=(k == 0), stop=(k == KT - 1))
                last.then_inc(gu_ready, 1)

            def hidden_T(b, r):
                pe.wait_ge(h_ready, b + 1)
                for f in range(2):
                    last = nc.tensor.transpose(pb[r][:, f * P:(f + 1) * P], HN[:, r, f * P:(f + 1) * P], ident[:])
                last.then_inc(ht_ready, 1)

            def down(b, r, slot):
                pe.wait_ge(down_in[r], (b // 2 + 1) * 16 if isinstance(b, int) else b * 8 + (16 - 8 * r))
                pe.wait_ge(ht_taken, b + 1)
                if refill(b):
                    pe.wait_ge(yb_ready, b - 1)
                for c in range(2):
                    for f in range(2):
                        last = mm(psS[r][:, c * HALF:(c + 1) * HALF], HT[:, r, f * P:(f + 1) * P],
                                  down_all[:, slot, f * S + c * HALF:f * S + (c + 1) * HALF], start=(f == 0), stop=(f == 1))
                last.then_inc(down_ready, 1)

            def pe_block(b, r, least):
                slot = pe_slot(b)
                slot_before = pe_slot(b - 1) if least >= 1 else None
                if least < NB - 1:
                    rows_T(b + 1, 1 - r, least + 1)
                gate_up(b, r, slot)
                if least >= 1:
                    down(b - 1, 1 - r, slot_before)
                hidden_T(b, r)

            rows_T(0, 0, 0)
            blocks(pe, pe_block)
            down(NB - 1, 0, pe_slot(NB - 1))

        @block.scalar
        def _(act):
            fn = nc.scalar.activation
            n_out = n_pt = 0

            def take(dst, src, scale=1.0, bias=None):
                nonlocal n_out
                act.wait_ge(out_ready, n_out + 1)
                if bias is None:
                    ins = fn(dst, src, ACT.Copy, scale=scale)
                else:
                    ins = fn(dst, src, ACT.Identity, scale=scale, bias=bias)
                ins.then_inc(out_taken, 1)
                n_out += 1

            def nxt():
                return pb[n_out % 2]

            for a, b in ((lamq[:, 0, :], t["a_lambda_q"][0].rearrange("m d -> d m")),
                         (lamq[:, 1, :], t["a_lambda_k"][0].rearrange("m d -> d m")),
                         (onehot, t["onehot"]), (relt, t["rel_table"]), (isel[0:4, 0:TAB_W], t["tabmask"]),
                         (causal[:], t["causal"]), (bones[:], t["blockones"]),
                         (hsel[:], t["headsel"].rearrange("h (a p) -> h a p", a=2)), (iota[:], t["iota"]),
                         (subg[0:64, :], t["a_subln_g"][0].rearrange("(d a) -> d a", a=1)),
                         (subg[64:128, :], t["a_subln_g"][0].rearrange("(d a) -> d a", a=1)),
                         (sink[:], t["b_sinks"][0:1, :].broadcast_to([P, 4]))):
                act.dma_start(a, b, allow_slow_non_contiguous=True).then_inc(const_in, 16)
            for j in range(NT):
                act.dma_start(xn[:, j, :], t["x"][0, j * P:(j + 1) * P, :]).then_inc(x_in, 16)
            act.wait_ge(c_ready, 1)
            fn(cT[:, 1, :], cT[:, 0, :], ACT.Exp, scale=-1.0).then_inc(act_step, 1)
            act.wait_ge(mod_ready, 1)
            for k in range(KT):
                for hf in range(2):
                    take(uT[:, k, hf * HALF:(hf + 1) * HALF], nxt()[:], scale=modT[:, 8 + k:9 + k], bias=modT[:, k:k + 1])
            act.wait_ge(lam_sum, 1)
            fn(lam[:, 0:2], psT[:, HALF:HALF + 2], ACT.Exp).then_inc(lam_exp, 1)
            for c in range(3):
                for hf in range(2):
                    dst = qT[:, c, :] if c < 2 else ikT
                    take(dst[:, hf * HALF:(hf + 1) * HALF], nxt()[:])
            for hf in range(2):
                take(iwT[:, hf * HALF:(hf + 1) * HALF], nxt()[0:8, :])
            take(iw[:, :, :].rearrange("p t h -> p (t h)"), nxt()[:, 0:8 * NT])
            s = 0
            for j in range(2, NT):
                for h in range(8):
                    act.wait_ge(scores_ready, s + 1)
                    if s >= 4:
                        act.wait_ge(relu_used, s - 3)
                    fn(SR[:, s % 4, 0:(j + 1) * P], psS[s % 2][:, 0:(j + 1) * P], ACT.Relu).then_inc(relu_taken, 1)
                    s += 1

            for name in ORDER:
                scale = (32 if name == "A" else 64) ** -0.5
                for c in range(2 + KCOLS[name]):
                    for hf in range(2):
                        dst, src = half_in_order(qT[:, c, :] if c < 2 else kT[:, c - 2, :], nxt()[:], name, hf)
                        take(dst, src, scale=scale if c < 2 else 1.0)
                        i = 2 * c + hf
                        if name == "A" and i == 4:
                            for g in range(3):
                                act.wait_ge(shift_ready, g + 1)
                                fn(fac[g], fac[g], ACT.Exp).then_inc(shift_exp, 1)
                        if name == "D" and i < 4:
                            act.wait_ge(ms_ready, i + 1)
                            fn(bm[:, i % 2, 0:HALF], bm[:, i % 2, 0:HALF], ACT.Sqrt, bias=epsc[:]).then_inc(rms_ready, 1)
                        if name in WITH_ADA:
                            c0 = 16 + 8 * WITH_ADA.index(name) + 2 * c + hf
                            take(modT[:, c0:c0 + 1], nxt()[:, 0:1])
                for j in range(NT):
                    take(V[:, j, 0:VCOLS[name]], nxt()[:, 0:VCOLS[name]])
                todo = list(units(name))

                def exps(i):
                    h, j, k0, k1 = todo[i]
                    n = (k1 - k0) * P
                    for m in range(2 if name == "A" else 1):
                        a = BASE[name] + (2 * i + m if name == "A" else i)
                        act.wait_ge(biased, a + 1)
                        fn(SR[:, a % 4, 0:n], SR[:, a % 4, 0:n], ACT.Exp, bias=negm[:, a:a + 1],
                           accum_out=den[:, a:a + 1]).then_inc(probs_ready, 1)

                def copy_probs(i):
                    nonlocal n_pt
                    h, j, k0, k1 = todo[i]
                    u = ORDER.index(name) * 32 + i
                    if u >= 2 and i < 2:
                        pass
                    elif i >= 2:
                        act.wait_ge(out_ready, n_out)
                    for b, c in enumerate(range(k0, k1, 4)):
                        wd = (min(c + 4, k1) - c) * P
                        act.wait_ge(pT_ready, n_pt + 1)
                        at = turned_place(name, i, b) * HALF
                        fn(turned(name, i)[:, b * HALF:b * HALF + wd], psT[:, at:at + wd], ACT.Copy).then_inc(pT_copied, 1)
                        n_pt += 1

                def take_output(i):
                    h, j, k0, k1 = todo[i]
                    dst = tile_tokens(oT[:, RAW[name], h // 2, :], name, j)
                    take(dst[(h % 2) * 64:(h % 2) * 64 + 64], nxt()[0:64, 0:P])

                for i in range(-EXP_AHEAD[name], len(todo)):
                    if i + EXP_AHEAD[name] < len(todo):
                        exps(i + EXP_AHEAD[name])
                    if 0 <= i + TURN_AHEAD[name] < len(todo):
                        copy_probs(i + TURN_AHEAD[name])
                    if i >= 0:
                        take_output(i)
                if name == "B":
                    for h in range(4):
                        ins = fn(rec[:, h:32:4], negm[:, h:32:4], ACT.Exp, bias=sink[:, h:h + 1])
                    ins.then_inc(sink_exp, 1)
            act.wait_ge(mod_ready, 2)
            for r, c0 in ((0, 16), (1, 40)):
                act.dma_start(scratch["gates"][r].rearrange("(k p) -> p k", p=P), modT[:, c0:c0 + 8],
                              allow_slow_non_contiguous=True).then_inc(gcols_out, 16)
            stand(act, 1)

            def leading_weights(n):
                act.wait_ge(wb_in[n % 4], 32 * (n // 4 + 1))
                fn(ghi[n % 4], graw[n % 4], ACT.Copy).then_inc(w_hi, 1)

            for k in range(KT):
                if k == 2:
                    leading_weights(0)
                fn(uhi[k], uT[:, k, :], ACT.Copy).then_inc(u_hi, 1)
            leading_weights(1)
            for n in range(4 * KT):
                if n + 2 < 4 * KT:
                    leading_weights(n + 2)
                act.wait_ge(gate_ready, n + 1)
                if n >= 4:
                    act.wait_ge(proj_taken, n - 3)
                fn(SR[:, n % 4, :], psS[n % 2][:], ACT.Sigmoid).then_inc(sig_ready, 1)
            stand(act, 2)

            def take_vT(j):
                nonlocal n_out
                for hf in range(2):
                    act.wait_ge(out_ready, n_out + 1)
                    for q in range(4):
                        k = 4 * hf + q
                        ins = fn(vT[:, k, j * P:(j + 1) * P], pb[n_out % 2][:, q * P:(q + 1) * P], ACT.Identity,
                                 scale=modT[:, 32 + k:33 + k], bias=modT[:, 24 + k:25 + k])
                    ins.then_inc(out_taken, 1)
                    n_out += 1

            def take_logits(i, j0, j1):
                act.wait_ge(logitT_ready, i + 1)
                fn(logitT[:, j0 * P:j1 * P], psT[0:NE, j0 * P:j1 * P], ACT.Copy).then_inc(logitT_taken, 1)

            for j in range(NT):
                act.wait_ge(var_ready, j + 1)
                fn(sd[:, 0:1], mv[:, 0, 1:2], ACT.Sqrt, bias=epsc[:]).then_inc(sd_ready, 1)
                if j >= 2:
                    take_vT(j - 2)
            take_vT(NT - 2)
            take_logits(0, 0, 4)
            take_vT(NT - 1)
            take_logits(1, 4, 6)
            take_logits(2, 6, 8)
            stand(act, 3)

            act.wait_ge(logit_max, 1)
            fn(route[:, 0], route[:, 0], ACT.Exp).then_inc(logit_exp, 1)

            def take_rows(b, r, least):
                act.wait_ge(xt_ready, b + 1)
                if refill(b):
                    act.wait_ge(gu_ready, b - 1)
                for k in range(KT):
                    ins = fn(XT[:, r, k * P:(k + 1) * P], psT[:, k * P:(k + 1) * P], ACT.Identity,
                             scale=modT[:, 32 + k:33 + k], bias=modT[:, 24 + k:25 + k])
                ins.then_inc(xt_taken, 1)

            def store_results(b, r):
                act.wait_ge(yb_ready, b + 1)
                act.dma_start(scratch["yb"][bass.ds(b * P, P), :] if not isinstance(b, int) else
                              scratch["yb"][b * P:(b + 1) * P, :], YB[:, r, :]).then_inc(yb_out[r], 16)

            def act_block(b, r, least):
                if least < NB - 1:
                    take_rows(b + 1, 1 - r, least + 1)
                act.wait_ge(gu_ready, b + 1)
                if refill(b):
                    act.wait_ge(h_ready, b - 1)
                fn(SIG[:, r, :], pb[r][:, 0:FF], ACT.Sigmoid).then_inc(gsig_ready, 1)
                act.wait_ge(ht_ready, b + 1)
                if refill(b):
                    act.wait_ge(down_ready, b - 1)
                fn(HT[:, r, :], pb[r][:, 0:FF], ACT.Copy).then_inc(ht_taken, 1)
                if least >= 1:
                    store_results(b - 1, 1 - r)

            take_rows(0, 0, 0)
            blocks(act, act_block)
            store_results(NB - 1, 0)
            def weigh_first(j):
                q = 2 * (j % 2)
                act.wait_ge(pick_in[q], 16 * (j // 2 + 1))
                if j >= 4:
                    act.wait_ge(out_done[j % 4], 16 * (j // 4))
                fn(SR[:, j % 4, :], picks[:, q, :], ACT.Copy, scale=topw[:, j:j + 1]).then_inc(first_weighed, 1)

            weigh_first(0)
            for turn in range(NT + 1):
                if turn + 1 < NT:
                    weigh_first(turn + 1)
                if turn >= 1:
                    j = turn - 1
                    c = ln_cols[:, j % 4, :]
                    act.wait_ge(ln_var, j + 1)
                    fn(c[:, 2:3], c[:, 1:2], ACT.Sqrt, bias=epsc[:]).then_inc(ln_sd, 1)
                    act.wait_ge(ln_shift, j + 1)
                    fn(SR[:, j % 4, :], SR[:, j % 4, :], ACT.Identity, scale=c[:, 3:4], bias=c[:, 4:5]).then_inc(normed, 1)

        @block.gpsimd
        def _(pool):
            pool.wait_ge(cond_ready, 1)
            for m in range(32):
                piece = ada_w[m % 2]
                pool.wait_ge(ada_in[m % 2], 16 * (m // 2 + 1))
                nc.gpsimd.tensor_tensor(piece, piece, cT[:, 1, :].unsqueeze(2).broadcast_to([P, KT, P]), ALU.mult
                                        ).then_inc(piece_step, 1)
                for i, n in enumerate((4, 2, 1)):
                    pool.wait_ge(piece_step, 3 * m + i + 1)
                    nc.gpsimd.tensor_tensor(piece[:, 0:n, :], piece[:, 0:n, :], piece[:, n:2 * n, :], ALU.add
                                            ).then_inc(piece_step if n > 1 else piece_summed, 1)
            pool.wait_ge(a_biased, 1)
            for h in range(4):
                strip(pool, stripAD[:, h, :], "D", h, stripD_in)
            pool.wait_ge(stripD_in, 64)
            n = 0
            for j in range(2, NT):
                pool.wait_ge(sel_ready, j - 1)
                for h in range(4):
                    if n >= 2:
                        pool.wait_ge(biased, BASE["D"] + 8 + n - 1)
                    elif n == 0:
                        pool.wait_ge(norm_taken, 4 + 24 + 4)
                        pool.wait_ge(sum_done, 2)
                    wd = (j + 1) * P
                    nc.gpsimd.tensor_tensor(bm[:, n % 2, 0:wd], stripAD[:, h, S - wd:S], idx_tile(j), ALU.add
                                            ).then_inc(bm_ready, 1)
                    n += 1
            stand(pool, 1)
            stand(pool, 2)
            stand(pool, 3)
            pool.wait_ge(x1_out, 16 * NT)
            pool.wait_ge(slots_ready, 1)

            def gather_rows(b, r, least):
                if refill(b):
                    pool.wait_ge(xt_ready, b - 1)
                idx = slot_idx[:, b:b + 1] if isinstance(b, int) else slot_idx[:, bass.ds(b, 1)]
                nc.gpsimd.tensor_copy(slot_now[:, r:r + 1], idx).then_inc(pool_step, 1)
                pool.wait_ge(pool_step, b + 1)
                pool.sem_inc(gather_go, 1)
                nc.gpsimd.indirect_dma_start(XG[:, r, :], None, scratch["x1"],
                                             bass.IndirectOffsetOnAxis(ap=slot_now[:, r:r + 1], axis=0)
                                             ).then_inc(xg_in[r], 16)

            blocks(pool, gather_rows)
            pool.wait_ge(yb_out[0], 16 * (NB // 2 + 1))
            pool.wait_ge(yb_out[1], 16 * (NB // 2))

            def gather_picks(j):
                for m in range(2):
                    c = 2 * j + m
                    if m == 0 and j >= 2:
                        pool.wait_ge(y_added, j - 1)
                    nc.gpsimd.indirect_dma_start(picks[:, c % 4, :], None, scratch["yb"],
                                                 bass.IndirectOffsetOnAxis(ap=dest_idx[:, 8 * m + j:8 * m + j + 1], axis=0)
                                                 ).then_inc(pick_in[c % 4], 16)

            gather_picks(0)
            gather_picks(1)
            pool.wait_ge(rows2_in, 48)
            for turn in range(NT + 1):
                if turn + 2 < NT:
                    gather_picks(turn + 2)
                if turn >= 1:
                    y = SR[:, (turn - 1) % 4, :]
                    pool.wait_ge(normed, turn)
                    nc.gpsimd.tensor_tensor(y, y, rows[:, 4, :], ALU.mult).then_inc(scaled, 1)

        @block.vector
        def _(dve):
            v = nc.vector
            n_self = 0

            def step(ins):
                nonlocal n_self
                n_self += 1
                ins.then_inc(dve_step, 1)
                dve.wait_ge(dve_step, n_self)

            v.memset(epsc[:], EPS)
            v.memset(ones_col[:], 1.0)
            dve.wait_ge(vecs_T, 1)
            v.tensor_copy(badaT[:], psT[:, 0:48])
            v.tensor_copy(cT[:, 0, :], psT[:, 48:56]).then_inc(c_ready, 1)
            dve.wait_ge(act_step, 1)
            step(v.tensor_scalar(cT[:, 1, :], cT[:, 1, :], 1.0, None, ALU.add))
            step(v.reciprocal(cT[:, 1, :], cT[:, 1, :]))
            v.tensor_tensor(cT[:, 1, :], cT[:, 1, :], cT[:, 0, :], ALU.mult).then_inc(cond_ready, 1)
            dve.wait_ge(cond_ready, 1)
            for n in range(4):
                acc = ada_acc[:, n * HALF:(n + 1) * HALF]
                src = ring[n] if n < 2 else ada_uT[n - 2]
                dve.wait_ge(w_landed[n] if n < 2 else ada_uT_in[n - 2], 16)
                step(v.tensor_scalar(acc, src[:, 0, :], cT[:, 1, 0:1], None, ALU.mult))
                for k in range(1, KT):
                    step(v.scalar_tensor_tensor(acc, src[:, k, :], cT[:, 1, k:k + 1], acc, ALU.mult, ALU.add))
                dve.sem_inc(ada_used, 1)
                dve.sem_inc(ada_summed, 1)
            dve.wait_ge(mod_sum, 1)
            step(v.tensor_tensor(modT[:, 0:16], psT[:, 0:16], badaT[:, 0:16], ALU.add))
            v.tensor_scalar(modT[:, 8:16], modT[:, 8:16], 1.0, None, ALU.add).then_inc(mod_ready, 1)
            dve.wait_ge(const_in, 16 * N_CONST)
            v.memset(PT[0:32, 1, 0:P], 1.0)
            v.tensor_tensor(PT[0:32, 1, P:P + 2], lamq[:, 0, :], lamq[:, 1, :], ALU.mult).then_inc(lam_ops, 1)
            n = 0
            for name, h0, width, *_ in TABLES:
                for c in range(0, width + P, HALF):
                    wd = min(HALF, width + P - c)
                    at = TAB_OFF[name] + c
                    dve.wait_ge(tab_ready, n + 1)
                    v.tensor_tensor(isel[0:4, at:at + wd], psS[n % 2][0:4, 0:wd], isel[0:4, at:at + wd], ALU.add
                                    ).then_inc(tab_taken, 1)
                    n += 1
            dve.wait_ge(lam_exp, 1)
            step(v.tensor_tensor(lam[:, 2:3], lam[:, 1:2], lam[:, 0:1], ALU.subtract))
            step(v.tensor_scalar(lam[:, 3:4], lam[:, 2:3], -LAM0, None, ALU.add))
            step(v.tensor_scalar(subg[:], subg[:], 1.0 - LAM0, None, ALU.mult))

            def top_k(j, r0=0, r1=TOPK // 8):
                acc = idx_tile(j)
                for _ in range(r0, r1):
                    step(v.max(top8[:], acc))
                    step(v.match_replace(acc, top8[:], acc, TAKEN))
                if r1 == TOPK // 8:
                    v.tensor_scalar(acc, acc, TAKEN, MASKED, ALU.not_equal, ALU.mult).then_inc(sel_ready, 1)

            dve.wait_ge(tab_out, 16)
            early = [(2, i) for i in range(TOPK // 8)] + [(3, i) for i in range(8)]
            s = 0
            for j in range(2, NT):
                acc = idx_tile(j)
                wd = (j + 1) * P
                for h in range(8):
                    dve.wait_ge(relu_taken, s + 1)
                    if h == 0:
                        ins = v.tensor_scalar(acc, SR[:, s % 4, 0:wd], iw[:, j, 0:1], None, ALU.mult)
                    else:
                        ins = v.scalar_tensor_tensor(acc, SR[:, s % 4, 0:wd], iw[:, j, h:h + 1], acc, ALU.mult, ALU.add)
                    ins.then_inc(relu_used, 1)
                    s += 1
                    dve.wait_ge(relu_used, s)
                    if j >= 3:
                        tile, i = early.pop(0)
                        top_k(tile, i, i + 1)
                step(v.tensor_tensor(acc[:, j * P:], acc[:, j * P:], causal[:], ALU.add))

            n_norm = n_diff = 0

            def norm_src():
                nonlocal n_norm
                dve.wait_ge(norm_ready, n_norm + 1)
                n_norm += 1
                return psT[:, ((n_norm - 1) % 2) * HALF:((n_norm - 1) % 2 + 1) * HALF]

            TOPS = {"B": ((3, 8), (4, 0, 12)), "C0": ((4, 12), (5, 0, 18)), "C1": ((5, 18), (6, 0, 19)),
                    "C2": ((6, 19), (7, 0, 16)), "A": (), "D": ()}
            last_steps = 16

            def last_tile(n):
                nonlocal last_steps
                top_k(NT - 1, last_steps, last_steps + n)
                last_steps += n

            for name in ORDER:
                for part in TOPS[name]:
                    top_k(*part)
                if name == "B":
                    dve.wait_ge(strip_in, 16 * 16)
                if name == "A":
                    for g in range(3):
                        for st in (fac[g], fden[g]):
                            for hf in range(2):
                                dst, src = rows_to_tokens(st, norm_src()[0:4, :], f"C{g}", hf)
                                v.tensor_copy(dst, src).then_inc(norm_taken, 1)
                                if n_norm % 3 == 1:
                                    last_tile(2)
                    dve.wait_ge(norm_taken, n_norm)
                    step(v.tensor_tensor(fmax, fac[0], fac[1], ALU.max))
                    step(v.tensor_tensor(fmax, fmax, fac[2], ALU.max))
                    for g in range(3):
                        v.tensor_tensor(fac[g], fac[g], fmax, ALU.subtract).then_inc(shift_ready, 1)
                    dve.wait_ge(shift_ready, 3)
                    for g in range(3):
                        dve.wait_ge(shift_exp, g + 1)
                        step(v.tensor_tensor(fden[g], fden[g], fac[g], ALU.mult))
                        if g:
                            step(v.tensor_tensor(fden[0], fden[0], fden[g], ALU.add))
                    step(v.reciprocal(fden[0], fden[0]))
                    for g in range(3):
                        ins = v.tensor_tensor(fac[g], fac[g], fden[0], ALU.mult)
                        if g < 2:
                            step(ins)
                    ins.then_inc(cols_ready, 1)
                    for g in range(3):
                        for pr in range(2):
                            for hf in range(2):
                                o = oT[:, RAW[f"C{g}"], pr, hf * HALF:(hf + 1) * HALF]
                                v.tensor_tensor(o, norm_src(), o, ALU.mult).then_inc(norm_taken, 1)
                                dve.wait_ge(norm_taken, n_norm)
                                if g:
                                    o0 = oT[:, 2, pr, hf * HALF:(hf + 1) * HALF]
                                    step(v.tensor_tensor(o0, o0, o, ALU.add))
                                if n_norm % 3 == 1:
                                    last_tile(1)
                    dve.sem_inc(sum_done, 1)
                    last_tile(TOPK // 8 - last_steps)
                if name == "A":
                    dve.wait_ge(stripAD_in, 64)
                if name == "D":
                    step(v.tensor_tensor(modT[:, 16:48], modT[:, 16:48], badaT[:, 16:48], ALU.add))
                    for c0 in (16, 32):
                        step(v.tensor_scalar(modT[:, c0:c0 + 8], modT[:, c0:c0 + 8], 1.0, None, ALU.add))
                    v.tensor_scalar(modT[:, 40:48], modT[:, 40:48], 1.0, None, ALU.add).then_inc(mod_ready, 1)
                    dve.wait_ge(stripD_in, 64)
                def difference(q):
                    hh, jj = q % 4, q // 4
                    wq = (jj + 1) * P
                    a0 = BASE["A"] + 2 * q
                    dve.wait_ge(probs_ready, a0 + 2)
                    step(v.reciprocal(rec[:, a0:a0 + 2], den[:, a0:a0 + 2]))
                    step(v.tensor_tensor(rec[:, a0 + 1:a0 + 2], rec[:, a0 + 1:a0 + 2], lam[:, 3:4], ALU.mult))
                    s0, s1 = a0 % 4, (a0 + 1) % 4
                    step(v.tensor_scalar(SR[:, s1, 0:wq], SR[:, s1, 0:wq], rec[:, a0 + 1:a0 + 2], None, ALU.mult))
                    v.scalar_tensor_tensor(SR[:, s0, 0:wq], SR[:, s0, 0:wq], rec[:, a0:a0 + 1], SR[:, s1, 0:wq],
                                           ALU.mult, ALU.add).then_inc(diff_ready, 1)

                for i, (h, j, k0, k1) in enumerate(units(name)):
                    if name == "A" and i:
                        difference(i - 1)
                    wd = (k1 - k0) * P
                    maps = 2 if name == "A" else 1
                    for m in range(maps):
                        a = BASE[name] + maps * i + m
                        dve.wait_ge(scores_ready, N_IDX + a + 1)
                        if a >= 4:
                            dve.wait_ge(pT_ready, BANKS[a - 4])
                        if name == "D" and j >= 2:
                            n = 4 * (j - 2) + h
                            dve.wait_ge(bm_ready, n + 1)
                            bias = bm[:, n % 2, 0:wd]
                        else:
                            bias = bias_strip(name, h, wd)
                        v.tensor_tensor_reduce(out=SR[:, a % 4, 0:wd], in0=score_place(name, a)[:, 0:wd], in1=bias, scale=1.0,
                                               scalar=sink[:, h:h + 1] if name == "B" else LOWEST,
                                               op0=ALU.add, op1=ALU.max, accum_out=mx[:, a:a + 1]).then_inc(scores_taken, 1)
                        dve.wait_ge(scores_taken, a + 1)
                        v.tensor_scalar(negm[:, a:a + 1], mx[:, a:a + 1], -1.0, None, ALU.mult).then_inc(biased, 1)
                    if name == "A":
                        if i == 31:
                            dve.wait_ge(biased, a + 1)
                            dve.sem_inc(a_biased, 1)
                        if i == 31:
                            difference(31)
                if name in ("B", "D"):
                    a0 = BASE[name]
                    dve.wait_ge(probs_ready, a0 + 32)
                    if name == "B":
                        dve.wait_ge(sink_exp, 1)
                        step(v.tensor_tensor(den[:, 0:32], den[:, 0:32], rec[:, 0:32], ALU.add))
                    step(v.reciprocal(rec[:, a0:a0 + 32], den[:, a0:a0 + 32]))
                    dve.wait_ge(pT_ready, BANKS[a0 + 31])
                    v.tensor_copy(bcols.rearrange("p (c n) -> p c n", n=64),
                                  rec[:, a0:a0 + 32].unsqueeze(2).broadcast_to([P, 32, 64])).then_inc(cols_ready, 1)
                    for pr in range(2):
                        for hf in range(2):
                            o = oT[:, RAW[name], pr, hf * HALF:(hf + 1) * HALF]
                            v.tensor_tensor(o, norm_src(), o, ALU.mult).then_inc(norm_taken, 1)
                if name == "A":
                    for i in range(4):
                        if i == 0:
                            dve.wait_ge(out_taken, OUTS["A"])
                        o = oT[:, 0, i // 2, (i % 2) * HALF:(i % 2 + 1) * HALF]
                        v.tensor_tensor(bm[:, i % 2, 0:HALF], o, o, ALU.mult).then_inc(sq_ready, 1)
                        v.tensor_copy(bm[:, i % 2, 0:HALF], norm_src()).then_inc(norm_taken, 1)
                        dve.wait_ge(norm_taken, n_norm)
                        dve.sem_inc(ms_ready, 1)
                        dve.wait_ge(rms_ready, i + 1)
                        step(v.reciprocal(bm[:, i % 2, 0:HALF], bm[:, i % 2, 0:HALF]))
                        step(v.scalar_tensor_tensor(o, o, subg[:], bm[:, i % 2, 0:HALF], ALU.mult, ALU.mult))
                    dve.sem_inc(sum_done, 1)
            stand(dve, 1)

            def rest(lo, x, hi, ready, count, done):
                dve.wait_ge(ready, count)
                v.tensor_tensor(lo, x, hi.bitcast(F32), ALU.subtract).then_inc(done, 1)

            for k in range(KT):
                if k == 2:
                    rest(glo[0], graw[0], ghi[0], w_hi, 1, w_lo)
                rest(uT_r[:, k, :], uT[:, k, :], uhi[k], u_hi, k + 1, u_lo)
            rest(glo[1], graw[1], ghi[1], w_hi, 2, w_lo)
            for n in range(4 * KT):
                if n + 2 < 4 * KT:
                    rest(glo[(n + 2) % 4], graw[(n + 2) % 4], ghi[(n + 2) % 4], w_hi, n + 3, w_lo)
                b, d = n // KT, n % KT
                dve.wait_ge(sig_ready, n + 1)
                dve.wait_ge(proj_ready, n + 1)
                for hf in range(2):
                    o = mrg[:, d, hf * HALF:(hf + 1) * HALF]
                    g = SR[:, n % 4, hf * HALF:(hf + 1) * HALF]
                    ins = v.tensor_tensor(g if b else o, pair[n % 2][hf], g, ALU.mult)
                ins.then_inc(proj_taken, 1)
                dve.wait_ge(proj_taken, n + 1)
                if b:
                    step(v.tensor_tensor(mrg[:, d, :], mrg[:, d, :], SR[:, n % 4, :], ALU.add))
            stand(dve, 2)

            def layer_norm(dst, tmp, r, n):
                for hf in range(2):
                    ins = v.bn_stats(stats[:, 0, hf, :], tmp[:, hf * HALF:(hf + 1) * HALF])
                    step(ins)
                step(v.bn_aggr(mv[:, 0, :], stats[:, 0, :, :].rearrange("p a b -> p (a b)")))
                dve.sem_inc(var_ready, 1)
                dve.wait_ge(sd_ready, n + 1)
                step(v.reciprocal(sd[:, 1:2], sd[:, 0:1]))
                step(v.tensor_scalar(dst, tmp, mv[:, 0, 0:1], sd[:, 1:2], ALU.subtract, ALU.mult))
                step(v.tensor_tensor(dst, dst, rows[:, r, :], ALU.mult))
                return v.tensor_tensor(dst, dst, rows[:, r + 1, :], ALU.add)

            dve.wait_ge(rows_in, 48)
            tmp = SR[:, 2, :]
            for j in range(NT):
                dve.wait_ge(y_ready, j + 1)
                v.tensor_tensor(tmp, psS[j % 2][:], rows[:, 0, :], ALU.mult).then_inc(y_taken, 1)
                dve.wait_ge(y_taken, j + 1)
                dve.wait_ge(xr_in[j % 2], 16 * (j // 2 + 1))
                step(v.scalar_tensor_tensor(tmp, SR[:, j % 2, :], ALPHA, tmp, ALU.mult, ALU.add))
                layer_norm(x1[:, j, :], tmp, 1, j).then_inc(x1_ready, 1)
            stand(dve, 3)

            dve.wait_ge(logit_ready, 1)
            dve.wait_ge(router_in, 32)
            b3 = lambda ap: ap.unsqueeze(2).broadcast_to([P, NT, NE])
            R = [route[:, i] for i in range(11)]
            c1 = small[:, 0:8]
            step(v.tensor_copy(R[0], pb[0][:, 0:P].rearrange("p (t e) -> p t e", t=NT)))
            step(v.tensor_reduce(c1, R[0], AX.X, ALU.max))
            step(v.tensor_tensor(R[0], R[0], b3(c1), ALU.subtract))
            dve.sem_inc(logit_max, 1)
            dve.wait_ge(logit_exp, 1)
            step(v.tensor_reduce(c1, R[0], AX.X, ALU.add))
            step(v.reciprocal(c1, c1))
            step(v.tensor_tensor(R[0], R[0], b3(c1), ALU.mult))
            step(v.tensor_tensor(R[1], R[0], PT[:, 0, P:P + NE].unsqueeze(1).broadcast_to([P, NT, NE]), ALU.add))
            grp = R[1].rearrange("p t (g m) -> p t g m", g=4)
            gs, ps_ = R[2][:, :, 0:4], R[2][:, :, 4:8]
            first = True
            for a in range(4):
                for b in range(a + 1, 4):
                    step(v.tensor_tensor(gs if first else ps_, grp[:, :, :, a], grp[:, :, :, b], ALU.add))
                    if not first:
                        step(v.tensor_tensor(gs, gs, ps_, ALU.max))
                    first = False

            def first_best(mask, vals, n, tmp_):
                iot = iota[:, 0:n].unsqueeze(1).broadcast_to([P, NT, n])
                spread = c1.unsqueeze(2).broadcast_to([P, NT, n])
                step(v.tensor_reduce(c1, vals, AX.X, ALU.max))
                step(v.tensor_tensor(tmp_, vals, spread, ALU.is_equal))
                step(v.tensor_tensor(tmp_, tmp_, iot, ALU.mult))
                step(v.tensor_reduce(c1, tmp_, AX.X, ALU.min))
                step(v.tensor_tensor(mask, iot, spread, ALU.is_equal))

            first_best(R[3][:, :, 0:4], gs, 4, R[4][:, :, 0:4])
            step(v.tensor_scalar(R[3][:, :, 4:8], R[3][:, :, 0:4], 0.0, MASKED, ALU.is_equal, ALU.mult))
            for m in range(4):
                step(v.tensor_tensor(R[5].rearrange("p t (g m) -> p t g m", g=4)[:, :, :, m],
                                     grp[:, :, :, m], R[3][:, :, 4:8], ALU.add))
            first_best(R[6], R[5], NE, R[4])
            step(v.tensor_scalar(R[7], R[6], 2.0 * MASKED, None, ALU.mult))
            step(v.tensor_tensor(R[5], R[5], R[7], ALU.add))
            first_best(R[8], R[5], NE, R[4])
            step(v.tensor_tensor(R[7], R[6], R[8], ALU.add))
            step(v.memset(earlier[:, 0:NE], 0.0))
            for j in range(NT):
                ins = v.tensor_tensor(earlier[:, (j + 1) * NE:(j + 2) * NE], earlier[:, j * NE:(j + 1) * NE],
                                      R[7][:, j, :], ALU.add)
                if j < NT - 1:
                    step(ins)
            ins.then_inc(counts_in, 1)
            dve.wait_ge(moe_const_in, 64)
            dve.wait_ge(ranks, 1)
            step(v.tensor_copy(R[1], pb[0][:, 0:P].rearrange("p (t e) -> p t e", t=NT)))
            cnt, nblk, bend, tmp16 = (small[:, 16 * i:16 * i + 16] for i in range(1, 5))
            step(v.tensor_copy(cnt, pb[0][:, P:P + NE]))
            step(v.tensor_scalar(nblk, cnt, 0.0, None, ALU.is_gt))
            for m in range(1, NT):
                step(v.scalar_tensor_tensor(nblk, cnt, float(m * P), nblk, ALU.is_gt, ALU.add))
            step(v.tensor_copy(bend, nblk))
            for sh in (1, 2, 4, 8):
                step(v.tensor_copy(tmp16, bend))
                step(v.tensor_tensor(bend[:, sh:NE], tmp16[:, sh:NE], tmp16[:, 0:NE - sh], ALU.add))
            step(v.tensor_tensor(blk_cmp, bend.unsqueeze(1).broadcast_to([P, NB, NE]),
                                 iota_row[:, 0:NB].unsqueeze(2).broadcast_to([P, NB, NE]), ALU.is_le))
            step(v.tensor_reduce(blk_sum, blk_cmp, AX.X, ALU.add))
            step(v.tensor_scalar(blk_sum, blk_sum, float(NE - 1), None, ALU.min))
            step(v.tensor_copy(block_expert[:], blk_sum))
            step(v.memset(blk_new, 1.0))
            step(v.tensor_tensor(blk_new[:, 1:NB], blk_sum[:, 1:NB], blk_sum[:, 0:NB - 1], ALU.not_equal))
            step(v.tensor_copy(block_new[:], blk_new))
            for sh in (1, 2, 4, 8, 16):
                step(v.tensor_copy(blk_tmp, blk_new))
                step(v.tensor_tensor(blk_new[:, sh:NB], blk_tmp[:, sh:NB], blk_tmp[:, 0:NB - sh], ALU.add))
            step(v.tensor_copy(block_slot[:], blk_new))
            step(v.tensor_scalar(block_slot[:], block_slot[:], 1, None, ALU.bitwise_and))
            dve.sem_inc(experts_ready, 1)
            step(v.tensor_tensor(tmp16, bend, nblk, ALU.subtract))
            for m, mask in ((0, R[6]), (1, R[8])):
                step(v.tensor_tensor(R[4], mask, R[1], ALU.mult))
                step(v.tensor_reduce(rank[:, 8 * m:8 * m + 8], R[4], AX.X, ALU.add))
                step(v.tensor_tensor(R[4], mask, tmp16.unsqueeze(1).broadcast_to([P, NT, NE]), ALU.mult))
                step(v.tensor_reduce(blk[:, 8 * m:8 * m + 8], R[4], AX.X, ALU.add))
            step(v.tensor_scalar(moved, rank, float(P), None, ALU.is_ge))
            for m in range(2, NT):
                step(v.scalar_tensor_tensor(moved, rank, float(m * P), moved, ALU.is_ge, ALU.add))
            step(v.scalar_tensor_tensor(rank, moved, -float(P), rank, ALU.mult, ALU.add))
            step(v.tensor_tensor(blk, blk, moved, ALU.add))
            step(v.scalar_tensor_tensor(moved, blk, float(P), rank, ALU.mult, ALU.add))
            step(v.tensor_copy(dest_idx[:], moved))
            for c in range(2 * NT):
                j = c % NT
                v.tensor_scalar(onehots[:, c * P:(c + 1) * P], iota_row, rank[:, c:c + 1], None, ALU.is_equal)
                v.tensor_scalar(block_hot[:, c, :], iota_row[:, 0:NB], blk[:, c:c + 1], token_id[:, j:j + 1],
                                      ALU.is_equal, ALU.mult).then_inc(hots_ready, 1)
            dve.wait_ge(slot_sum, 1)
            v.tensor_copy(slot_idx[:], pb[1][:, 0:NB]).then_inc(slots_ready, 1)
            for m, mask in ((0, R[6]), (1, R[8])):
                step(v.tensor_tensor(R[4], mask, R[0], ALU.mult))
                step(v.tensor_reduce(topw[:, 8 * m:8 * m + 8], R[4], AX.X, ALU.add))
            step(v.tensor_tensor(c1, topw[:, 0:8], topw[:, 8:16], ALU.add))
            step(v.reciprocal(c1, c1))
            for m in range(2):
                step(v.tensor_tensor(topw[:, 8 * m:8 * m + 8], topw[:, 8 * m:8 * m + 8], c1, ALU.mult))

            dve.wait_ge(rows2_in, 48)
            def results(b, r, least):
                dve.wait_ge(down_ready, b + 1)
                if refill(b):
                    dve.wait_ge(yb_out[r], b // 2 * 16 if isinstance(b, int) else b * 8 - 8 * r)
                v.tensor_tensor(YB[:, r, :], psS[r][:], rows[:, 3, :], ALU.mult).then_inc(yb_ready, 1)

            def dve_block(b, r, least):
                dve.wait_ge(gsig_ready, b + 1)
                v.tensor_tensor(SIG[:, r, :], pb[r][:, 0:FF], SIG[:, r, :], ALU.mult).then_inc(silu_ready, 1)
                dve.wait_ge(silu_ready, b + 1)
                if refill(b):
                    dve.wait_ge(ht_ready, b - 1)
                v.tensor_tensor(HN[:, r, :], pb[r][:, FF:2 * FF], SIG[:, r, :], ALU.mult).then_inc(h_ready, 1)
                if least >= 1:
                    results(b - 1, 1 - r, least - 1)

            blocks(dve, dve_block)
            results(NB - 1, 0, NB - 1)

            for turn in range(NT + 2):
                if turn < NT:
                    y = SR[:, turn % 4, :]
                    q = 2 * (turn % 2) + 1
                    dve.wait_ge(pick_in[q], 16 * (turn // 2 + 1))
                    dve.wait_ge(first_weighed, turn + 1)
                    v.scalar_tensor_tensor(y, picks[:, q, :], topw[:, 8 + turn:9 + turn], y, ALU.mult, ALU.add).then_inc(y_added, 1)
                if 1 <= turn <= NT:
                    j = turn - 1
                    y, c = SR[:, j % 4, :], ln_cols[:, j % 4, :]
                    dve.wait_ge(y_added, j + 1)
                    step(v.scalar_tensor_tensor(y, x1[:, j, :], ALPHA, y, ALU.mult, ALU.add))
                    for hf in range(2):
                        step(v.bn_stats(stats[:, 0, hf, :], y[:, hf * HALF:(hf + 1) * HALF]))
                    v.bn_aggr(c[:, 0:2], stats[:, 0, :, :].rearrange("p a b -> p (a b)")).then_inc(ln_var, 1)
                    dve.wait_ge(ln_sd, j + 1)
                    step(v.reciprocal(c[:, 3:4], c[:, 2:3]))
                    v.scalar_tensor_tensor(c[:, 4:5], c[:, 0:1], -1.0, c[:, 3:4], ALU.mult, ALU.mult).then_inc(ln_shift, 1)
                if turn >= 2:
                    y = SR[:, (turn - 2) % 4, :]
                    dve.wait_ge(scaled, turn - 1)
                    v.tensor_tensor(y, y, rows[:, 5, :], ALU.add).then_inc(fin_ready, 1)


_INS = ['x', 'c', 'rel_table', 'w_router', 'b_router', 'w_ada', 'b_ada', 'w_in', 'a_lambda_q', 'a_lambda_k',
        'a_subln_g', 'b_sinks', 'w_branch', 'w_out', 'ln1_g', 'ln1_b', 'w_exp_gate', 'w_exp_up', 'w_exp_down',
        'ln2_g', 'ln2_b']


def kernel(**inputs):
    import concourse.bacc as bacc
    from concourse.bass_utils import run_bass_kernel_spmd

    nc = bacc.Bacc("TRN2", target_bir_lowering=False, num_devices=1)
    arrays = {name: np.ascontiguousarray(inputs[name]) for name in _INS}
    arrays.update(table_constants())
    t = {name: nc.dram_tensor(f"in_{name}", a.shape, mybir.dt.from_np(a.dtype), kind="ExternalInput").ap()
         for name, a in arrays.items()}
    out = nc.dram_tensor("out", (1, S, D), F32, kind="ExternalOutput").ap()
    scratch = {"gtab": nc.dram_tensor("gtab", (4, TAB_W), F32, kind="Internal").ap(),
               "shifted": nc.dram_tensor("shifted", (4, P * (TAB_W + P + 1)), F32, kind="Internal").ap(),
               "x1": nc.dram_tensor("x1_rows", (S, D), F32, kind="Internal").ap(),
               "yb": nc.dram_tensor("block_results", (NB * P, D), F32, kind="Internal").ap(),
               "gates": nc.dram_tensor("gate_rows", (2, D), F32, kind="Internal").ap()}
    build(nc, t, out, scratch)
    r = run_bass_kernel_spmd(nc, [{f"in_{n}": a for n, a in arrays.items()}], core_ids=[0])
    return r.results[0]["out"]
```
